# Optimizing a Trainium2 kernel written in Bass

```python
import jax, jax.numpy as jnp
from jax import lax
import numpy as np
import math

D_MODEL = 1024
BATCH = 1
SEQ = 256
DEPTH = 2

CHUNK = 64
EPS = 1e-6
ROPE_BASE = 10000.0
RET_HEADS = 4
RET_DIM = 128
RET_VDIM = 128
ATT_HEADS = 8
ATT_DIM = 64
ATT_LEFT_CHUNKS = 8
REL_CLIP = 128
REL_SIZE = CHUNK - 1 + REL_CLIP + 1
SB_HEADS = 16
SB_DIM = 64
SB_BLOCK = 128
N_EXPERTS = 16
N_GROUPS = 4
TOP_K = 2
D_EXPERT = 512

N_EVEN = (DEPTH + 1) // 2
N_ODD = DEPTH // 2
RET_W = RET_HEADS * RET_DIM
RET_VW = RET_HEADS * RET_VDIM
ATT_W = ATT_HEADS * ATT_DIM
EVEN_IN = 2 * RET_W + 2 * RET_VW + 3 * ATT_W
EVEN_MIX = RET_VW + ATT_W
EVEN_SPLITS = (RET_W, 2 * RET_W, 2 * RET_W + RET_VW, 2 * RET_W + 2 * RET_VW,
               2 * RET_W + 2 * RET_VW + ATT_W, 2 * RET_W + 2 * RET_VW + 2 * ATT_W)
SB_W = SB_HEADS * SB_DIM
ODD_IN = 3 * SB_W


def rms_norm(x, gain):
    xf = x.astype(jnp.float32)
    y = xf * lax.rsqrt(jnp.mean(xf * xf, axis=-1, keepdims=True) + EPS)
    return (y * gain.astype(jnp.float32)).astype(x.dtype)

def head_rms(x):
    xf = x.astype(jnp.float32)
    return xf * lax.rsqrt(jnp.mean(xf * xf, axis=-1, keepdims=True) + EPS)

def rotary(x, pos):
    d = x.shape[-1]
    inv = ROPE_BASE ** (-jnp.arange(0, d, 2, dtype=jnp.float32) / d)
    ang = pos.astype(jnp.float32)[:, None] * inv[None, :]
    cos = jnp.cos(ang)[None, :, None, :]
    sin = jnp.sin(ang)[None, :, None, :]
    x1, x2 = jnp.split(x.astype(jnp.float32), 2, axis=-1)
    return jnp.concatenate([x1 * cos - x2 * sin, x1 * sin + x2 * cos], axis=-1).astype(x.dtype)

def retention(q, k, v):
    B_, S, H, dk = q.shape
    dv = v.shape[-1]
    nc = S // CHUNK
    log_g = jnp.log(1.0 - 2.0 ** (-5.0 - jnp.arange(H, dtype=jnp.float32)))
    idx = jnp.arange(CHUNK, dtype=jnp.float32)
    intra_dec = jnp.exp(log_g[:, None, None] * jnp.abs(idx[:, None] - idx[None, :]))
    q_dec = jnp.exp(log_g[:, None] * (idx[None, :] + 1.0))
    k_dec = jnp.exp(log_g[:, None] * (CHUNK - 1.0 - idx[None, :]))
    chunk_dec = jnp.exp(log_g * CHUNK)
    qc = q.astype(jnp.float32).reshape(B_, nc, CHUNK, H, dk)
    kc = k.astype(jnp.float32).reshape(B_, nc, CHUNK, H, dk)
    vc = v.astype(jnp.float32).reshape(B_, nc, CHUNK, H, dv)
    scores = jnp.einsum('bnihd,bnjhd->bnhij', qc, kc) * intra_dec
    o_intra = jnp.einsum('bnhij,bnjhe->bnihe', scores, vc)
    kv = jnp.einsum('bnjhd,hj,bnjhe->bnhde', kc, k_dec, vc)

    def step(state, kv_n):
        return state * chunk_dec[None, :, None, None] + kv_n, state

    init = jnp.zeros((B_, H, dk, dv), jnp.float32)
    _, prev = lax.scan(step, init, jnp.moveaxis(kv, 1, 0))
    prev = jnp.moveaxis(prev, 0, 1)
    o_cross = jnp.einsum('bnihd,hi,bnhde->bnihe', qc, q_dec, prev)
    return (o_intra + o_cross).reshape(B_, S, H, dv)

def chunk_attention(q, k, v, rel_bias):
    B_, S, H, d = q.shape
    nc = S // CHUNK
    band = ATT_LEFT_CHUNKS + 1

    def gather_band(t):
        tc = t.reshape(B_, nc, CHUNK, H, d)
        tp = jnp.pad(tc, ((0, 0), (ATT_LEFT_CHUNKS, 0), (0, 0), (0, 0), (0, 0)))
        return jnp.concatenate([tp[:, j:j + nc] for j in range(band)], axis=2)

    qc = q.reshape(B_, nc, CHUNK, H, d)
    kb = gather_band(k)
    vb = gather_band(v)
    kk = np.arange(band * CHUNK)
    dist = ATT_LEFT_CHUNKS * CHUNK + np.arange(CHUNK)[:, None] - kk[None, :]
    rel_idx = np.clip(dist, -(CHUNK - 1), REL_CLIP) + (CHUNK - 1)
    bias = rel_bias[:, rel_idx].astype(jnp.float32)
    valid = (np.arange(nc)[:, None] - ATT_LEFT_CHUNKS + kk[None, :] // CHUNK) >= 0
    s = jnp.einsum('bnihd,bnkhd->bnhik', qc, kb).astype(jnp.float32) * (d ** -0.5)
    s = s + bias[None, None]
    s = jnp.where(valid[None, :, None, None, :], s, -jnp.inf)
    p = jax.nn.softmax(s, axis=-1)
    o = jnp.einsum('bnhik,bnkhd->bnihd', p, vb.astype(jnp.float32))
    return o.reshape(B_, S, H, d).astype(q.dtype)

def stick_breaking(q, k, v):
    B_, S, H, d = q.shape
    scale = d ** -0.5
    outs = []
    for blk in range(S // SB_BLOCK):
        q0 = blk * SB_BLOCK
        kend = q0 + SB_BLOCK
        z = jnp.einsum('bihd,bjhd->bhij', q[:, q0:kend], k[:, :kend]).astype(jnp.float32) * scale
        causal = jnp.arange(kend)[None, :] < (q0 + jnp.arange(SB_BLOCK))[:, None]
        log_beta = jax.nn.log_sigmoid(z)
        log_1mb = jnp.where(causal, jax.nn.log_sigmoid(-z), 0.0)
        acc = lax.cumsum(log_1mb, axis=3, reverse=True) - log_1mb
        a = jnp.where(causal, jnp.exp(log_beta + acc), 0.0)
        outs.append(jnp.einsum('bhij,bjhd->bihd', a, v[:, :kend].astype(jnp.float32)))
    return jnp.concatenate(outs, axis=1).astype(q.dtype)

def even_mixer(h, w_in, w_out, q_norm_g, k_norm_g, rel_bias, pos):
    B_, S, _ = h.shape
    proj = h @ w_in
    rq, rk, rv, rg, aq, ak, av = jnp.split(proj, EVEN_SPLITS, axis=-1)
    rq = rotary(rq.reshape(B_, S, RET_HEADS, RET_DIM), pos)
    rk = rotary(rk.reshape(B_, S, RET_HEADS, RET_DIM), pos) * (RET_DIM ** -0.5)
    ret = retention(rq, rk, rv.reshape(B_, S, RET_HEADS, RET_VDIM))
    ret = head_rms(ret).reshape(B_, S, RET_VW).astype(h.dtype) * jax.nn.silu(rg)
    aq = rms_norm(aq.reshape(B_, S, ATT_HEADS, ATT_DIM), q_norm_g)
    ak = rms_norm(ak.reshape(B_, S, ATT_HEADS, ATT_DIM), k_norm_g)
    att = chunk_attention(aq, ak, av.reshape(B_, S, ATT_HEADS, ATT_DIM), rel_bias)
    att = att.reshape(B_, S, ATT_W)
    return jnp.concatenate([ret, att], axis=-1) @ w_out

def odd_mixer(h, w_in, w_out):
    B_, S, _ = h.shape
    q, k, v = jnp.split(h @ w_in, 3, axis=-1)
    shp = (B_, S, SB_HEADS, SB_DIM)
    o = stick_breaking(q.reshape(shp), k.reshape(shp), v.reshape(shp))
    return o.reshape(B_, S, SB_W) @ w_out

def grouped_moe(h, router_w, router_b, w_gate, w_up, w_down):
    B_, S, D = h.shape
    t = h.reshape(B_ * S, D)
    scores = jax.nn.sigmoid((t @ router_w).astype(jnp.float32))
    sel = scores + router_b.astype(jnp.float32)
    per_group = N_EXPERTS // N_GROUPS
    group_score = lax.top_k(sel.reshape(-1, N_GROUPS, per_group), TOP_K)[0].sum(-1)
    best_group = jnp.argmax(group_score, axis=-1)
    in_group = (jnp.arange(N_EXPERTS) // per_group)[None, :] == best_group[:, None]
    _, top_idx = lax.top_k(jnp.where(in_group, sel, -jnp.inf), TOP_K)
    top_s = jnp.take_along_axis(scores, top_idx, axis=-1)
    top_w = top_s / jnp.sum(top_s, axis=-1, keepdims=True)
    combine = jnp.einsum('nk,nke->ne', top_w, jax.nn.one_hot(top_idx, N_EXPERTS, dtype=jnp.float32))
    y = jnp.zeros((t.shape[0], D), jnp.float32)
    for e in range(N_EXPERTS):
        he = jax.nn.silu(t @ w_gate[e]) * (t @ w_up[e])
        y = y + combine[:, e:e + 1] * (he @ w_down[e]).astype(jnp.float32)
    return y.reshape(B_, S, D).astype(h.dtype)

def first_inputs(seed: int = 0) -> dict:
    key = jax.random.key(seed)
    ks = jax.random.split(key, 20)

    def nrm(k, shape, s):
        return jax.random.normal(k, shape, jnp.float32) * s

    return {
        "x": nrm(ks[0], (BATCH, SEQ, D_MODEL), 1.0),
        "c": nrm(ks[1], (BATCH, D_MODEL), 1.0),
        "ada_w": nrm(ks[2], (DEPTH, D_MODEL, 6 * D_MODEL), 0.5 * D_MODEL ** -0.5),
        "ada_b": nrm(ks[3], (DEPTH, 6 * D_MODEL), 0.02),
        "norm1_g": 1.0 + nrm(ks[4], (DEPTH, D_MODEL), 0.02),
        "norm2_g": 1.0 + nrm(ks[5], (DEPTH, D_MODEL), 0.02),
        "even_w_in": nrm(ks[6], (N_EVEN, D_MODEL, EVEN_IN), D_MODEL ** -0.5),
        "even_w_out": nrm(ks[7], (N_EVEN, EVEN_MIX, D_MODEL), EVEN_MIX ** -0.5),
        "att_q_norm_g": 1.0 + nrm(ks[8], (N_EVEN, ATT_DIM), 0.02),
        "att_k_norm_g": 1.0 + nrm(ks[9], (N_EVEN, ATT_DIM), 0.02),
        "att_rel_bias": nrm(ks[10], (N_EVEN, ATT_HEADS, REL_SIZE), 0.2),
        "odd_w_in": nrm(ks[11], (N_ODD, D_MODEL, ODD_IN), D_MODEL ** -0.5),
        "odd_w_out": nrm(ks[12], (N_ODD, SB_W, D_MODEL), SB_W ** -0.5),
        "router_w": nrm(ks[13], (D_MODEL, N_EXPERTS), D_MODEL ** -0.5),
        "router_b": nrm(ks[14], (N_EXPERTS,), 0.01),
        "exp_w_gate": nrm(ks[15], (DEPTH, N_EXPERTS, D_MODEL, D_EXPERT), D_MODEL ** -0.5),
        "exp_w_up": nrm(ks[16], (DEPTH, N_EXPERTS, D_MODEL, D_EXPERT), D_MODEL ** -0.5),
        "exp_w_down": nrm(ks[17], (DEPTH, N_EXPERTS, D_EXPERT, D_MODEL), D_EXPERT ** -0.5),
    }

def first_block(x, c, ada_w, ada_b, norm1_g, norm2_g, even_w_in, even_w_out,
              att_q_norm_g, att_k_norm_g, att_rel_bias, odd_w_in, odd_w_out,
              router_w, router_b, exp_w_gate, exp_w_up, exp_w_down):
    S = x.shape[1]
    pos = jnp.arange(S, dtype=jnp.int32)
    c_act = jax.nn.silu(c)
    for layer in range(DEPTH):
        mod = (c_act @ ada_w[layer] + ada_b[layer])[:, None, :]
        sh1, sc1, g1, sh2, sc2, g2 = jnp.split(mod, 6, axis=-1)
        h = rms_norm(x, norm1_g[layer]) * (1.0 + sc1) + sh1
        i = layer // 2
        if layer % 2 == 0:
            mix = even_mixer(h, even_w_in[i], even_w_out[i], att_q_norm_g[i],
                             att_k_norm_g[i], att_rel_bias[i], pos)
        else:
            mix = odd_mixer(h, odd_w_in[i], odd_w_out[i])
        x = x + g1 * mix
        h = rms_norm(x, norm2_g[layer]) * (1.0 + sc2) + sh2
        x = x + g2 * grouped_moe(h, router_w, router_b, exp_w_gate[layer],
                                 exp_w_up[layer], exp_w_down[layer])
    return x


HEAD_DIM = 64
N_A_LAYERS = DEPTH // 2
N_B_LAYERS = DEPTH - N_A_LAYERS
MEM_LEN = 256
MEM_HEADS = 4
MEM_W = MEM_HEADS * HEAD_DIM
RWKV_HEADS = (D_MODEL - MEM_W) // HEAD_DIM
RWKV_W = RWKV_HEADS * HEAD_DIM
DECAY_LORA = 64
AAA_LORA = 64
GATE_LORA = 128
RWKV_SHIFT_W = 3 * RWKV_W + DECAY_LORA + AAA_LORA + GATE_LORA
A_IN_W = RWKV_SHIFT_W + MEM_W
DIL_GROUPS = ((128, 1), (512, 4), (2048, 16))
DIL_GROUP_HEADS = 4
DIL_HEADS = len(DIL_GROUPS) * DIL_GROUP_HEADS
DIL_W = DIL_HEADS * HEAD_DIM
DIL_OUT_W = DIL_GROUP_HEADS * HEAD_DIM
BLOCK = 128
NUM_BUCKETS = 32
MAX_DISTANCE = 2048
D_FF = 2816
NORM_EPS = 1e-6
LNX_EPS = 64e-5
NEG_INF = -1e30


def rms_norm_2(x, g):
    xf = x.astype(jnp.float32)
    y = xf * lax.rsqrt(jnp.mean(xf * xf, axis=-1, keepdims=True) + NORM_EPS)
    return (y * g.astype(jnp.float32)).astype(x.dtype)

def split_heads(t):
    return t.reshape(t.shape[:-1] + (t.shape[-1] // HEAD_DIM, HEAD_DIM))

def swiglu_ffn(x, norm_g, w_in, w_out):
    gate, up = jnp.split(rms_norm_2(x, norm_g) @ w_in, 2, axis=-1)
    return (jax.nn.silu(gate) * up) @ w_out

def token_shift(p, mu):
    prev = jnp.pad(p, ((0, 0), (1, 0), (0, 0)))[:, :-1]
    return p + mu * (prev - p)

def rwkv7_scan(r, w, k, v, kk, a):
    b, _, h, n = r.shape

    def step(state, inp):
        r_t, w_t, k_t, v_t, kk_t, a_t = inp
        sa = jnp.einsum('bhvk,bhk->bhv', state, -kk_t)
        state = (state * w_t[:, :, None, :]
                 + sa[..., None] * (kk_t * a_t)[:, :, None, :]
                 + v_t[..., None] * k_t[:, :, None, :])
        return state, jnp.einsum('bhvk,bhk->bhv', state, r_t)

    xs = tuple(jnp.moveaxis(t.astype(jnp.float32), 1, 0) for t in (r, w, k, v, kk, a))
    _, ys = lax.scan(step, jnp.zeros((b, h, n, n), jnp.float32), xs)
    return jnp.moveaxis(ys, 0, 1)

def rwkv7_mix(p, mu, w0, w_up, a0, a_up, g_up, kk_scale, k_a, r_k, lnx_g, lnx_b):
    out_dtype = p.dtype
    b, s = p.shape[:2]
    p = token_shift(p, mu).astype(jnp.float32)
    cuts = [RWKV_W, 2 * RWKV_W, 3 * RWKV_W, 3 * RWKV_W + DECAY_LORA,
            3 * RWKV_W + DECAY_LORA + AAA_LORA]
    r, k, v, w_lo, a_lo, g_lo = jnp.split(p, cuts, axis=-1)
    w_log = -jax.nn.softplus(-(w0 + jnp.tanh(w_lo) @ w_up)) - 0.5
    decay = jnp.exp(-jnp.exp(w_log))
    a = jax.nn.sigmoid(a0 + a_lo @ a_up)
    g = jax.nn.sigmoid(g_lo) @ g_up
    kk = split_heads(k * kk_scale)
    kk = kk / jnp.maximum(jnp.linalg.norm(kk, axis=-1, keepdims=True), 1e-12)
    k = k * (1.0 + (a - 1.0) * k_a)
    r_h, k_h, v_h, a_h, w_h = (split_heads(t) for t in (r, k, v, a, decay))
    y = rwkv7_scan(r_h, w_h, k_h, v_h, kk, a_h)
    mean = jnp.mean(y, axis=-1, keepdims=True)
    var = jnp.mean(jnp.square(y - mean), axis=-1, keepdims=True)
    y = ((y - mean) * lax.rsqrt(var + LNX_EPS)).reshape(b, s, RWKV_W) * lnx_g + lnx_b
    bonus = jnp.sum(r_h * k_h * r_k, axis=-1, keepdims=True) * v_h
    y = (y + bonus.reshape(b, s, RWKV_W)) * g
    return y.astype(out_dtype)

def memory_attention(q, mem, mem_norm_g, w_kv, q_gain, k_gain):
    k, v = jnp.split(rms_norm_2(mem, mem_norm_g) @ w_kv, 2, axis=-1)
    k = rms_norm_2(split_heads(k), k_gain)
    v = split_heads(v)
    q = rms_norm_2(q, q_gain)
    logits = jnp.einsum('bshd,bmhd->bhsm', q, k).astype(jnp.float32) / math.sqrt(HEAD_DIM)
    probs = jax.nn.softmax(logits, axis=-1)
    return jnp.einsum('bhsm,bmhd->bshd', probs.astype(v.dtype), v)

def padded_len(seq_len, dil):
    unit = dil * BLOCK
    return -(-seq_len // unit) * unit

def strided_blocks(t, dil, s_pad):
    b, s = t.shape[:2]
    t = jnp.pad(t, ((0, 0), (0, s_pad - s)) + ((0, 0),) * (t.ndim - 2))
    t = t.reshape((b, s_pad // dil, dil) + t.shape[2:])
    t = jnp.moveaxis(t, 2, 1)
    return t.reshape((b, dil, s_pad // (dil * BLOCK), BLOCK) + t.shape[3:])

def unstride_blocks(t, seq_len):
    b, dil, nb, blk = t.shape[:4]
    t = t.reshape((b, dil, nb * blk) + t.shape[4:])
    t = jnp.moveaxis(t, 1, 2)
    return t.reshape((b, dil * nb * blk) + t.shape[3:])[:, :seq_len]

def with_prev_block(t):
    prev = jnp.pad(t[:, :, :-1], ((0, 0), (0, 0), (1, 0), (0, 0), (0, 0), (0, 0)))
    return jnp.concatenate([prev, t], axis=3)

def t5_bucket(dist):
    max_exact = NUM_BUCKETS // 2
    d_f = jnp.maximum(dist, 1).astype(jnp.float32)
    large = max_exact + (jnp.log(d_f / max_exact) / math.log(MAX_DISTANCE / max_exact)
                         * (NUM_BUCKETS - max_exact)).astype(jnp.int32)
    large = jnp.minimum(large, NUM_BUCKETS - 1)
    return jnp.where(dist < max_exact, dist, large)

def band_mask_and_bias(window, dil, n_blocks, table):
    span = window // dil
    qi = jnp.arange(BLOCK)[:, None]
    kj = jnp.arange(2 * BLOCK)[None, :]
    dsub = BLOCK + qi - kj
    band = (dsub >= 0) & (dsub <= span)
    first = (jnp.arange(n_blocks)[:, None, None] > 0) | (kj[None] >= BLOCK)
    mask = band[None] & first
    bias = jnp.transpose(table[t5_bucket(jnp.maximum(dsub, 0) * dil)], (2, 0, 1))
    return mask, bias

def shared_kv_blocks(x, kv_norm, kv_w, k_gain):
    k, v = jnp.split(rms_norm_2(x, kv_norm) @ kv_w, 2, axis=-1)
    k = rms_norm_2(split_heads(k), k_gain)
    v = split_heads(v)
    seq_len = x.shape[1]
    k_blocks, v_blocks = [], []
    for g, (_, dil) in enumerate(DIL_GROUPS):
        hs = slice(g * DIL_GROUP_HEADS, (g + 1) * DIL_GROUP_HEADS)
        s_pad = padded_len(seq_len, dil)
        k_blocks.append(strided_blocks(k[:, :, hs], dil, s_pad))
        v_blocks.append(strided_blocks(v[:, :, hs], dil, s_pad))
    return k_blocks, v_blocks

def dilated_attention(q, k_blocks, v_blocks, q_gain, rel_bias, seq_len):
    q = rms_norm_2(q, q_gain)
    scale = 1.0 / math.sqrt(HEAD_DIM)
    outs, lses = [], []
    for g, (window, dil) in enumerate(DIL_GROUPS):
        hs = slice(g * DIL_GROUP_HEADS, (g + 1) * DIL_GROUP_HEADS)
        qb = strided_blocks(q[:, :, hs], dil, padded_len(seq_len, dil))
        kw = with_prev_block(k_blocks[g])
        vw = with_prev_block(v_blocks[g]).astype(jnp.float32)
        mask, bias = band_mask_and_bias(window, dil, qb.shape[2], rel_bias[:, hs])
        logits = jnp.einsum('brnqhd,brnkhd->brnhqk', qb, kw).astype(jnp.float32) * scale
        logits = jnp.where(mask[:, None], logits + bias, NEG_INF)
        m = jnp.max(logits, axis=-1, keepdims=True)
        p = jnp.exp(logits - m)
        l = jnp.sum(p, axis=-1, keepdims=True)
        o = jnp.einsum('brnhqk,brnkhd->brnqhd', p, vw) / jnp.swapaxes(l, 3, 4)
        lse = jnp.swapaxes(m + jnp.log(l), 3, 4)
        outs.append(unstride_blocks(o, seq_len))
        lses.append(unstride_blocks(lse, seq_len))
    weights = jax.nn.softmax(jnp.stack(lses), axis=0)
    return jnp.sum(weights * jnp.stack(outs), axis=0).astype(q.dtype)

def second_inputs(seed: int = 0) -> dict:
    key = jax.random.key(seed)
    keys = iter(jax.random.split(key, 48))

    def normal(shape, scale):
        return jax.random.normal(next(keys), shape, jnp.float32) * scale

    def gain(shape):
        return 1.0 + normal(shape, 0.02)

    def uniform(shape, lo, hi):
        return jax.random.uniform(next(keys), shape, jnp.float32, lo, hi)

    d, f = D_MODEL, D_FF
    return {
        'x': normal((BATCH, SEQ, d), 1.0),
        'mem': normal((BATCH, MEM_LEN, d), 1.0),
        'ffn_pre_norm': gain((DEPTH, d)),
        'ffn_pre_w_in': normal((DEPTH, d, 2 * f), d ** -0.5),
        'ffn_pre_w_out': normal((DEPTH, f, d), f ** -0.5),
        'mix_norm': gain((DEPTH, d)),
        'ffn_post_norm': gain((DEPTH, d)),
        'ffn_post_w_in': normal((DEPTH, d, 2 * f), d ** -0.5),
        'ffn_post_w_out': normal((DEPTH, f, d), f ** -0.5),
        'mem_norm': gain((DEPTH, d)),
        'mem_w_kv': normal((DEPTH, d, 2 * MEM_W), d ** -0.5),
        'mem_q_norm': gain((DEPTH, HEAD_DIM)),
        'mem_k_norm': gain((DEPTH, HEAD_DIM)),
        'a_w_in': normal((N_A_LAYERS, d, A_IN_W), d ** -0.5),
        'a_shift_mu': uniform((N_A_LAYERS, RWKV_SHIFT_W), 0.0, 1.0),
        'a_w0': uniform((N_A_LAYERS, RWKV_W), -6.0, -1.0),
        'a_w_up': normal((N_A_LAYERS, DECAY_LORA, RWKV_W), 0.5 * DECAY_LORA ** -0.5),
        'a_a0': normal((N_A_LAYERS, RWKV_W), 0.1),
        'a_a_up': normal((N_A_LAYERS, AAA_LORA, RWKV_W), AAA_LORA ** -0.5),
        'a_g_up': normal((N_A_LAYERS, GATE_LORA, RWKV_W), GATE_LORA ** -0.5),
        'a_kk_scale': 0.85 + normal((N_A_LAYERS, RWKV_W), 0.02),
        'a_k_a': gain((N_A_LAYERS, RWKV_W)),
        'a_r_k': normal((N_A_LAYERS, RWKV_HEADS, HEAD_DIM), 0.1),
        'a_lnx_g': gain((N_A_LAYERS, RWKV_W)),
        'a_lnx_b': normal((N_A_LAYERS, RWKV_W), 0.01),
        'a_w_out': normal((N_A_LAYERS, RWKV_W + MEM_W, d), (RWKV_W + MEM_W) ** -0.5),
        'b_w_q': normal((N_B_LAYERS, d, DIL_W + MEM_W), d ** -0.5),
        'b_q_norm': gain((N_B_LAYERS, HEAD_DIM)),
        'b_w_out': normal((N_B_LAYERS, DIL_OUT_W + MEM_W, d), (DIL_OUT_W + MEM_W) ** -0.5),
        'kv_norm': gain((d,)),
        'kv_w': normal((d, 2 * DIL_W), d ** -0.5),
        'kv_k_norm': gain((HEAD_DIM,)),
        'rel_bias': normal((NUM_BUCKETS, DIL_HEADS), 0.2),
    }

def second_block(x, mem, ffn_pre_norm, ffn_pre_w_in, ffn_pre_w_out, mix_norm,
              ffn_post_norm, ffn_post_w_in, ffn_post_w_out,
              mem_norm, mem_w_kv, mem_q_norm, mem_k_norm,
              a_w_in, a_shift_mu, a_w0, a_w_up, a_a0, a_a_up, a_g_up,
              a_kk_scale, a_k_a, a_r_k, a_lnx_g, a_lnx_b, a_w_out,
              b_w_q, b_q_norm, b_w_out, kv_norm, kv_w, kv_k_norm, rel_bias):
    b, s = x.shape[:2]
    k_blocks, v_blocks = None, None
    for layer in range(DEPTH):
        x = x + 0.5 * swiglu_ffn(x, ffn_pre_norm[layer], ffn_pre_w_in[layer], ffn_pre_w_out[layer])
        u = rms_norm_2(x, mix_norm[layer])
        if layer < N_A_LAYERS:
            i = layer
            proj = u @ a_w_in[i]
            y_main = rwkv7_mix(proj[..., :RWKV_SHIFT_W], a_shift_mu[i], a_w0[i], a_w_up[i],
                               a_a0[i], a_a_up[i], a_g_up[i], a_kk_scale[i], a_k_a[i],
                               a_r_k[i], a_lnx_g[i], a_lnx_b[i])
            y_mem = memory_attention(split_heads(proj[..., RWKV_SHIFT_W:]), mem, mem_norm[layer],
                                     mem_w_kv[layer], mem_q_norm[layer], mem_k_norm[layer])
            y = jnp.concatenate([y_main, y_mem.reshape(b, s, MEM_W)], axis=-1) @ a_w_out[i]
        else:
            j = layer - N_A_LAYERS
            q_all = u @ b_w_q[j]
            y_dil = dilated_attention(split_heads(q_all[..., :DIL_W]), k_blocks, v_blocks,
                                      b_q_norm[j], rel_bias, s)
            y_mem = memory_attention(split_heads(q_all[..., DIL_W:]), mem, mem_norm[layer],
                                     mem_w_kv[layer], mem_q_norm[layer], mem_k_norm[layer])
            y = jnp.concatenate([y_dil.reshape(b, s, DIL_OUT_W),
                                 y_mem.reshape(b, s, MEM_W)], axis=-1) @ b_w_out[j]
        x = x + y
        x = x + 0.5 * swiglu_ffn(x, ffn_post_norm[layer], ffn_post_w_in[layer], ffn_post_w_out[layer])
        if layer == N_A_LAYERS - 1:
            k_blocks, v_blocks = shared_kv_blocks(x, kv_norm, kv_w, kv_k_norm)
    return x


def setup_inputs(seed=0):
    out = dict(first_inputs(seed))
    for name, value in second_inputs(seed + 1).items():
        if name != "x":
            out[name + "_2"] = value
    return out


def reference(
    x, c, ada_w, ada_b, norm1_g, norm2_g, even_w_in, even_w_out, att_q_norm_g, att_k_norm_g,
    att_rel_bias, odd_w_in, odd_w_out, router_w, router_b, exp_w_gate, exp_w_up, exp_w_down,
    mem_2, ffn_pre_norm_2, ffn_pre_w_in_2, ffn_pre_w_out_2, mix_norm_2, ffn_post_norm_2,
    ffn_post_w_in_2, ffn_post_w_out_2, mem_norm_2, mem_w_kv_2, mem_q_norm_2, mem_k_norm_2,
    a_w_in_2, a_shift_mu_2, a_w0_2, a_w_up_2, a_a0_2, a_a_up_2, a_g_up_2, a_kk_scale_2, a_k_a_2,
    a_r_k_2, a_lnx_g_2, a_lnx_b_2, a_w_out_2, b_w_q_2, b_q_norm_2, b_w_out_2, kv_norm_2, kv_w_2,
    kv_k_norm_2, rel_bias_2,
):
    x = first_block(
        x, c, ada_w, ada_b, norm1_g, norm2_g, even_w_in, even_w_out, att_q_norm_g, att_k_norm_g,
        att_rel_bias, odd_w_in, odd_w_out, router_w, router_b, exp_w_gate, exp_w_up, exp_w_down,
    )
    return second_block(
        x, mem_2, ffn_pre_norm_2, ffn_pre_w_in_2, ffn_pre_w_out_2, mix_norm_2, ffn_post_norm_2,
        ffn_post_w_in_2, ffn_post_w_out_2, mem_norm_2, mem_w_kv_2, mem_q_norm_2, mem_k_norm_2,
        a_w_in_2, a_shift_mu_2, a_w0_2, a_w_up_2, a_a0_2, a_a_up_2, a_g_up_2, a_kk_scale_2,
        a_k_a_2, a_r_k_2, a_lnx_g_2, a_lnx_b_2, a_w_out_2, b_w_q_2, b_q_norm_2, b_w_out_2,
        kv_norm_2, kv_w_2, kv_k_norm_2, rel_bias_2,
    )


_drawn_inputs = setup_inputs


def setup_inputs(seed=0):
    import zlib

    import numpy as np

    out = dict(_drawn_inputs(seed))
    spreads = {}
    factors = {'att_q_norm_g': 8.0,
     'att_k_norm_g': 3.64,
     'ffn_pre_norm_2': 4.765,
     'mix_norm_2': 3.517,
     'ffn_post_norm_2': 5.769,
     'mem_norm_2': 8.0,
     'mem_q_norm_2': 8.0,
     'mem_k_norm_2': 8.0,
     'a_w_up_2': 5.368,
     'a_a0_2': 3.176,
     'a_kk_scale_2': 64.0,
     'a_k_a_2': 6.016,
     'a_lnx_g_2': 52.633,
     'a_lnx_b_2': 64.0,
     'b_q_norm_2': 8.0,
     'kv_norm_2': 22.355,
     'kv_k_norm_2': 21.697,
     'rel_bias_2': 17.36}
    for name, (base, spread) in spreads.items():
        noise = np.random.default_rng([zlib.crc32(name.encode()), seed]).standard_normal(out[name].shape)
        drawn = base * np.exp(spread * noise) if base else spread * noise
        out[name] = __import__('jax').numpy.asarray(drawn.astype(out[name].dtype))
    for name, factor in factors.items():
        out[name] = (out[name] * factor).astype(out[name].dtype)
    return out
```

```python
from contextlib import ExitStack
import math

import numpy as np
import concourse.bass as bass
from concourse import mybir

F32 = mybir.dt.float32
BF16 = mybir.dt.bfloat16
U32 = mybir.dt.uint32
ALU = mybir.AluOpType
ACT = mybir.ActivationFunctionType
AX = mybir.AxisListType

P = 128
T = 256
NT = T // P
D = 1024
KD = D // P
EPS = 1e-6
LNX_EPS = 64e-5
NEG = -1e30
SLOTS = 6
SLOT = 4096
CHUNK = 64
EVEN_W = 3584
ODD_W = 3072
A_W = 2816
SHIFT_TILES = 20
NE = 16
DFF = 2816
HC = 256
MOE_CHUNKS = NE * 512 // HC
FFN_CHUNKS = DFF // HC
ADA_W = 6 * D
ADA_HALF = ADA_W // 2
ADA_BLOCKS = 2 * KD
DECAY = math.exp(-0.5)


def constants():
    f = np.float32
    i = np.arange(P)
    c = {}
    same = (i[:, None] // CHUNK) == (i[None, :] // CHUNK)
    jj, tt = i[:, None], i[None, :]
    lower = np.array([[float(j < e) for j in range(4)] for e in range(4)]).reshape(1, 16)
    keep = np.concatenate([
        np.eye(P), np.ones((P, P)), np.where(jj >= tt, -1.0, 0.0), -np.ones((P, P)),
        (jj <= tt) & same, same, (i < 64)[:, None], (i >= 64)[:, None], np.repeat(lower, P, 0)], 1).astype(f)
    lv = [((jj >> (l + 1)) == (tt >> (l + 1))) & (((jj >> l) & 1) == 0) & (((tt >> l) & 1) == 1)
          for l in range(6)]
    rw_masks = np.concatenate(lv[1:] + [lv[0], lv[0].T, (jj < tt) & same], 1).astype(f)
    tok = np.arange(T)
    dec = []
    for h in range(4):
        lg = np.log(1.0 - 2.0 ** (-5.0 - h))
        m = np.exp(lg * np.abs(tok[None, :] - tok[:, None])) * (128.0 ** -0.5)
        m = m * ((tok[:, None] // CHUNK) <= (tok[None, :] // CHUNK))
        dec.append(np.concatenate([m[:P], m[P:, P:]], 1))
    inv = (10000.0 ** (-np.arange(0, 128, 2, dtype=np.float32) / np.float32(128))).astype(f)
    ang = (tok.astype(f)[:, None] * inv[None, :]).astype(f)
    rope = np.concatenate([np.cos(ang).reshape(2, P, 64).transpose(1, 0, 2).reshape(P, 128),
                           np.sin(ang).reshape(2, P, 64).transpose(1, 0, 2).reshape(P, 128)], 1)
    am = np.where((tok[None, :] // CHUNK) <= (tok[:, None] // CHUNK), 0.0, NEG)
    even = np.concatenate([np.concatenate(dec, 1), rope, am[:P, :P][::-1], am[P:][::-1]], 1).astype(f)
    reset = np.ones((P, T), f)
    reset[:, ::CHUNK] = 0.0
    dist = 255 - np.arange(512)
    hot_rel = np.zeros((256, 512), f)
    hot_rel[np.clip(dist, -63, 128) + 63, np.arange(512)] = 1.0
    d = np.maximum(dist, 0)
    df = np.maximum(d, 1).astype(np.float64)
    large = np.minimum(16 + np.floor(np.log(df / 16) / math.log(128) * 16 + 1e-9).astype(int), 31)
    bucket = np.where(d < 16, d, large)
    hot_t5 = np.zeros((32, 512), f)
    hot_t5[bucket, np.arange(512)] = 1.0
    ban = np.zeros((12, 512), f)
    for g, dil in enumerate((1, 4, 16)):
        ok = (dist >= 0) & (dist % dil == 0)
        if g == 0:
            ok &= dist <= 128
        ban[4 * g:4 * g + 4] = np.where(ok, 0.0, NEG)
    return {"c_keep": keep, "c_rw_masks": rw_masks, "c_even": even, "c_anti": np.eye(P, dtype=f)[::-1].copy(), "c_reset": reset, "c_hot_rel": hot_rel,
            "c_hot_t5": hot_t5, "c_ban": ban}


class Plan:

    def __init__(self):
        self.blocks = []
        self.gemms = {}
        self.swi = {}
        self.gemm_chunks = 0
        self.swi_chunks = 0
        self.swi_n = 0

    def add(self, kind, what, free):
        self.blocks.append((kind, what, free))
        return len(self.blocks) - 1

    def gemm(self, name, width):
        n = -(-width // 512)
        g = dict(base=self.gemm_chunks, n=n, width=width, first=len(self.blocks))
        for c in range(n):
            self.gemm_chunks += 1
            self.add("gemm", (name, c), ("gemm_done", self.gemm_chunks))
        self.gemms[name] = g

    def gemm_short(self, name):
        g = dict(base=self.gemm_chunks, n=2, width=D, first=len(self.blocks))
        self.gemm_chunks += 2
        self.add("short", name, ("gemm_done", self.gemm_chunks))
        self.gemms[name] = g

    def swiglu(self, name, chunks):
        s = dict(base=self.swi_chunks, n=chunks, first=len(self.blocks), no=self.swi_n, units=chunks // 2)
        self.swi_n += 1
        used = 2 * self.swi_n + self.swi_chunks
        for u in range(chunks // 2):
            done = self.swi_chunks + 2 * u + 2
            self.add("gate", (name, u), ("gate_done", done))
            self.add("up", (name, u), ("up_done", done))
            self.add("down", (name, u), ("hid_used", used + 2 * u + 2))
        if chunks % 2:
            self.add("half", name, ("up_done", self.swi_chunks + chunks))
            self.add("down_half", name, ("hid_used", used + chunks))
        self.swi_chunks += chunks
        self.swi[name] = s


def plan():
    p = Plan()
    for b in range(ADA_BLOCKS):
        p.add("ada", b, ("ada_used", b + 1))
    p.gemm("even_in", EVEN_W)
    p.gemm("even_out", D)
    p.swiglu("moe0", MOE_CHUNKS)
    p.gemm("odd_in", ODD_W)
    p.gemm("odd_out", D)
    p.swiglu("moe1", MOE_CHUNKS)
    p.swiglu("pre0", FFN_CHUNKS)
    p.gemm("mem0", 512)
    p.gemm("a_in", A_W)
    p.add("rwkv", 0, ("rwkv_over", 1))
    p.gemm("a_out", D)
    p.swiglu("post0", FFN_CHUNKS)
    p.gemm("kv", 1536)
    p.swiglu("pre1", FFN_CHUNKS)
    p.gemm("mem1", 512)
    p.gemm("b_q", D)
    p.gemm_short("b_out")
    p.swiglu("post1", FFN_CHUNKS)
    return p


PL = plan()

HT, XN, PROJ, ROWS, WORK = 0, 2048, 4096, 11264, 15360
POOL = 24576
NORMS = ["n_even", "n_moe0", "n_odd", "n_moe1", "n_pre0", "n_mem0", "n_mix0", "n_post0", "n_kv", "n_pre1",
         "n_mem1", "n_mix1", "n_post1"]
JOB_BASE = {"att": 0, "mem0": 16, "mem1": 24, "dil": 32}


def build(nc, a, out):
    ctx = ExitStack()
    with ctx:
        def sb(name, shape, dt=F32):
            return ctx.enter_context(nc.sbuf_tensor(name, shape, dt))

        sems = {}

        def sem(name):
            if name not in sems:
                sems[name] = ctx.enter_context(nc.semaphore(name))
            return sems[name]

        scratch_bias = nc.dram_tensor("bias_rows", [20, 512], F32, kind="Internal").ap()

        ring = sb("ring", [P, SLOTS * SLOT])
        pool = sb("pool", [P, POOL])
        x = sb("x", [P, NT, D])
        keep = sb("keep", [P, a["c_keep"].shape[1]])
        gcols = sb("gcols", [P, 13, KD])
        rcols = sb("rcols", [P, 50])
        omu = sb("omu", [P, SHIFT_TILES])
        mcols = sb("mcols", [P, 2, 4, KD])
        mgain = sb("mgain", [P, 4, KD])
        cact = sb("cact", [P, KD])
        tiny = sb("tiny", [P, 162])
        zbf = sb("zbf", [P, P], BF16)
        gains64 = sb("gains64", [P, 8, 64])
        router_w = sb("router_w", [P, KD, NE])
        router_b = sb("router_b", [P, NE])
        psum = ctx.enter_context(nc.psum_tensor("psum", [P, 8, 512], F32))

        def bank(b, n=1):
            return psum[:, b, :] if n == 1 else psum[:, b:b + n, :].rearrange("p b n -> p (b n)")

        def view(off, *dims):
            n = int(np.prod(dims))
            v = pool[:, off:off + n]
            if len(dims) == 2:
                return v.rearrange("p (a b) -> p a b", a=dims[0])
            if len(dims) == 3:
                return v.rearrange("p (a b c) -> p a b c", a=dims[0], b=dims[1])
            return v

        off = 0
        K = {}
        for nm, w in (("ident", 128), ("ones", 128), ("neg_from", 128), ("neg_ones", 128), ("chunk_incl", 128),
                      ("head_ones", 128), ("head_cols", 2), ("lower", 16)):
            K[nm] = keep[:, off:off + w]
            off += w
        ident = K["ident"]

        hT = view(HT, KD, T)
        xn = view(XN, NT, D)
        acc = view(PROJ, ADA_W)
        grow = [[view(ROWS + 2048 * l + 1024 * j, D) for j in range(2)] for l in range(2)]

        def slot(b):
            s = b % SLOTS
            return ring[:, s * SLOT:(s + 1) * SLOT]

        def bc(ap, shape):
            return ap.to_broadcast(shape)

        csilu = cact
        ss = tiny[:, 0:2]
        var = tiny[:, 2:4]
        rstd = tiny[:, 4:6]
        hss = tiny[:, 8:40]
        hvar = tiny[:, 40:72]
        hrstd = tiny[:, 72:104]
        nmax = tiny[:, 104:106]
        esum = tiny[:, 106:110]
        erec = tiny[:, 6:8]
        mx = tiny[:, 110:112]
        pend = tiny[:, 112:136].rearrange("p (i c) -> p i c", c=4)
        bonus = tiny[:, 136:160]

        memx = view(ROWS, NT, D)
        NSRC = {n: (memx if n.startswith("n_mem") else x[:, :, :]) for n in NORMS}
        NGAIN = {"n_even": mgain[:, 0, :], "n_moe0": mgain[:, 1, :], "n_odd": mgain[:, 2, :],
                 "n_moe1": mgain[:, 3, :], "n_pre0": gcols[:, 4, :], "n_pre1": gcols[:, 5, :],
                 "n_mix0": gcols[:, 6, :], "n_mix1": gcols[:, 7, :], "n_post0": gcols[:, 8, :],
                 "n_post1": gcols[:, 9, :], "n_mem0": gcols[:, 10, :], "n_mem1": gcols[:, 11, :],
                 "n_kv": gcols[:, 12, :]}
        NSHIFT = {"n_even": mcols[:, 0, 0, :], "n_moe0": mcols[:, 0, 2, :], "n_odd": mcols[:, 1, 0, :],
                  "n_moe1": mcols[:, 1, 2, :]}
        XSEEN = {"n_even": 0, "n_moe0": 1, "n_odd": 2, "n_moe1": 3, "n_pre0": 4, "n_mem0": 0, "n_mix0": 5,
                 "n_post0": 6, "n_kv": 7, "n_pre1": 7, "n_mem1": 0, "n_mix1": 8, "n_post1": 9}

        proj_e = view(PROJ, NT, EVEN_W)
        decay_t = view(WORK, 4, 384)
        rope_c = view(WORK + 1536, NT, 64)
        rope_s = view(WORK + 1664, NT, 64)
        att_ban = view(WORK + 1792, 384)
        qk_t = view(WORK + 2176, 8, T)
        ret_s = view(WORK + 4224, 2, 384)
        att_p = view(WORK + 4992, 2, 768)
        att_pt = view(WORK + 6528, 768)
        anti = view(WORK + 7296, P)
        rot_a = view(WORK + 4992, 2, 512)
        rot_b = view(WORK + 6016, 2, 512)

        def bias_att(h, t):
            o = HT + 384 * h if h < 5 else ROWS + 2048 + 384 * (h - 5)
            return view(o, P) if t == 0 else view(o + P, T)

        qf = view(PROJ, KD, T)
        kf = view(PROJ + 2048, KD, T)
        v_o = view(PROJ + 4096, NT, D)
        SBW = WORK
        sb_abs = [view(SBW + 1536 * i, 384) for i in range(2)]
        sb_sp = [view(SBW + 1536 * i + 384, 384) for i in range(2)]
        sb_a = [view(SBW + 1536 * i + 768, 384) for i in range(2)]
        sb_zero = view(SBW + 3072, P)
        spread = keep[:, 0:256].bitcast(BF16)
        comb_b = view(WORK, NE, T)
        hid = [view(WORK + 4096, 2, HC), view(WORK + 4608, 2, HC)]
        comb_t = view(WORK + 5120, T)[0:NE, :]
        ada1 = view(WORK + 6144, ADA_HALF)
        rt = view(WORK + 5376, 512)
        rt_sc, comb_tok = rt[:, 0:32], rt[:, 448:480]
        mem_kt = view(ROWS + 3072, 2, T)
        mem_v = view(ROWS + 3584, NT, 256)
        mem_kv = view(WORK, NT, 512)
        q_mem_a = view(PROJ + 5120, NT, 256)
        F = view(PROJ, SHIFT_TILES, T)
        sh_tmp = [view(PROJ + 5632 + 260 * i, 260) for i in range(4)]
        W = [view(WORK + 1536 * i, 6, T) for i in range(6)]
        Wf = [view(WORK + 1536 * i, 1536) for i in range(6)]
        Fr, Fk, Fv = F[:, 0:6, :], F[:, 6:12, :], F[:, 12:18, :]
        rw_reset = view(XN, T)
        v_tok, b_tok, k_tok = (view(WORK + 1536 * i, NT, 768) for i in range(3))
        TT = view(ROWS, 6, 4, P)
        U = view(WORK + 6144, NT, 768)
        gate = view(HT, NT, 768)
        t_lt = view(PROJ + 3072, 4, P)
        t_t = view(PROJ + 3584, 4, P)
        t_x = view(PROJ + 4096, 4, P)
        t_lm = view(PROJ + 4608, 4, P)
        Z = view(PROJ + 3072, 768)
        SA = view(PROJ + 5632, NT, 768)
        state = view(ROWS + 3072, 6, P)
        bm = view(PROJ + 4608, 4, P)
        km = view(HT + 1536, 4, P)
        y_r = xn[:, :, 0:768]
        yc = view(PROJ + 3072, NT, 768)
        kd_t = view(PROJ, 6, T)
        v_d = view(PROJ + 1536, NT, 768)
        kd = view(WORK, NT, 768)
        q_d = view(PROJ + 3072, NT, D)
        qd_t = view(PROJ + 5120, 8, T)

        def bias_dil(g, h, t):
            o = WORK + 384 * (4 * g + h)
            return view(o, P) if t == 0 else view(o + P, T)

        def job(kind, h, t):
            half = slice(64 * (h % 2), 64 * (h % 2) + 64)
            qs = slice(P * t, P * t + P)
            if kind == "att":
                n = P * (t + 1)
                return ([dict(q=qk_t[half, h // 2, qs], k=qk_t[half, 4 + h // 2, 0:n], n=n,
                              bias=bias_att(h, t),
                              v=[proj_e[:, kt, 3072 + 64 * h:3136 + 64 * h] for kt in range(t + 1)])],
                        xn[:, t, 512 + 64 * h:576 + 64 * h])
            if kind in ("mem0", "mem1"):
                q = qk_t[half, h // 2, qs] if kind == "mem0" else qd_t[half, 6 + h // 2, qs]
                o = xn[:, t, 768 + 64 * h:832 + 64 * h] if kind == "mem0" else \
                    xn[:, t, 256 + 64 * h:320 + 64 * h]
                return ([dict(q=q, k=mem_kt[half, h // 2, :], n=T, bias=None,
                              v=[mem_v[:, kt, 64 * h:64 * h + 64] for kt in range(NT)])], o)
            n = P * (t + 1)
            segs = []
            for g in range(3):
                hh = 4 * g + h
                segs.append(dict(q=qd_t[half, hh // 2, qs], k=kd_t[half, hh // 2, 0:n], n=n,
                                 bias=bias_dil(g, h, t),
                                 v=[v_d[:, kt, 64 * hh:64 * hh + 64] for kt in range(t + 1)]))
            return segs, xn[:, t, 64 * h:64 * h + 64]

        JOBS = {"att": [("att", h, t) for h in range(8) for t in range(NT)],
                "mem0": [("mem0", h, t) for h in range(4) for t in range(NT)],
                "mem1": [("mem1", h, t) for h in range(4) for t in range(NT)],
                "dil": [("dil", h, t) for h in range(4) for t in range(NT)]}

        def gemm_dst(name, c):
            lo = 512 * c
            hi = min(lo + 512, PL.gemms[name]["width"])
            if name == "even_in":
                return "copy", proj_e[:, :, lo:hi]
            if name == "odd_in":
                if c < 2:
                    return "feat", qf[:, 4 * c:4 * c + 4, :]
                if c < 4:
                    return "feat", kf[:, 4 * c - 8:4 * c - 4, :]
                return "copy", v_o[:, :, lo - 2048:hi - 2048]
            if name in ("mem0", "mem1"):
                return "copy", mem_kv[:, :, :]
            if name == "a_in":
                return ("copy", q_mem_a[:, :, :]) if c == 5 else ("shift", c)
            if name == "kv":
                return "kv", c
            if name == "b_q":
                return "copy", q_d[:, :, lo:hi]
            if name in ("even_out", "odd_out"):
                return "resid_g", (0 if name == "even_out" else 1, c)
            return "resid", c

        KV_PARTS = {0: [(0, 512, kd, 0)], 1: [(0, 256, kd, 512), (256, 512, v_d, 0)], 2: [(0, 512, v_d, 256)]}

        X_AFTER = {"even_out": 1, "odd_out": 3, "a_out": 6, "b_out": 9}
        EVAC = []
        nact = ndve = 0
        for name, g in PL.gemms.items():
            for c in range(g["n"]):
                kind = gemm_dst(name, c)[0]
                if kind in ("copy", "feat", "kv"):
                    nact += 1
                    ndve += 1
                    EVAC.append([("ev_act", nact), ("ev_dve", ndve)])
                elif kind == "shift":
                    EVAC.append([("shift_mixed", 4 * c + 4)])
                else:
                    EVAC.append([("x_new", X_AFTER[name])] if c else
                                [("resid_first", list(X_AFTER).index(name) + 1)])

        def moved(name, c):
            return EVAC[PL.gemms[name]["base"] + c]

        block = ctx.enter_context(nc.Block())

        @block.sync
        def _(sp):
            def landed(b):
                return sem(f"landed{b % SLOTS}")

            def slot_free(b):
                if b >= SLOTS:
                    freed, count = PL.blocks[b - SLOTS][2]
                    sp.wait_ge(sem(freed), count)

            def static_block(b):
                kind, what, _ = PL.blocks[b]
                slot_free(b)
                dst = slot(b)
                if kind == "ada":
                    src = a["ada_w"][0].rearrange("(p t) n -> p (t n)", t=KD)[:, what * ADA_HALF:(what + 1) * ADA_HALF]
                    sp.dma_start(dst[:, 0:ADA_HALF], src).then_inc(landed(b), 16)
                elif kind == "gemm":
                    name, c = what
                    g = PL.gemms[name]
                    src = {"even_in": a["even_w_in"][0], "even_out": a["even_w_out"][0], "odd_in": a["odd_w_in"][0],
                           "odd_out": a["odd_w_out"][0], "mem0": a["mem_w_kv_2"][0], "mem1": a["mem_w_kv_2"][1],
                           "a_in": a["a_w_in_2"][0], "a_out": a["a_w_out_2"][0], "kv": a["kv_w_2"],
                           "b_q": a["b_w_q_2"][0]}[name]
                    n = min(512, g["width"] - 512 * c)
                    sp.dma_start(dst.rearrange("p (k n) -> p k n", k=KD)[:, :, 0:n],
                                 src.rearrange("(k p) n -> p k n", p=P)[:, :, 512 * c:512 * c + n])\
                      .then_inc(landed(b), 16)
                elif kind == "short":
                    sp.dma_start(dst.rearrange("p (k n) -> p k n", k=4),
                                 a["b_w_out_2"][0].rearrange("(k p) n -> p k n", p=P)).then_inc(landed(b), 16)
                elif kind == "rwkv":
                    for n, (o, src) in enumerate((
                            (0, a["a_w_up_2"][0]), (0, a["a_a_up_2"][0]), (768, a["a_g_up_2"][0]),
                            (1536, a["a_lnx_g_2"][0].partition_broadcast(P)),
                            (2304, a["a_lnx_b_2"][0].partition_broadcast(P)), (3072, a["c_rw_masks"]))):
                        rows = dst[64:P] if n == 1 else dst[0:src.shape[0]]
                        sp.dma_start(rows[:, o:o + src.shape[1]], src).then_inc(sem("rwkv_in"), 16)
                elif kind in ("gate", "up", "down"):
                    name, u = what
                    layer = int(name[-1])
                    if name.startswith("moe"):
                        src = a[{"gate": "exp_w_gate", "up": "exp_w_up", "down": "exp_w_down"}[kind]][layer, u]
                        k = 4 if kind == "down" else KD
                        src = src.rearrange("(k p) n -> p k n", p=P)
                    else:
                        w_in = a[f"ffn_{name[:-1]}_w_in_2"][layer].rearrange("(k p) n -> p k n", p=P)
                        w_out = a[f"ffn_{name[:-1]}_w_out_2"][layer].rearrange("(k p) n -> p k n", p=P)
                        k = 4 if kind == "down" else KD
                        src = {"gate": w_in[:, :, 512 * u:512 * u + 512],
                               "up": w_in[:, :, DFF + 512 * u:DFF + 512 * u + 512],
                               "down": w_out[:, 4 * u:4 * u + 4, :]}[kind]
                    sp.dma_start(dst.rearrange("p (k n) -> p k n", k=k), src).then_inc(landed(b), 16)
                elif kind == "half":
                    layer = int(what[-1])
                    w_in = a[f"ffn_{what[:-1]}_w_in_2"][layer].rearrange("(k p) (g n) -> p g k n", p=P, g=2)
                    d4 = dst.rearrange("p (g k n) -> p g k n", g=2, k=KD)
                    for g in range(2):
                        sp.dma_start(d4[:, g], w_in[:, g, :, DFF - HC:DFF]).then_inc(sem(f"half{g}"), 16)
                else:
                    layer = int(what[-1])
                    w_out = a[f"ffn_{what[:-1]}_w_out_2"][layer].rearrange("(k p) n -> p k n", p=P)
                    sp.dma_start(dst[:, 0:2048].rearrange("p (k n) -> p k n", k=2), w_out[:, 20:22, :])\
                      .then_inc(landed(b), 16)

            def moe_units(name):
                s = PL.swi[name]
                layer = int(name[-1])
                used = 2 * (s["no"] + 1) + s["base"]
                with sp.Fori(1, s["units"] // 2) as i:
                    for q in range(2):
                        b = s["first"] + 3 * q
                        e = 2 * i + q
                        sp.wait_ge(sem("gate_done"), s["base"] + 4 * i + 2 * q - 2)
                        sp.dma_start(slot(b).rearrange("p (k n) -> p k n", k=KD),
                                     a["exp_w_gate"][layer, e].rearrange("(k p) n -> p k n", p=P))\
                          .then_inc(landed(b), 16)
                        sp.wait_ge(sem("up_done"), s["base"] + 4 * i + 2 * q - 2)
                        sp.dma_start(slot(b + 1).rearrange("p (k n) -> p k n", k=KD),
                                     a["exp_w_up"][layer, e].rearrange("(k p) n -> p k n", p=P))\
                          .then_inc(landed(b + 1), 16)
                        sp.wait_ge(sem("hid_used"), used + 4 * i + 2 * q - 2)
                        sp.dma_start(slot(b + 2).rearrange("p (k n) -> p k n", k=4),
                                     a["exp_w_down"][layer, e].rearrange("(k p) n -> p k n", p=P))\
                          .then_inc(landed(b + 2), 16)
                        if layer == 0:
                            sp.wait_ge(sem("ada_used"), ADA_BLOCKS + 2 * i + q)
                            sp.dma_start(ada1, a["ada_w"][1].rearrange("(p t) (h n) -> p t h n", t=KD, h=2)[:, i, q, :])\
                              .then_inc(sem("ada1_landed"), 16)

            b = 0
            while b < len(PL.blocks):
                kind, what, _ = PL.blocks[b]
                if kind == "gate" and what[0].startswith("moe") and what[1] == 2:
                    if what[0] == "moe0":
                        sp.wait_ge(sem("moe_ready"), 1)
                        for q in range(2):
                            sp.wait_ge(sem("ada_used"), ADA_BLOCKS + q)
                            sp.dma_start(ada1, a["ada_w"][1].rearrange("(p t) (h n) -> p t h n", t=KD, h=2)[:, 0, q, :])\
                              .then_inc(sem("ada1_landed"), 16)
                    moe_units(what[0])
                    b += 3 * (PL.swi[what[0]]["units"] - 2)
                    continue
                static_block(b)
                b += 1
            sp.wait_ge(sem("x_new"), 10)
            sp.dma_start(out.rearrange("a (t p) d -> p (a t) d", p=P), x[:, :, :]).then_inc(sem("stored"), 16)
            sp.wait_ge(sem("stored"), 16)

        @block.gpsimd
        def _(pl):
            pl.dma_start(cact[:, :], a["c"].rearrange("a (p t) -> p (a t)", t=KD)).then_inc(sem("c_in"), 16)
            pl.dma_start(x[:, :, :], a["x"].rearrange("a (t p) d -> p (a t) d", p=P)).then_inc(sem("x_in"), 16)
            pl.dma_start(keep[:, :], a["c_keep"]).then_inc(sem("keep_in"), 16)
            pl.dma_start(gcols[:, :, :], a["gain_cols"].rearrange("p (n k) -> p n k", k=KD)).then_inc(sem("cols_in"), 16)
            pl.dma_start(rcols[:, :], a["rwkv_cols"]).then_inc(sem("cols_in"), 16)
            pl.dma_start(gains64[:, :, :], a["gains64"].partition_broadcast(P).rearrange("p (n d) -> p n d", d=64))\
              .then_inc(sem("cols_in"), 16)
            pl.dma_start(router_b[:, :], a["router_b"].partition_broadcast(P)).then_inc(sem("cols_in"), 16)
            pl.dma_start(router_w[:, :, :], a["router_w"].rearrange("(k p) n -> p k n", p=P)).then_inc(sem("cols_in"), 16)
            pl.memset(acc, 0.0).then_inc(sem("acc_zero"), 1)
            pl.memset(zbf[:, :], 0.0).then_inc(sem("zbf_zero"), 1)
            pl.wait_ge(sem("acc_zero"), 1)
            pl.dma_start(acc[0:1, :], a["ada_b"][0:1, :]).then_inc(sem("ada_b_in"), 16)
            hot = view(WORK + 2176, 4, 512)
            pl.dma_start(hot[:, 0:2, :], a["c_hot_rel"].rearrange("(k p) n -> p k n", p=P)).then_inc(sem("hot_in"), 16)
            pl.dma_start(hot[0:32, 2, :], a["c_hot_t5"]).then_inc(sem("hot_in"), 16)
            pl.dma_start(hot[0:12, 3, :], a["c_ban"]).then_inc(sem("hot_in"), 16)
            pl.dma_start(view(WORK + 4224, 2, 8), a["rel_t"].rearrange("(k p) n -> p k n", p=P)).then_inc(sem("hot_in"), 16)
            pl.dma_start(view(WORK + 4240, 12)[0:32, :], a["rel_bias_2"]).then_inc(sem("hot_in"), 16)
            pl.dma_start(view(WORK, 2176), a["c_even"]).then_inc(sem("even_in"), 16)
            pl.wait_ge(sem("bias_rows"), 2)
            pl.dma_start(scratch_bias[0:8, :], view(WORK + 4256, 512)[0:8, :]).then_inc(sem("bias_out"), 16)
            pl.dma_start(scratch_bias[8:20, :], view(WORK + 4768, 512)[0:12, :]).then_inc(sem("bias_out"), 16)
            pl.wait_ge(sem("bias_out"), 32)

            def toeplitz(dst, row, t):
                n = P * (t + 1)
                src = bass.AP(tensor=scratch_bias.tensor, offset=row * 512 + 128 - P * t, ap=[[1, P], [1, n]])
                return pl.dma_start(dst, src)

            pl.wait_ge(sem("gemm_done"), PL.gemms["even_in"]["base"] + PL.gemms["even_in"]["n"])
            for h in range(8):
                for t in range(NT):
                    toeplitz(bias_att(h, t), h, t).then_inc(sem("bias_in"), 16)
            pl.dma_start(anti, a["c_anti"]).then_inc(sem("anti_in"), 16)
            pl.wait_ge(sem("bias_in"), 256)
            pl.wait_ge(sem("even_in"), 16)
            for h in range(8):
                for t in range(NT):
                    b_ = bias_att(h, t)
                    pl.tensor_tensor(b_, b_, att_ban[:, 0:P] if t == 0 else att_ban[:, P:384], ALU.add)\
                      .then_inc(sem("bias_banned"), 1)
            pl.wait_ge(sem("x_new"), 1)
            pl.memset(acc, 0.0).then_inc(sem("acc_zero"), 1)
            pl.wait_ge(sem("acc_zero"), 2)
            pl.dma_start(acc[0:1, :], a["ada_b"][1:2, :]).then_inc(sem("ada_b_in"), 16)
            pl.wait_ge(sem("x_new"), 4)
            pl.dma_start(memx, a["mem_2"].rearrange("a (t p) d -> p (a t) d", p=P)).then_inc(sem("mem_in"), 16)
            pl.wait_ge(sem("norm_T"), 4 * (NORMS.index("n_mix0") + 1))
            pl.wait_ge(sem("heads_ok"), 3)
            pl.dma_start(rw_reset, a["c_reset"]).then_inc(sem("reset_in"), 16)
            pl.wait_ge(sem("x_new"), 7)
            pl.dma_start(memx, a["mem_2"].rearrange("a (t p) d -> p (a t) d", p=P)).then_inc(sem("mem_in"), 16)
            pl.wait_ge(sem("x_new"), 8)
            pl.wait_ge(sem("heads_ok"), 5)
            pl.wait_ge(sem("gemm_done"), PL.gemms["b_q"]["base"] + 1)
            for g in range(3):
                for h in range(4):
                    for t in range(NT):
                        toeplitz(bias_dil(g, h, t), 8 + 4 * g + h, t).then_inc(sem("bias2_in"), 16)
            pl.dma_start(anti, a["c_anti"]).then_inc(sem("bias2_in"), 16)

        def flat(v):
            return v if len(v.shape) == 2 else v.rearrange("p a b -> p (a b)")

        def blocks_tok(src, tiles, dst):
            s = [src(j, t) for j in range(tiles) for t in range(NT)]
            return [(s[4 * b:4 * b + 4], dst(2 * b, min(2, tiles - 2 * b))) for b in range(-(-tiles // 2))]

        def blocks_feat(srcv, dst):
            s = [srcv[:, i, P * t:P * t + P] for t in range(NT) for i in range(6)]
            return [(s[4 * b:4 * b + 4], dst[:, 512 * b:512 * b + 512]) for b in range(3)]

        def into(v):
            return lambda j, n: flat(v[:, j:j + n, :])

        TRS = {
            "ret_qk": blocks_tok(lambda j, t: proj_e[:, t, P * j:P * j + P], 8, into(qk_t)),
            "att_qk": blocks_tok(lambda j, t: proj_e[:, t, 2048 + P * j:2048 + P * j + P], 8, into(qk_t)),
            "even_mix": blocks_tok(lambda j, t: xn[:, t, P * j:P * j + P], 8, into(hT)),
            "odd_mix": blocks_tok(lambda j, t: xn[:, t, P * j:P * j + P], 8, into(hT)),
            "mem0_k": blocks_tok(lambda j, t: mem_kv[:, t, P * j:P * j + P], 2, into(mem_kt)),
            "mem0_q": blocks_tok(lambda j, t: q_mem_a[:, t, P * j:P * j + P], 2, into(qk_t)),
            "rw_v": blocks_feat(Fv, flat(v_tok)),
            "rw_b": blocks_feat(W[5], flat(b_tok)),
            "rw_k": blocks_feat(Fk, flat(k_tok)),
            "a_mix": blocks_tok(lambda j, t: xn[:, t, P * j:P * j + P], 8, into(hT)),
            "kd": blocks_tok(lambda j, t: kd[:, t, P * j:P * j + P], 6, into(kd_t)),
            "mem1_k": blocks_tok(lambda j, t: mem_kv[:, t, P * j:P * j + P], 2, into(mem_kt)),
            "dil_q": blocks_tok(lambda j, t: q_d[:, t, P * j:P * j + P], 8, into(qd_t)),
            "b_mix": blocks_tok(lambda j, t: xn[:, t, P * j:P * j + P], 4, into(hT)),
        }
        TR_BASE, n = {}, 0
        for nm, bl in TRS.items():
            TR_BASE[nm] = n
            n += len(bl)

        def tr_counts(nm):
            e = TR_BASE[nm] + len(TRS[nm])
            return (e + 1) // 2, e // 2

        @block.tensor
        def _(pe):
            def landed(b):
                pe.wait_ge(sem(f"landed{b % SLOTS}"), 16 * sum(1 for k in range(b % SLOTS, b + 1, SLOTS) if PL.blocks[k][0] not in ("half", "rwkv")))

            def transposes(nm, *ready):
                for r in ready:
                    pe.wait_ge(sem(r[0]), r[1])
                for i, (srcs, _) in enumerate(TRS[nm]):
                    B = TR_BASE[nm] + i
                    e = B - 4
                    if e >= 0:
                        pe.wait_ge(sem("tr_act" if e % 2 == 0 else "tr_dve"), e // 2 + 1)
                    for k, src in enumerate(srcs):
                        m = pe.transpose(bank(4 + B % 4)[:, P * k:P * k + P], src, ident)
                    m.then_inc(sem("tr_done"), 1)

            def transposed(nm):
                na, nd = tr_counts(nm)
                if na > 0:
                    pe.wait_ge(sem("tr_act"), na)
                if nd > 0:
                    pe.wait_ge(sem("tr_dve"), nd)

            def norm(nm):
                n = NORMS.index(nm)
                pe.wait_ge(sem("norm_xn"), 2 * (n + 1))
                for b in range(4):
                    for k in range(2):
                        for t in range(NT):
                            j = 2 * b + k
                            m = pe.transpose(bank(b)[:, T * k + P * t:T * k + P * t + P],
                                             xn[:, t, P * j:P * j + P], ident)
                    m.then_inc(sem("norm_T"), 1)
                pe.wait_ge(sem("norm_act"), 4 * (n + 1))
                pe.wait_ge(sem("norm_dve"), 4 * (n + 1))

            def gemm(nm):
                g = PL.gemms[nm]
                for c in range(g["n"]):
                    G = g["base"] + c
                    kind = gemm_dst(nm, c)[0]
                    if G >= 4:
                        for e in EVAC[G - 4]:
                            pe.wait_ge(sem(e[0]), e[1])
                    n = min(512, g["width"] - 512 * c)
                    if nm == "b_out":
                        if c == 0:
                            landed(g["first"])
                        wt = slot(g["first"]).rearrange("p (k n) -> p k n", k=4)[:, :, 512 * c:512 * c + 512]
                        ks = 4
                    else:
                        landed(g["first"] + c)
                        wt = slot(g["first"] + c).rearrange("p (k n) -> p k n", k=KD)
                        ks = KD
                    pair = 2 * (G % 4)
                    if kind in ("feat", "shift"):
                        for f in range(4):
                            o = bank(pair + f // 2)[:, T * (f % 2):T * (f % 2) + T]
                            for k in range(ks):
                                m = pe.matmul(o, wt[:, k, P * f:P * f + P], hT[:, k, :], start=k == 0, stop=k == ks - 1)
                    else:
                        for t in range(NT):
                            for k in range(ks):
                                m = pe.matmul(bank(pair + t)[:, 0:n], hT[:, k, P * t:P * t + P], wt[:, k, 0:n],
                                              start=k == 0, stop=k == ks - 1)
                    m.then_inc(sem("gemm_done"), 1)

            def swiglu(nm):
                s = PL.swi[nm]
                G0, first = s["base"], s["first"]

                def zero_products(start):
                    for b in range(4):
                        m = pe.matmul(bank(b), zbf[:, :], spread, start=start, stop=not start, skip_group_check=True)
                        if start and b >= 2:
                            m.then_inc(sem("hid_used"), 1)
                        if not start and b == 3:
                            m.then_inc(sem("sums_done"), 1)

                def gate_up(c, q, unit, land):
                    u, half = q // 2, q % 2
                    if unit is not None and unit * 2 >= s["n"] - 1:
                        b = first + 3 * unit
                        lots = slot(b).rearrange("p (g k n) -> p g k n", g=2, k=KD)
                        parts = [(lots[:, 0], 0), (lots[:, 1], 0)]
                    else:
                        b = first + 3 * u
                        parts = [(slot(b + j).rearrange("p (k n) -> p k n", k=KD), HC * half) for j in range(2)]
                    for j, (wt, o) in enumerate(parts):
                        if half == 0:
                            land(j)
                        pe.wait_ge(sem("silu_done" if j == 0 else "hid_ready"), max(G0 + c, 1) if isinstance(c, int) else G0 + c)
                        for f in range(2):
                            for k in range(KD):
                                m = pe.matmul(bank(4 + 2 * (q % 2) + j)[:, T * f:T * f + T],
                                              wt[:, k, o + P * f:o + P * f + P], hT[:, k, :],
                                              start=k == 0, stop=k == KD - 1)
                        m.then_inc(sem("gate_done" if j == 0 else "up_done"), 1)

                def down(c, q, unit, land):
                    u, half = q // 2, q % 2
                    lasthalf = unit is not None and unit * 2 >= s["n"] - 1
                    b = first + 3 * unit + 1 if lasthalf else first + 3 * u + 2
                    if half == 0:
                        land(2)
                    pe.wait_ge(sem("hid_ready"), G0 + c + 2)
                    wt = slot(b)[:, 0:2048 if lasthalf else 4096].rearrange("p (k n) -> p k n", n=D)
                    for f in range(2):
                        for t in range(NT):
                            for h in range(2):
                                m = pe.matmul(bank(2 * t + h), hid[q % 2][:, f, P * t:P * t + P],
                                              wt[:, (0 if lasthalf else 2 * half) + f, 512 * h:512 * h + 512],
                                              start=False, stop=False, skip_group_check=True)
                    m.then_inc(sem("hid_used"), 1)

                def static_land(unit):
                    def land(j):
                        if unit * 2 >= s["n"] - 1:
                            if j < 2:
                                pe.wait_ge(sem(f"half{j}"), 16 * (s["no"] - 1))
                            else:
                                landed(first + 3 * unit + 1)
                        else:
                            landed(first + 3 * unit + j)
                    return land

                base_land = {}
                for r in range(SLOTS):
                    b = first + r
                    base_land[r] = 16 * sum(1 for k in range(b % SLOTS, b + 1, SLOTS)
                                            if PL.blocks[k][0] not in ("half", "rwkv"))

                def loop_land(i, ahead, u):
                    def land(j):
                        pe.wait_ge(sem(f"landed{(first + 3 * u + j) % SLOTS}"),
                                   base_land[3 * u + j] + 16 * ahead + 16 * i)
                    return land

                if XSEEN["n_" + nm] > 0:
                    pe.wait_ge(sem("x_new"), XSEEN["n_" + nm])
                zero_products(True)
                gate_up(0, 0, 0, static_land(0))
                loops = (s["n"] - 1) // 4
                with pe.Fori(0, loops) as i:
                    for q in range(4):
                        nx = (q + 1) % 4
                        gate_up(4 * i + q + 1, nx, None, loop_land(i, 1 if q == 3 else 0, nx // 2))
                        down(4 * i + q, q, None, loop_land(i, 0, q // 2))
                for c in range(4 * loops, s["n"]):
                    if c + 1 < s["n"]:
                        gate_up(c + 1, (c + 1) % 4, (c + 1) // 2, static_land((c + 1) // 2))
                    down(c, c % 4, c // 2, static_land(c // 2))
                zero_products(False)

            def attention(kind, *ready):
                for r in ready:
                    pe.wait_ge(sem(r[0]), r[1])
                jobs, base = JOBS[kind], JOB_BASE[kind]
                for j in range(len(jobs) + 2):
                    J = base + j
                    if j < len(jobs):
                        if J > 1:
                            pe.wait_ge(sem("att_exp"), J - 1)
                        lg = psum[:, 2 * (j % 2):2 * (j % 2) + 2, :].rearrange("p b n -> p (b n)")
                        for k, sg in enumerate(job(*jobs[j])[0]):
                            o = lg[:, T * k:T * k + sg["n"]]
                            if sg["bias"] is not None:
                                pe.matmul(o, anti, sg["bias"], start=True, stop=False)
                            m = pe.matmul(o, sg["q"], sg["k"], start=sg["bias"] is None, stop=True)
                        m.then_inc(sem("att_scores"), 1)
                    if 0 <= j - 2:
                        J2 = J - 2
                        pe.wait_ge(sem("att_pts"), J2 + 1)
                        if J2 > 1:
                            pe.wait_ge(sem("att_o"), J2 - 1)
                        vs = [v for sg in job(*jobs[j - 2])[0] for v in sg["v"]]
                        for k, v in enumerate(vs):
                            m = pe.matmul(bank(6 + j % 2)[:, 0:64], att_pt[:, P * k:P * k + P], v,
                                          start=k == 0, stop=k == len(vs) - 1)
                        m.then_inc(sem("att_pv"), 1)
                    if 0 <= j - 1 < len(jobs):
                        J1 = J - 1
                        pe.wait_ge(sem("att_exp"), J1 + 1)
                        if J1 > 0:
                            pe.wait_ge(sem("att_pts"), J1)
                        k = 0
                        for sg_i, sg in enumerate(job(*jobs[j - 1])[0]):
                            for kt in range(len(sg["v"])):
                                o = T * sg_i + P * kt
                                m = pe.transpose(bank(4, 2)[:, P * k:P * k + P],
                                                 att_p[:, (j - 1) % 2, o:o + P], ident)
                                k += 1
                        m.then_inc(sem("att_pt"), 1)

            def modulation(layer):
                for j, part in enumerate((0, 1, 3, 4)):
                    for k in range(KD):
                        o = D * part + P * k
                        m = pe.matmul(bank(4)[:, KD * j + k:KD * j + k + 1], acc[:, o:o + P], K["ones"][:, 0:1],
                                      start=True, stop=True)
                m.then_inc(sem("mod_cols"), 1)
                for j, part in enumerate((2, 5)):
                    for h in range(2):
                        o = D * part + 512 * h
                        m = pe.matmul(bank(2 * j + h), K["ones"], acc[:, o:o + 512], start=True, stop=True)
                m.then_inc(sem("mod_rows"), 1)

            pe.wait_ge(sem("keep_in"), 16)
            pe.wait_ge(sem("hot_in"), 80)
            hot = view(WORK + 2176, 4, 512)
            for k in range(2):
                m = pe.matmul(bank(6)[0:8, :], view(WORK + 4224, 2, 8)[:, k, :], hot[:, k, :], start=k == 0, stop=k == 1)
            m.then_inc(sem("bias_ps"), 1)
            pe.matmul(bank(7)[0:12, :], view(WORK + 4240, 12)[0:32, :], hot[0:32, 2, :], start=True, stop=True)\
              .then_inc(sem("bias_ps"), 1)
            pe.wait_ge(sem("ada_used"), ADA_BLOCKS)
            modulation(0)
            norm("n_even")
            pe.wait_ge(sem("mod_moved"), 1)
            gemm("even_in")
            pe.wait_ge(sem("rotated"), 1)
            transposes("ret_qk")
            transposed("ret_qk")
            for h in range(5):
                if h < 4:
                    if h > 1:
                        pe.wait_ge(sem("ret_decayed"), h - 1)
                    o = bank(h % 2)
                    pe.matmul(o[:, 0:T], qk_t[:, 4 + h, 0:P], qk_t[:, h, :], start=True, stop=True)
                    pe.matmul(o[:, T:T + P], qk_t[:, 4 + h, P:T], qk_t[:, h, P:T], start=True, stop=True)\
                      .then_inc(sem("ret_scores"), 1)
                if h >= 1:
                    g = h - 1
                    pe.wait_ge(sem("ret_decayed"), g + 1)
                    if g > 1:
                        pe.wait_ge(sem("ret_moved"), g - 1)
                    o = bank(2 + g % 2)
                    v = proj_e[:, :, D + P * g:D + P * g + P]
                    s = ret_s[:, g % 2, :]
                    pe.matmul(o[:, 0:P], s[:, 0:P], v[:, 0, :], start=True, stop=True)
                    pe.matmul(o[:, P:T], s[:, P:T], v[:, 0, :], start=True, stop=False)
                    pe.matmul(o[:, P:T], s[:, T:T + P], v[:, 1, :], start=False, stop=True)\
                      .then_inc(sem("ret_pv"), 1)
            transposes("att_qk", ("heads_ok", 1))
            transposed("att_qk")
            attention("att", ("bias_banned", 16), ("anti_in", 16))
            transposes("even_mix", ("att_o", 16), ("even_mixed", 1))
            transposed("even_mix")
            gemm("even_out")

            def router(layer):
                pe.wait_ge(sem("x_new"), 1 + 2 * layer)
                for t in range(NT):
                    for k in range(KD):
                        m = pe.matmul(bank(4)[:, NE * t:NE * t + NE], hT[:, k, P * t:P * t + P], router_w[:, k, :],
                                      start=k == 0, stop=k == KD - 1)
                m.then_inc(sem("router_ps"), 1)
                pe.wait_ge(sem("comb_tok"), layer + 1)
                for t in range(NT):
                    m = pe.transpose(bank(5)[0:NE, P * t:P * t + P], comb_tok[:, NE * t:NE * t + NE], ident)
                m.then_inc(sem("comb_T_ps"), 1)
                pe.wait_ge(sem("comb_T"), layer + 1)
                for e in range(NE):
                    m = pe.matmul(bank(e // 2)[:, T * (e % 2):T * (e % 2) + T],
                                  bc(ident[0:NE, e:e + 1], [NE, P]), comb_t, start=True, stop=True)
                    if e % 2:
                        m.then_inc(sem("comb_ps"), 1)
                pe.wait_ge(sem("comb_act"), 4 * (layer + 1))
                pe.wait_ge(sem("comb_dve"), 4 * (layer + 1))

            norm("n_moe0")
            router(0)
            swiglu("moe0")
            pe.wait_ge(sem("ada_used"), 2 * ADA_BLOCKS)
            pe.wait_ge(sem("x_new"), 2)
            modulation(1)
            norm("n_odd")
            gemm("odd_in")
            for e in moved("odd_in", 5):
                pe.wait_ge(sem(e[0]), e[1])
            for s_ in range(18):
                if s_ < 16:
                    h = s_
                    half = slice(64 * (h % 2), 64 * (h % 2) + 64)
                    kk, qq = kf[half, h // 2, :], qf[half, h // 2, :]
                    if h > 1:
                        pe.wait_ge(sem("sb_soft"), h - 1)
                    if h > 1:
                        pe.wait_ge(sem("sb_exp"), h - 1)
                    for bk in (h % 2, 2 + h % 2):
                        last = bk >= 2
                        pe.matmul(bank(bk)[:, 0:P], kk[:, 0:P], qq[:, 0:P], start=True, stop=not last,
                                  skip_group_check=True)
                        pe.matmul(bank(bk)[:, P:T], kk[:, 0:P], qq[:, P:T], start=not last, stop=not last,
                                  skip_group_check=True)
                        m = pe.matmul(bank(bk)[:, T:T + P], kk[:, P:T], qq[:, P:T], start=not last, stop=not last,
                                      skip_group_check=True)
                        if not last:
                            m.then_inc(sem("sb_z"), 1)
                if 1 <= s_ <= 16:
                    h = s_ - 1
                    pe.wait_ge(sem("sb_masked"), h + 1)
                    o, sp_ = bank(2 + h % 2), sb_sp[h % 2]
                    pe.matmul(o[:, 0:P], K["neg_from"], sp_[:, 0:P], start=False, stop=False, skip_group_check=True)
                    pe.matmul(o[:, P:T], K["neg_from"], sp_[:, P:T], start=False, stop=False, skip_group_check=True)
                    pe.matmul(o[:, P:T], K["neg_ones"], sp_[:, T:T + P], start=False, stop=False,
                              skip_group_check=True)
                    pe.matmul(o[:, T:T + P], K["neg_from"], sp_[:, T:T + P], start=False, stop=True,
                              skip_group_check=True).then_inc(sem("sb_sums"), 1)
                if s_ >= 2:
                    h = s_ - 2
                    pe.wait_ge(sem("sb_weights"), h + 1)
                    if h > 1:
                        pe.wait_ge(sem("sb_out"), h - 1)
                    o, av = bank(4 + h % 2), sb_a[h % 2]
                    v = v_o[:, :, 64 * h:64 * h + 64]
                    pe.matmul(o[:, 0:64], av[:, 0:P], v[:, 0, :], start=True, stop=True)
                    pe.matmul(o[:, 64:128], av[:, P:T], v[:, 0, :], start=True, stop=False)
                    pe.matmul(o[:, 64:128], av[:, T:T + P], v[:, 1, :], start=False, stop=True)\
                      .then_inc(sem("sb_pv"), 1)
            transposes("odd_mix", ("sb_out", 16))
            transposed("odd_mix")
            gemm("odd_out")
            norm("n_moe1")
            router(1)
            swiglu("moe1")
            norm("n_pre0")
            swiglu("pre0")
            norm("n_mem0")
            gemm("mem0")
            transposes("mem0_k", ("heads_ok", 2))
            norm("n_mix0")
            gemm("a_in")
            pe.wait_ge(sem("shift_mixed"), SHIFT_TILES)
            transposes("mem0_q", ("heads_ok", 3))
            transposed("mem0_q")
            attention("mem0")
            pe.wait_ge(sem("att_o"), 24)
            pe.wait_ge(sem("rwkv_in"), 96)
            par = slot(PL.gemms["a_in"]["first"] + 6)
            pe.wait_ge(sem("rw_low"), 2)
            for i in range(6):
                m = pe.matmul(bank(i // 2)[:, T * (i % 2):T * (i % 2) + T], par[0:64, P * i:P * i + P],
                              F[0:64, 18, :], start=True, stop=True)
            m.then_inc(sem("rw_w_ps"), 1)
            for i in range(6):
                m = pe.matmul(bank(3 + i // 2)[:, T * (i % 2):T * (i % 2) + T], par[64:P, P * i:P * i + P],
                              F[64:P, 18, :], start=True, stop=True)
            m.then_inc(sem("rw_a_ps"), 1)
            pe.wait_ge(sem("rw_sig"), 1)
            for n in range(6):
                t, s = n // 3, n % 3
                m = pe.matmul(bank((6 + n // 2) % 8)[:, T * (n % 2):T * (n % 2) + T], F[:, 19, P * t:P * t + P],
                              par[:, 768 + T * s:768 + T * s + T], start=True, stop=True)
            m.then_inc(sem("rw_g_ps"), 1)
            pe.wait_ge(sem("rw_sq"), 1)
            pe.wait_ge(sem("rw_sig"), 2)
            for i in range(6):
                m = pe.matmul(bank(3 + i // 2)[:, T * (i % 2):T * (i % 2) + T], K["head_ones"], W[4][:, i, :],
                              start=True, stop=True)
            m.then_inc(sem("rw_ss_ps"), 1)
            pe.wait_ge(sem("rw_rk"), 1)
            for t in range(NT):
                for i in range(6):
                    m = pe.matmul(bank(1)[:, 12 * t + 2 * i:12 * t + 2 * i + 2], W[4][:, i, P * t:P * t + P],
                                  K["head_cols"], start=True, stop=True)
            m.then_inc(sem("rw_bonus_ps"), 1)
            pe.wait_ge(sem("rw_gate"), 1)
            pe.wait_ge(sem("rw_ss"), 1)
            pe.wait_ge(sem("rw_bonus"), 1)
            transposes("rw_v", ("rw_scaled", 1))
            transposes("rw_b")
            transposes("rw_k")
            transposed("rw_k")
            for i in range(6):
                if i > 0:
                    pe.wait_ge(sem("rw_u"), i)
                if i > 0:
                    pe.wait_ge(sem("rw_t"), i)
                halves = [slice(64 * e, 64 * e + 64) for e in range(2)]
                for e in range(2):
                    for t in range(NT):
                        tk = slice(P * t, P * t + P)
                        bT, kkT, kT = W[5][halves[e], i, tk], W[3][halves[e], i, tk], Fk[halves[e], i, tk]
                        pe.matmul(bank(e)[:, P * t:P * t + P], bT, kkT, start=True, stop=True)
                        pe.matmul(bank(e)[:, T + P * t:T + P * t + P], kkT, bT, start=True, stop=True)
                        m = pe.matmul(bank(2 + e)[:, P * t:P * t + P], kT, kkT, start=True, stop=True)
                m.then_inc(sem("rw_l_ps"), 1)
                for l in range(5):
                    pe.wait_ge(sem("rw_lm"), 5 * i + l + 1)
                    for m4 in range(4):
                        m = pe.matmul(bank(4)[:, P * m4:P * m4 + P], t_lm[:, m4, :], t_t[:, m4, :], start=True, stop=True)
                    m.then_inc(sem("rw_x_ps"), 1)
                    pe.wait_ge(sem("rw_x"), 5 * i + l + 1)
                    for m4 in range(4):
                        pe.matmul(bank(5)[:, P * m4:P * m4 + P], TT[:, i, m4, :], t_x[:, m4, :], start=True, stop=True)
                        m = pe.matmul(bank(6)[:, P * m4:P * m4 + P], t_x[:, m4, :], TT[:, i, m4, :], start=True, stop=True)
                    m.then_inc(sem("rw_tx_ps"), 1)
                pe.wait_ge(sem("rw_m"), i + 1)
                for e in range(2):
                    for t in range(NT):
                        m = pe.matmul(bank(7)[:, P * t + 64 * e:P * t + 64 * e + 64], t_lm[:, 2 * e + t, :],
                                      v_tok[:, t, P * i + 64 * e:P * i + 64 * e + 64], start=True, stop=True)
                m.then_inc(sem("rw_u_ps"), 1)
            pe.wait_ge(sem("rw_u"), 6)
            for c in range(4):
                t, q0 = c // 2, 64 * (c % 2)
                pe.wait_ge(sem("rw_state"), c + 1)
                if c > 0:
                    pe.wait_ge(sem("rw_y"), c)
                for i in range(6):
                    m = pe.matmul(bank(0, 2)[:, P * i:P * i + P], W[3][:, i, P * t:P * t + P], state[:, i, :],
                                  start=True, stop=True)
                m.then_inc(sem("rw_z_ps"), 1)
                for i in range(6):
                    m = pe.matmul(bank(2, 2)[:, P * i:P * i + P], Fr[:, i, P * t:P * t + P], state[:, i, :],
                                  start=True, stop=True)
                m.then_inc(sem("rw_y_ps"), 1)
                pe.wait_ge(sem("rw_z"), c + 1)
                for h in range(12):
                    m = pe.matmul(bank(4, 2)[:, 64 * h:64 * h + 64], TT[:, h // 2, 2 * (h % 2) + t, :],
                                  Z[:, 64 * h:64 * h + 64], start=True, stop=True)
                m.then_inc(sem("rw_sa_ps"), 1)
                pe.wait_ge(sem("rw_sa"), c + 1)
                rows = slice(q0, q0 + 64)
                for i in range(6):
                    cols = slice(P * i, P * i + P)
                    o = bank(6, 2)[:, cols]
                    pe.matmul(o, b_tok[rows, t, cols], SA[rows, t, cols], start=True, stop=False)
                    m = pe.matmul(o, k_tok[rows, t, cols], v_tok[rows, t, cols], start=False, stop=True)
                m.then_inc(sem("rw_new_ps"), 1)
            for i in range(6):
                if i > 0:
                    pe.wait_ge(sem("rw_bk"), i)
                pe.wait_ge(sem("rw_y"), 4)
                pe.wait_ge(sem("rw_z"), 4)
                for e in range(2):
                    half = slice(64 * e, 64 * e + 64)
                    for t in range(NT):
                        tk = slice(P * t, P * t + P)
                        pe.matmul(bank(e)[:, P * t:P * t + P], W[5][half, i, tk], Fr[half, i, tk], start=True, stop=True)
                        m = pe.matmul(bank(2 + e)[:, P * t:P * t + P], Fk[half, i, tk], Fr[half, i, tk],
                                      start=True, stop=True)
                m.then_inc(sem("rw_bk_ps"), 1)
                pe.wait_ge(sem("rw_bk"), i + 1)
                if i > 0:
                    pe.wait_ge(sem("rw_yadd"), i)
                for e in range(2):
                    for t in range(NT):
                        o = bank(4)[:, P * t + 64 * e:P * t + 64 * e + 64]
                        hs = slice(P * i + 64 * e, P * i + 64 * e + 64)
                        pe.matmul(o, bm[:, 2 * e + t, :], SA[:, t, hs], start=True, stop=False)
                        m = pe.matmul(o, km[:, 2 * e + t, :], v_tok[:, t, hs], start=False, stop=True)
                m.then_inc(sem("rw_g2_ps"), 1)
            transposes("a_mix", ("rw_out", 1))
            transposed("a_mix")
            gemm("a_out")
            norm("n_post0")
            swiglu("post0")
            norm("n_kv")
            gemm("kv")
            transposes("kd", ("heads_ok", 4))
            norm("n_pre1")
            swiglu("pre1")
            norm("n_mem1")
            gemm("mem1")
            transposes("mem1_k", ("heads_ok", 5))
            norm("n_mix1")
            gemm("b_q")
            transposes("dil_q", ("heads_ok", 6))
            transposed("dil_q")
            attention("mem1")
            attention("dil", ("bias2_in", 25 * 16))
            transposes("b_mix", ("att_o", 40))
            transposed("b_mix")
            gemm("b_out")
            norm("n_post1")
            swiglu("post1")

        @block.scalar
        def _(act):
            done = [0]

            def step(ins):
                done[0] += 1
                ins.then_inc(sem("act_step"), 1)
                act.wait_ge(sem("act_step"), done[0])

            def norm(nm):
                n = NORMS.index(nm)
                if nm == "n_even":
                    act.wait_ge(sem("x_in"), 16)
                elif nm == "n_mem0":
                    act.wait_ge(sem("mem_in"), 16)
                elif nm == "n_mem1":
                    act.wait_ge(sem("mem_in"), 32)
                if XSEEN[nm] > 0:
                    act.wait_ge(sem("x_new"), XSEEN[nm])
                if 2 * n > 0:
                    act.wait_ge(sem("norm_xn"), 2 * n)
                for t in range(NT):
                    act.activation(xn[:, t, :], NSRC[nm][:, t, :], ACT.Square, accum_out=ss[:, t:t + 1])\
                       .then_inc(sem("norm_ss"), 1)
                act.wait_ge(sem("norm_var"), n + 1)
                act.activation(rstd, var, ACT.Sqrt).then_inc(sem("norm_rstd"), 1)
                for j in (0, 1, 4, 5):
                    b = j // 2
                    act.wait_ge(sem("norm_T"), 4 * n + b + 1)
                    shift = NSHIFT[nm][:, j:j + 1] if nm in NSHIFT else 0.0
                    act.activation(hT[:, j, :], bank(b)[:, T * (j % 2):T * (j % 2) + T], ACT.Identity, bias=shift,
                                   scale=NGAIN[nm][:, j:j + 1]).then_inc(sem("norm_act"), 1)

            def gemm(nm):
                g = PL.gemms[nm]
                for c in range(g["n"]):
                    G = g["base"] + c
                    kind, dst = gemm_dst(nm, c)
                    if kind.startswith("resid"):
                        continue
                    act.wait_ge(sem("gemm_done"), G + 1)
                    ps = bank(2 * (G % 4))
                    if kind == "copy":
                        d = dst[:, 0, :]
                        act.activation(d, ps[:, 0:d.shape[1]], ACT.Copy).then_inc(sem("ev_act"), 1)
                    elif kind == "feat":
                        act.activation(flat(dst[:, 0:2, :]), ps, ACT.Copy,
                                       scale=0.125 if c < 2 else 1.0).then_inc(sem("ev_act"), 1)
                    elif kind == "kv":
                        for lo, hi, d, o in KV_PARTS[c]:
                            m = act.activation(d[:, 0, o:o + hi - lo], ps[:, lo:hi], ACT.Copy)
                        m.then_inc(sem("ev_act"), 1)
                    else:
                        for f in range(4):
                            n = 4 * c + f
                            if n > 3:
                                act.wait_ge(sem("shift_mixed"), n - 3)
                            tmp = sh_tmp[n % 4]
                            act.activation(tmp[:, 1:T + 1], bank(2 * (G % 4) + f // 2)[:, T * (f % 2):T * (f % 2) + T],
                                           ACT.Copy, scale=rcols[:, n:n + 1]).then_inc(sem("shift_mu"), 1)

            def transposes(nm):
                for i, (srcs, dst) in enumerate(TRS[nm]):
                    B = TR_BASE[nm] + i
                    if B % 2 == 0:
                        act.wait_ge(sem("tr_done"), B + 1)
                        act.activation(dst, bank(4 + B % 4)[:, 0:P * len(srcs)], ACT.Copy).then_inc(sem("tr_act"), 1)

            def heads(n):
                act.wait_ge(sem("heads_var"), n + 1)
                act.activation(hrstd, hvar, ACT.Sqrt).then_inc(sem("heads_rstd"), 1)

            def swiglu(nm):
                s = PL.swi[nm]
                G0 = s["base"]
                used = 2 * s["no"] + s["base"]

                def silu(c, q):
                    act.wait_ge(sem("gate_done"), G0 + c + 1)
                    act.wait_ge(sem("hid_used"), used + c + 1)
                    act.activation(flat(hid[q % 2]), bank(4 + 2 * (q % 2)), ACT.Silu).then_inc(sem("silu_done"), 1)

                loops = (s["n"] - 1) // 4
                with act.Fori(0, loops) as i:
                    for q in range(4):
                        silu(4 * i + q, q)
                for c in range(4 * loops, s["n"]):
                    silu(c, c % 4)

            def attention(kind):
                jobs, base = JOBS[kind], JOB_BASE[kind]
                for j in range(len(jobs) + 1):
                    J = base + j
                    if j < len(jobs):
                        segs = job(*jobs[j])[0]
                        n = segs[0]["n"]
                        act.wait_ge(sem("att_logits"), J + 1)
                        if J > 1:
                            act.wait_ge(sem("att_pt"), J - 1)
                        src = bank(2 * (j % 2), 2).rearrange("p (s n) -> p s n", n=T)[:, 0:len(segs), 0:n]
                        dst = att_p[:, j % 2, :].rearrange("p (s n) -> p s n", n=T)[:, 0:len(segs), 0:n]
                        act.activation(dst, src, ACT.Exp, bias=nmax[:, j % 2:j % 2 + 1],
                                       accum_out=esum[:, j % 4:j % 4 + 1]).then_inc(sem("att_exp"), 1)
                    if j >= 1:
                        J1 = J - 1
                        nb = sum(len(sg["v"]) for sg in job(*jobs[j - 1])[0])
                        act.wait_ge(sem("att_pt"), J1 + 1)
                        if J1 > 0:
                            act.wait_ge(sem("att_pv"), J1)
                        act.activation(att_pt[:, 0:P * nb], bank(4, 2)[:, 0:P * nb], ACT.Copy)\
                           .then_inc(sem("att_pts"), 1)

            act.wait_ge(sem("cols_in"), 80)
            act.wait_ge(sem("keep_in"), 16)

            act.wait_ge(sem("c_in"), 16)
            act.activation(csilu[:, :], cact[:, :], ACT.Silu).then_inc(sem("silu_done"), 1)

            def modulation(layer):
                act.wait_ge(sem("mod_rows"), layer + 1)
                for j in range(2):
                    act.activation(grow[layer][j], bank(2 * j, 2), ACT.Copy).then_inc(sem("mod_rows_in"), 1)

            modulation(0)
            norm("n_even")
            gemm("even_in")
            act.wait_ge(sem("ev_act"), 7)
            act.wait_ge(sem("ev_dve"), 7)
            act.activation(proj_e[:, :, 1536:2048], proj_e[:, :, 1536:2048], ACT.Silu).then_inc(sem("even_gate"), 1)
            transposes("ret_qk")
            for h in range(4):
                act.wait_ge(sem("ret_pv"), h + 1)
                act.activation(xn[:, :, P * h:P * h + P], bank(2 + h % 2)[:, 0:T].rearrange("p (t n) -> p t n", t=NT),
                               ACT.Copy).then_inc(sem("ret_moved"), 1)
            heads(0)
            heads(1)
            transposes("att_qk")
            attention("att")
            transposes("even_mix")

            def router(layer):
                act.wait_ge(sem("router_ps"), layer + 1)
                act.activation(rt_sc, bank(4)[:, 0:2 * NE], ACT.Sigmoid).then_inc(sem("router_sig"), 1)
                for b in range(0, 8, 2):
                    act.wait_ge(sem("comb_ps"), 8 * layer + b + 1)
                    act.activation(flat(comb_b[:, 2 * b:2 * b + 2, :]), bank(b), ACT.Copy).then_inc(sem("comb_act"), 1)

            norm("n_moe0")
            router(0)
            swiglu("moe0")
            act.wait_ge(sem("x_new"), 2)
            modulation(1)
            norm("n_odd")
            gemm("odd_in")
            for s_ in range(17):
                if s_ < 16:
                    h = s_
                    act.wait_ge(sem("sb_z"), h + 1)
                    if h > 1:
                        act.wait_ge(sem("sb_soft"), h - 1)
                    step(act.activation(sb_abs[h % 2], bank(h % 2)[:, 0:384], ACT.Abs))
                    step(act.activation(sb_abs[h % 2], sb_abs[h % 2], ACT.Exp, scale=-1.0))
                    act.activation(sb_abs[h % 2], sb_abs[h % 2], ACT.Ln, bias=1.0).then_inc(sem("sb_ln"), 1)
                if s_ >= 1:
                    h = s_ - 1
                    act.wait_ge(sem("sb_sums"), h + 1)
                    if h > 1:
                        act.wait_ge(sem("sb_pv"), h - 1)
                    act.activation(sb_a[h % 2], bank(2 + h % 2)[:, 0:384], ACT.Exp).then_inc(sem("sb_exp"), 1)
            transposes("odd_mix")
            norm("n_moe1")
            router(1)
            swiglu("moe1")
            norm("n_pre0")
            swiglu("pre0")
            norm("n_mem0")
            gemm("mem0")
            heads(2)
            transposes("mem0_k")
            norm("n_mix0")
            gemm("a_in")
            heads(3)
            transposes("mem0_q")
            attention("mem0")
            act.wait_ge(sem("shift_mixed"), SHIFT_TILES)
            act.activation(F[0:64, 18, :], F[0:64, 18, :], ACT.Tanh).then_inc(sem("rw_low"), 1)
            act.activation(F[:, 19, :], F[:, 19, :], ACT.Sigmoid).then_inc(sem("rw_low"), 1)
            act.wait_ge(sem("rw_w_ps"), 1)
            for i in range(6):
                m = act.activation(W[0][:, i, :], bank(i // 2)[:, T * (i % 2):T * (i % 2) + T], ACT.Sigmoid,
                                   bias=rcols[:, 20 + i:21 + i])
            m.then_inc(sem("rw_sig"), 1)
            act.wait_ge(sem("rw_a_ps"), 1)
            for i in range(6):
                m = act.activation(W[1][:, i, :], bank(3 + i // 2)[:, T * (i % 2):T * (i % 2) + T], ACT.Sigmoid,
                                   bias=rcols[:, 26 + i:27 + i])
            m.then_inc(sem("rw_sig"), 1)
            act.wait_ge(sem("rw_g_ps"), 1)
            for n in range(3):
                m = act.activation(flat(gate)[:, 512 * n:512 * n + 512], bank((6 + n) % 8), ACT.Copy)
            m.then_inc(sem("rw_gate"), 1)
            act.wait_ge(sem("rw_ssr"), 1)
            act.activation(Wf[5], Wf[5], ACT.Sqrt).then_inc(sem("rw_kkn"), 1)
            act.wait_ge(sem("rw_prev"), 1)
            act.activation(Wf[0], Wf[0], ACT.Exp, scale=-DECAY).then_inc(sem("rw_dec"), 1)
            act.wait_ge(sem("rw_decayed"), 1)
            act.activation(Wf[0], Wf[2], ACT.Exp, scale=DECAY).then_inc(sem("rw_dec"), 1)
            act.wait_ge(sem("rw_decayed"), 2)
            act.activation(Wf[0], Wf[2], ACT.Exp, scale=-DECAY).then_inc(sem("rw_dec"), 1)
            for nm in ("rw_v", "rw_b", "rw_k"):
                transposes(nm)
            for i in range(6):
                for l in range(5):
                    act.wait_ge(sem("rw_x_ps"), 5 * i + l + 1)
                    if 5 * i + l > 0:
                        act.wait_ge(sem("rw_tx_ps"), 5 * i + l)
                    act.activation(flat(t_x), bank(4), ACT.Copy).then_inc(sem("rw_x"), 1)
                act.wait_ge(sem("rw_u_ps"), i + 1)
                act.activation(U[:, :, P * i:P * i + P], bank(7)[:, 0:T].rearrange("p (t n) -> p t n", t=NT),
                               ACT.Copy).then_inc(sem("rw_u"), 1)
            for c in range(4):
                t, rows = c // 2, slice(64 * (c % 2), 64 * (c % 2) + 64)
                act.wait_ge(sem("rw_y_ps"), c + 1)
                act.activation(y_r[rows, t, :], bank(2, 2)[rows, 0:768], ACT.Copy).then_inc(sem("rw_y"), 1)
            act.wait_ge(sem("rw_yvar"), 1)
            act.activation(hrstd, hvar, ACT.Sqrt).then_inc(sem("rw_yrstd"), 1)
            transposes("a_mix")
            norm("n_post0")
            swiglu("post0")
            norm("n_kv")
            gemm("kv")
            heads(4)
            transposes("kd")
            norm("n_pre1")
            swiglu("pre1")
            norm("n_mem1")
            gemm("mem1")
            heads(5)
            transposes("mem1_k")
            norm("n_mix1")
            gemm("b_q")
            heads(6)
            transposes("dil_q")
            attention("mem1")
            attention("dil")
            transposes("b_mix")
            norm("n_post1")
            swiglu("post1")

        @block.vector
        def _(dve):
            done = [0]

            def step(ins):
                done[0] += 1
                ins.then_inc(sem("dve_step"), 1)
                dve.wait_ge(sem("dve_step"), done[0])

            def norm(nm):
                n = NORMS.index(nm)
                dve.wait_ge(sem("norm_ss"), 2 * (n + 1))
                step(dve.tensor_scalar(var, ss, 1.0 / D, EPS, ALU.mult, ALU.add))
                dve.reciprocal(var, var).then_inc(sem("norm_var"), 1)
                dve.wait_ge(sem("norm_rstd"), n + 1)
                for t in range(NT):
                    dve.tensor_scalar(xn[:, t, :], NSRC[nm][:, t, :], rstd[:, t:t + 1], None, ALU.mult)\
                       .then_inc(sem("norm_xn"), 1)
                for j in (2, 3, 6, 7):
                    b = j // 2
                    dve.wait_ge(sem("norm_T"), 4 * n + b + 1)
                    if nm in NSHIFT:
                        m = dve.tensor_scalar(hT[:, j, :], bank(b)[:, T * (j % 2):T * (j % 2) + T], NGAIN[nm][:, j:j + 1],
                                              NSHIFT[nm][:, j:j + 1], ALU.mult, ALU.add)
                    else:
                        m = dve.tensor_scalar(hT[:, j, :], bank(b)[:, T * (j % 2):T * (j % 2) + T], NGAIN[nm][:, j:j + 1], None, ALU.mult)
                    m.then_inc(sem("norm_dve"), 1)

            def gemm(nm):
                g = PL.gemms[nm]
                for c in range(g["n"]):
                    G = g["base"] + c
                    kind, dst = gemm_dst(nm, c)
                    dve.wait_ge(sem("gemm_done"), G + 1)
                    pair = 2 * (G % 4)
                    ps = bank(pair + 1)
                    if kind == "copy":
                        d = dst[:, 1, :]
                        dve.tensor_copy(d, ps[:, 0:d.shape[1]]).then_inc(sem("ev_dve"), 1)
                    elif kind == "feat":
                        dve.tensor_scalar(flat(dst[:, 2:4, :]), ps, 0.125 if c < 2 else 1.0, None, ALU.mult)\
                           .then_inc(sem("ev_dve"), 1)
                    elif kind == "kv":
                        for lo, hi, d, o in KV_PARTS[c]:
                            m = dve.tensor_copy(d[:, 1, o:o + hi - lo], ps[:, lo:hi])
                        m.then_inc(sem("ev_dve"), 1)
                    elif kind == "shift":
                        for f in range(4):
                            n = 4 * c + f
                            dve.wait_ge(sem("shift_mu"), n - n % 2 + 2)
                            m = dve.scalar_tensor_tensor(
                                out=F[:, n, :], in0=bank(pair + f // 2)[:, T * (f % 2):T * (f % 2) + T],
                                scalar=omu[:, n:n + 1], in1=sh_tmp[n % 4][:, 0:T], op0=ALU.mult, op1=ALU.add)
                            m.then_inc(sem("shift_mixed"), 1)
                    else:
                        cols = slice(512 * c, 512 * c + 512)
                        both = psum[:, pair:pair + 2, :]
                        if kind == "resid_g":
                            row = grow[dst[0]][0][:, cols].unsqueeze(1)
                            step(dve.tensor_tensor(xn[:, :, cols], both, bc(row, [P, NT, 512]), ALU.mult))
                            m = dve.tensor_tensor(x[:, :, cols], x[:, :, cols], xn[:, :, cols], ALU.add)
                        else:
                            m = dve.tensor_tensor(x[:, :, cols], x[:, :, cols], both, ALU.add)
                        if c == 1:
                            m.then_inc(sem("x_new"), 1)
                        else:
                            m.then_inc(sem("resid_first"), 1)

            def transposes(nm):
                for i, (srcs, dst) in enumerate(TRS[nm]):
                    B = TR_BASE[nm] + i
                    if B % 2 == 1:
                        dve.wait_ge(sem("tr_done"), B + 1)
                        dve.tensor_copy(dst, bank(4 + B % 4)[:, 0:P * len(srcs)]).then_inc(sem("tr_dve"), 1)

            def heads(n, parts, width, gains, scale=1.0):
                col = 0
                for v in parts:
                    H = v.shape[1]
                    sq = pool[:, XN:XN + H * width].rearrange("p (h d) -> p h d", h=H) if n > 1 else \
                        pool[:, WORK + 4992:WORK + 4992 + H * width].rearrange("p (h d) -> p h d", h=H)
                    step(dve.tensor_tensor(sq, v, v, ALU.mult))
                    m = dve.tensor_reduce(hss[:, col:col + H], sq, AX.X, ALU.add)
                    step(m)
                    col += H
                if col < 32:
                    step(dve.memset(hss[:, col:32], 1.0))
                step(dve.tensor_scalar(hvar, hss, 1.0 / width, EPS, ALU.mult, ALU.add))
                dve.reciprocal(hvar, hvar).then_inc(sem("heads_var"), 1)
                dve.wait_ge(sem("heads_rstd"), n + 1)
                col = 0
                for v in parts:
                    H = v.shape[1]
                    m = dve.tensor_tensor(v, v, bc(hrstd[:, col:col + H].unsqueeze(2), [P, H, width]), ALU.mult)
                    col += H
                    step(m)
                    for lo, hi, g, s in gains:
                        vv = v[:, lo:hi, :]
                        step(dve.scalar_tensor_tensor(out=vv, in0=vv, scalar=s,
                                                      in1=bc(gains64[:, g, :].unsqueeze(1), [P, hi - lo, width]),
                                                      op0=ALU.mult, op1=ALU.mult))

            def attention(kind):
                jobs, base = JOBS[kind], JOB_BASE[kind]
                for j in range(len(jobs) + 2):
                    J = base + j
                    if j < len(jobs):
                        segs = job(*jobs[j])[0]
                        n = segs[0]["n"]
                        dve.wait_ge(sem("att_scores"), J + 1)
                        if J > 1:
                            dve.wait_ge(sem("att_exp"), J - 1)
                        lg = bank(2 * (j % 2), 2).rearrange("p (s n) -> p s n", n=T)
                        step(dve.tensor_reduce(mx[:, j % 2:j % 2 + 1], lg[:, 0:len(segs), 0:n], AX.XY, ALU.max))
                        dve.tensor_scalar(nmax[:, j % 2:j % 2 + 1], mx[:, j % 2:j % 2 + 1], -1.0, None, ALU.mult)\
                           .then_inc(sem("att_logits"), 1)
                    if j >= 2:
                        o = job(*jobs[j - 2])[1]
                        if J > 1:
                            dve.wait_ge(sem("att_pv"), J - 1)
                        step(dve.reciprocal(erec[:, j % 2:j % 2 + 1], esum[:, (j - 2) % 4:(j - 2) % 4 + 1]))
                        dve.tensor_scalar(o, bank(6 + j % 2)[:, 0:64], erec[:, j % 2:j % 2 + 1], None, ALU.mult)\
                           .then_inc(sem("att_o"), 1)

            def swiglu(nm):
                s = PL.swi[nm]
                G0 = s["base"]
                moe = nm.startswith("moe")

                def product(c, q, e):
                    dve.wait_ge(sem("silu_done"), G0 + c + 2)
                    dve.wait_ge(sem("up_done"), G0 + c + 1)
                    h = hid[q % 2]
                    m = dve.tensor_tensor(flat(h), flat(h), bank(5 + 2 * (q % 2)), ALU.mult)
                    if moe:
                        m.then_inc(sem("hid_prod"), 1)
                        dve.wait_ge(sem("hid_prod"), G0 + c + 1)
                        m = dve.tensor_tensor(h[:, :, :], h[:, :, :],
                                              bc(comb_b[:, e, :].unsqueeze(1), [P, 2, T]), ALU.mult)
                    m.then_inc(sem("hid_ready"), 1)

                def ada_part(i, q):
                    dve.wait_ge(sem("ada1_landed"), 32 * i + 16 * q + 16)
                    half = acc[:, q * ADA_HALF:(q + 1) * ADA_HALF]
                    dve.scalar_tensor_tensor(out=half, in0=ada1, scalar=csilu[:, bass.ds(i, 1)], in1=half,
                                             op0=ALU.mult, op1=ALU.add).then_inc(sem("ada_used"), 1)

                if nm == "moe0":
                    dve.wait_ge(sem("ada_b_in"), 32)
                loops = (s["n"] - 1) // 4
                with dve.Fori(0, loops) as i:
                    for q in range(4):
                        product(4 * i + q, q, 2 * i + q // 2)
                        if nm == "moe0" and q % 2:
                            ada_part(i, q // 2)
                for c in range(4 * loops, s["n"]):
                    product(c, c % 4, c // 2)
                    if nm == "moe0" and c % 2:
                        ada_part(loops, (c % 4) // 2)
                dve.wait_ge(sem("sums_done"), s["no"] + 1)
                for t in range(NT):
                    ps = bank(2 * t, 2)
                    if moe:
                        step(dve.tensor_tensor(xn[:, t, :], ps, grow[int(nm[-1])][1], ALU.mult))
                        m = dve.tensor_tensor(x[:, t, :], x[:, t, :], xn[:, t, :], ALU.add)
                    else:
                        m = dve.scalar_tensor_tensor(out=x[:, t, :], in0=ps, scalar=0.5, in1=x[:, t, :],
                                                     op0=ALU.mult, op1=ALU.add)
                    m.then_inc(sem("x_new" if t else "x_part"), 1)

            def mod_cols(layer):
                dve.wait_ge(sem("mod_cols"), layer + 1)
                step(dve.tensor_copy(mcols[:, layer].rearrange("p j k -> p (j k)"), bank(4)[:, 0:4 * KD]))
                for j in range(2):
                    m = dve.scalar_tensor_tensor(out=mgain[:, 2 * layer + j, :], in0=mcols[:, layer, 1 + 2 * j, :],
                                                 scalar=1.0, in1=gcols[:, layer + 2 * j, :], op0=ALU.add, op1=ALU.mult)
                m.then_inc(sem("mod_moved"), 1)

            dve.wait_ge(sem("bias_ps"), 2)
            dve.wait_ge(sem("hot_in"), 80)
            dve.tensor_copy(view(WORK + 4256, 512)[0:8, :], bank(6)[0:8, :]).then_inc(sem("bias_rows"), 1)
            dve.tensor_tensor(view(WORK + 4768, 512)[0:12, :], bank(7)[0:12, :], view(WORK + 2176, 4, 512)[0:12, 3, :],
                              ALU.add).then_inc(sem("bias_rows"), 1)
            dve.wait_ge(sem("cols_in"), 80)
            dve.tensor_scalar(omu[:, :], rcols[:, 0:SHIFT_TILES], -1.0, 1.0, ALU.mult, ALU.add).then_inc(sem("hid_ready"), 1)
            dve.wait_ge(sem("silu_done"), 1)
            dve.wait_ge(sem("ada_b_in"), 16)
            for b in range(ADA_BLOCKS):
                t, q = b // 2, b % 2
                dve.wait_ge(sem(f"landed{b % SLOTS}"), 16 * (b // SLOTS + 1))
                half = acc[:, q * ADA_HALF:(q + 1) * ADA_HALF]
                if b >= 2:
                    if b > 1:
                        dve.wait_ge(sem("ada_used"), b - 1)
                dve.scalar_tensor_tensor(out=half, in0=slot(b)[:, 0:ADA_HALF], scalar=csilu[:, t:t + 1], in1=half,
                                         op0=ALU.mult, op1=ALU.add).then_inc(sem("ada_used"), 1)
            mod_cols(0)
            dve.wait_ge(sem("keep_in"), 16)
            norm("n_even")
            gemm("even_in")
            dve.wait_ge(sem("ev_act"), 7)
            dve.wait_ge(sem("ev_dve"), 7)
            dve.wait_ge(sem("even_in"), 16)
            dve.wait_ge(sem("bias_out"), 32)
            for t in range(NT):
                v = proj_e[:, t, 0:1024].rearrange("p (h d) -> p h d", h=8)
                x1, x2 = v[:, :, 0:64], v[:, :, 64:128]
                co = bc(rope_c[:, t, :].unsqueeze(1), [P, 8, 64])
                si = bc(rope_s[:, t, :].unsqueeze(1), [P, 8, 64])
                r = [z.rearrange("p (h d) -> p h d", h=8) for z in (rot_a[:, 0, :], rot_a[:, 1, :],
                                                                    rot_b[:, 0, :], rot_b[:, 1, :])]
                dve.tensor_tensor(r[0], x1, co, ALU.mult)
                dve.tensor_tensor(r[1], x2, si, ALU.mult)
                dve.tensor_tensor(r[2], x1, si, ALU.mult)
                step(dve.tensor_tensor(r[3], x2, co, ALU.mult))
                dve.tensor_tensor(x1, r[0], r[1], ALU.subtract)
                step(dve.tensor_tensor(x2, r[2], r[3], ALU.add))
            dve.memset(tiny[:, 160:161], 0.0).then_inc(sem("rotated"), 1)
            transposes("ret_qk")
            for h in range(4):
                dve.wait_ge(sem("ret_scores"), h + 1)
                if h > 1:
                    dve.wait_ge(sem("ret_pv"), h - 1)
                dve.tensor_tensor(ret_s[:, h % 2, :], bank(h % 2)[:, 0:384], decay_t[:, h, :], ALU.mult)\
                   .then_inc(sem("ret_decayed"), 1)
            dve.wait_ge(sem("norm_T"), 4)
            qk = [proj_e[:, t, 2048:3072].rearrange("p (h d) -> p h d", h=16) for t in range(NT)]
            heads(0, qk, 64, [(0, 8, 0, 0.125), (8, 16, 1, 1.0)])
            dve.memset(tiny[:, 160:161], 0.0).then_inc(sem("heads_ok"), 1)
            dve.wait_ge(sem("ret_moved"), 4)
            rr = [xn[:, t, 0:512].rearrange("p (h d) -> p h d", h=4) for t in range(NT)]
            heads(1, rr, P, [])
            dve.wait_ge(sem("even_gate"), 1)
            dve.tensor_tensor(xn[:, :, 0:512], xn[:, :, 0:512], proj_e[:, :, 1536:2048], ALU.mult)\
               .then_inc(sem("even_mixed"), 1)
            transposes("att_qk")
            attention("att")
            transposes("even_mix")
            gemm("even_out")

            def router(layer):
                dve.wait_ge(sem("router_sig"), layer + 1)
                sel, cmp_, eq = rt[:, 32:64], rt[:, 64:192], rt[:, 192:320]
                rank, pick, gs = rt[:, 320:352], rt[:, 352:384], rt[:, 384:392]
                gpick, tot = rt[:, 392:400], rt[:, 400:402]
                step(dve.tensor_tensor(sel.rearrange("p (t e) -> p t e", t=NT), rt_sc.rearrange("p (t e) -> p t e", t=NT),
                                       bc(router_b[:, :].unsqueeze(1), [P, NT, NE]), ALU.add))

                def ranks(v, groups, out_):
                    n = 16 * groups
                    v3 = v.rearrange("p (g e) -> p g e", e=4)
                    other = bc(v3.unsqueeze(2), [P, groups, 4, 4])
                    own = bc(v3.unsqueeze(3), [P, groups, 4, 4])
                    c4 = cmp_[:, 0:n].rearrange("p (g e j) -> p g e j", g=groups, e=4)
                    q4 = eq[:, 0:n].rearrange("p (g e j) -> p g e j", g=groups, e=4)
                    dve.tensor_tensor(c4, other, own, ALU.is_gt)
                    step(dve.tensor_tensor(q4, other, own, ALU.is_equal))
                    step(dve.tensor_tensor(eq[:, 0:n].rearrange("p (g k) -> p g k", g=groups),
                                           eq[:, 0:n].rearrange("p (g k) -> p g k", g=groups),
                                           bc(K["lower"].unsqueeze(1), [P, groups, 16]), ALU.mult))
                    step(dve.tensor_tensor(cmp_[:, 0:n], cmp_[:, 0:n], eq[:, 0:n], ALU.add))
                    step(dve.tensor_reduce(out_, cmp_[:, 0:n].rearrange("p (g j) -> p g j", j=4), AX.X, ALU.add))

                ranks(sel, 8, rank)
                step(dve.tensor_scalar(pick, rank, 1.5, None, ALU.is_lt))
                step(dve.tensor_tensor(sel, sel, pick, ALU.mult))
                step(dve.tensor_reduce(gs, sel.rearrange("p (g e) -> p g e", e=4), AX.X, ALU.add))
                ranks(gs, 2, gpick)
                step(dve.tensor_scalar(gpick, gpick, 0.5, None, ALU.is_lt))
                step(dve.tensor_tensor(pick.rearrange("p (g e) -> p g e", e=4), pick.rearrange("p (g e) -> p g e", e=4),
                                       bc(gpick.unsqueeze(2), [P, 8, 4]), ALU.mult))
                step(dve.tensor_tensor(pick, pick, rt_sc, ALU.mult))
                step(dve.tensor_reduce(tot, pick.rearrange("p (t e) -> p t e", t=NT), AX.X, ALU.add))
                step(dve.reciprocal(tot, tot))
                dve.tensor_tensor(comb_tok.rearrange("p (t e) -> p t e", t=NT), pick.rearrange("p (t e) -> p t e", t=NT),
                                  bc(tot.unsqueeze(2), [P, NT, NE]), ALU.mult).then_inc(sem("comb_tok"), 1)
                dve.wait_ge(sem("comb_T_ps"), layer + 1)
                dve.tensor_copy(comb_t, bank(5)[0:NE, 0:T]).then_inc(sem("comb_T"), 1)
                for b in range(1, 8, 2):
                    dve.wait_ge(sem("comb_ps"), 8 * layer + b + 1)
                    dve.tensor_copy(flat(comb_b[:, 2 * b:2 * b + 2, :]), bank(b)).then_inc(sem("comb_dve"), 1)

            norm("n_moe0")
            router(0)
            dve.memset(tiny[:, 160:161], 0.0).then_inc(sem("moe_ready"), 1)
            swiglu("moe0")
            mod_cols(1)
            dve.wait_ge(sem("mod_rows_in"), 4)
            norm("n_odd")
            gemm("odd_in")
            step(dve.memset(sb_zero, 0.0))
            for s_ in range(18):
                if s_ < 16:
                    h = s_
                    dve.wait_ge(sem("sb_ln"), h + 1)
                    if h > 1:
                        dve.wait_ge(sem("sb_sums"), h - 1)
                    dve.scalar_tensor_tensor(out=sb_sp[h % 2], in0=bank(h % 2)[:, 0:384], scalar=0.0, in1=sb_abs[h % 2],
                                             op0=ALU.max, op1=ALU.add).then_inc(sem("sb_soft"), 1)
                    dve.wait_ge(sem("sb_soft"), h + 1)
                    diag = sb_sp[h % 2].rearrange("p (b n) -> p b n", b=3)
                    dve.copy_predicated(diag[:, 0, :], K["neg_from"].bitcast(U32), sb_zero)
                    dve.copy_predicated(diag[:, 2, :], K["neg_from"].bitcast(U32), sb_zero)\
                       .then_inc(sem("sb_masked"), 1)
                if 1 <= s_ <= 16:
                    h = s_ - 1
                    dve.wait_ge(sem("sb_exp"), h + 1)
                    diag = sb_a[h % 2].rearrange("p (b n) -> p b n", b=3)
                    dve.copy_predicated(diag[:, 0, :], K["neg_from"].bitcast(U32), sb_zero)
                    dve.copy_predicated(diag[:, 2, :], K["neg_from"].bitcast(U32), sb_zero)\
                       .then_inc(sem("sb_weights"), 1)
                if s_ >= 2:
                    h = s_ - 2
                    dve.wait_ge(sem("sb_pv"), h + 1)
                    dve.tensor_copy(xn[:, :, 64 * h:64 * h + 64],
                                    bank(4 + h % 2)[:, 0:128].rearrange("p (t d) -> p t d", t=NT))\
                       .then_inc(sem("sb_out"), 1)
            transposes("odd_mix")
            gemm("odd_out")
            norm("n_moe1")
            router(1)
            swiglu("moe1")
            norm("n_pre0")
            swiglu("pre0")
            norm("n_mem0")
            gemm("mem0")

            def mem_keys(n, q):
                for e in moved(f"mem{q}", 0):
                    dve.wait_ge(sem(e[0]), e[1])
                mk = [mem_kv[:, t, 0:256].rearrange("p (h d) -> p h d", h=4) for t in range(NT)]
                dve.wait_ge(sem("norm_T"), 4 * (NORMS.index(f"n_mem{q}") + 1))
                heads(n, mk, 64, [(0, 4, 4 + q, 1.0)])
                dve.tensor_copy(mem_v, mem_kv[:, :, 256:512]).then_inc(sem("heads_ok"), 1)
                transposes(f"mem{q}_k")

            mem_keys(2, 0)
            norm("n_mix0")
            for z in sh_tmp:
                m = dve.memset(z[:, 0:1], 0.0)
            step(m)
            gemm("a_in")
            dve.wait_ge(sem("shift_mixed"), SHIFT_TILES)
            dve.wait_ge(sem("rwkv_in"), 96)
            par = slot(PL.gemms["a_in"]["first"] + 6)
            for e in moved("a_in", 5):
                dve.wait_ge(sem(e[0]), e[1])
            mq = [q_mem_a[:, t, :].rearrange("p (h d) -> p h d", h=4) for t in range(NT)]
            dve.wait_ge(sem("norm_T"), 4 * (NORMS.index("n_mix0") + 1))
            heads(3, mq, 64, [(0, 4, 2, 0.125)])
            dve.memset(tiny[:, 160:161], 0.0).then_inc(sem("heads_ok"), 1)
            transposes("mem0_q")
            attention("mem0")
            for i in range(6):
                m = dve.tensor_scalar(W[3][:, i, :], Fk[:, i, :], rcols[:, 32 + i:33 + i], None, ALU.mult)
            step(m)
            dve.tensor_tensor(Wf[4], Wf[3], Wf[3], ALU.mult).then_inc(sem("rw_sq"), 1)
            dve.wait_ge(sem("rw_sig"), 1)
            dve.wait_ge(sem("reset_in"), 16)
            for i in range(6):
                m = dve.tensor_tensor_scan(W[2][:, i, :], rw_reset, W[0][:, i, :], 0.0, ALU.mult, ALU.add)
            step(m)
            dve.tensor_tensor(Wf[0], Wf[2], Wf[0], ALU.subtract).then_inc(sem("rw_prev"), 1)
            dve.wait_ge(sem("rw_ss_ps"), 1)
            dve.tensor_scalar(Wf[5], bank(3, 3), 1e-24, None, ALU.max).then_inc(sem("rw_ss"), 1)
            dve.wait_ge(sem("rw_ss"), 1)
            dve.reciprocal(Wf[5], Wf[5]).then_inc(sem("rw_ssr"), 1)
            dve.wait_ge(sem("rw_sig"), 2)
            for i in range(6):
                m = dve.tensor_scalar(W[4][:, i, :], W[1][:, i, :], -1.0, rcols[:, 38 + i:39 + i], ALU.add, ALU.mult)
            step(m)
            step(dve.scalar_tensor_tensor(out=flat(Fk), in0=Wf[4], scalar=1.0, in1=flat(Fk), op0=ALU.add, op1=ALU.mult))
            for i in range(6):
                m = dve.scalar_tensor_tensor(out=W[4][:, i, :], in0=Fr[:, i, :], scalar=rcols[:, 44 + i:45 + i],
                                             in1=Fk[:, i, :], op0=ALU.mult, op1=ALU.mult)
            m.then_inc(sem("rw_rk"), 1)
            dve.wait_ge(sem("rw_kkn"), 1)
            step(dve.tensor_tensor(Wf[3], Wf[3], Wf[5], ALU.mult))
            step(dve.tensor_tensor(Wf[1], Wf[1], Wf[3], ALU.mult))
            dve.wait_ge(sem("rw_dec"), 1)
            dve.tensor_tensor(Wf[3], Wf[3], Wf[0], ALU.mult).then_inc(sem("rw_decayed"), 1)
            dve.wait_ge(sem("rw_dec"), 2)
            dve.tensor_tensor(Wf[5], Wf[1], Wf[0], ALU.mult)
            dve.tensor_tensor(flat(Fk), flat(Fk), Wf[0], ALU.mult).then_inc(sem("rw_decayed"), 1)
            dve.wait_ge(sem("rw_dec"), 3)
            dve.tensor_tensor(flat(Fr), flat(Fr), Wf[0], ALU.mult)
            for c in range(4):
                m = dve.tensor_copy(pend[:, :, c:c + 1], W[0][:, :, 64 * c + 63:64 * c + 64])
            step(m)
            dve.wait_ge(sem("rw_bonus_ps"), 1)
            dve.tensor_copy(bonus, bank(1)[:, 0:24]).then_inc(sem("rw_bonus"), 1)
            dve.memset(state, 0.0).then_inc(sem("rw_scaled"), 1)
            for nm in ("rw_v", "rw_b", "rw_k"):
                transposes(nm)
            levels = par[:, 3072:3712].rearrange("p (l n) -> p l n", l=5)
            lvl0_t, lvl0, strict = par[:, 3712:3840], par[:, 3840:3968], par[:, 3968:4096]

            def four(m_):
                return bc(m_.unsqueeze(1), [P, 4, P])

            for i in range(6):
                dve.wait_ge(sem("rw_l_ps"), i + 1)
                pv = psum[:, 0:2, 0:T].rearrange("p e (t n) -> p e t n", t=NT)
                lo_ = psum[:, 0:2, T:2 * T].rearrange("p e (t n) -> p e t n", t=NT)
                if i > 0:
                    dve.wait_ge(sem("rw_u_ps"), i)
                if i == 0:
                    dve.wait_ge(sem("tr_act"), tr_counts("rw_v")[0])
                    dve.wait_ge(sem("tr_act"), tr_counts("rw_k")[0])
                m = None
                lt4 = t_lt.rearrange("p (e t) n -> p e t n", e=2)
                x4 = t_lm.rearrange("p (e t) n -> p e t n", e=2)
                for e in range(2):
                    dve.tensor_tensor(lt4[:, e], pv[:, e], bc(strict.unsqueeze(1), [P, 2, P]), ALU.mult)
                    m = dve.tensor_tensor(x4[:, e], lo_[:, e], bc(lvl0.unsqueeze(1), [P, 2, P]), ALU.mult)
                step(m)
                step(dve.tensor_tensor(t_t, four(ident), t_lm, ALU.subtract))
                step(dve.tensor_tensor(t_lm, t_lt, four(lvl0_t), ALU.mult))
                step(dve.tensor_tensor(TT[:, i], four(ident), t_lm, ALU.subtract))
                for l in range(5):
                    dve.tensor_tensor(t_lm, t_lt, four(levels[:, l, :]), ALU.mult).then_inc(sem("rw_lm"), 1)
                    dve.wait_ge(sem("rw_tx_ps"), 5 * i + l + 1)
                    dve.tensor_tensor(flat(t_t), flat(t_t), bank(5), ALU.subtract)
                    step(dve.tensor_tensor(TT[:, i].rearrange("p m n -> p (m n)"), TT[:, i].rearrange("p m n -> p (m n)"),
                                           bank(6), ALU.subtract))
                for e in range(2):
                    m = dve.tensor_tensor(x4[:, e], psum[:, 2 + e, 0:T].rearrange("p (t n) -> p t n", t=NT),
                                          bc(strict.unsqueeze(1), [P, 2, P]), ALU.mult)
                m.then_inc(sem("rw_m"), 1)
                dve.wait_ge(sem("rw_m"), i + 1)
                dve.memset(tiny[:, 161:162], 0.0).then_inc(sem("rw_t"), 1)
            step(dve.memset(SA, 0.0))
            dve.memset(tiny[:, 161:162], 0.0).then_inc(sem("rw_state"), 1)
            for c in range(4):
                t, q0 = c // 2, 64 * (c % 2)
                rows = slice(q0, q0 + 64)
                dve.wait_ge(sem("rw_z_ps"), c + 1)
                dve.wait_ge(sem("rw_u"), 6)
                dve.tensor_tensor(Z, bank(0, 2)[:, 0:768], U[:, t, :], ALU.add).then_inc(sem("rw_z"), 1)
                dve.wait_ge(sem("rw_sa_ps"), c + 1)
                dve.tensor_scalar(SA[rows, t, :], bank(4, 2)[rows, 0:768], -1.0, None, ALU.mult)\
                   .then_inc(sem("rw_sa"), 1)
                dve.wait_ge(sem("rw_new_ps"), c + 1)
                dve.wait_ge(sem("rw_y_ps"), c + 1)
                for e in range(2):
                    hf = slice(64 * e, 64 * e + 64)
                    st = state[hf, :, hf]
                    new = bank(6, 2)[hf, 0:768].rearrange("p (i n) -> p i n", i=6)[:, :, hf]
                    m = dve.tensor_tensor(st, st, new, ALU.add)
                step(m)
                for e in range(2):
                    hf = slice(64 * e, 64 * e + 64)
                    st = state[hf, :, hf]
                    m = dve.tensor_tensor(st, st, bc(pend[hf, :, c:c + 1], [64, 6, 64]), ALU.mult)
                m.then_inc(sem("rw_state"), 1)
            for i in range(6):
                dve.wait_ge(sem("rw_bk_ps"), i + 1)
                if i > 0:
                    dve.wait_ge(sem("rw_g2_ps"), i)
                for e in range(2):
                    inc = bc(K["chunk_incl"].unsqueeze(1), [P, 2, P])
                    dve.tensor_tensor(bm[:, 2 * e:2 * e + 2, :], psum[:, e, 0:T].rearrange("p (t n) -> p t n", t=NT),
                                      inc, ALU.mult)
                    m = dve.tensor_tensor(km[:, 2 * e:2 * e + 2, :], psum[:, 2 + e, 0:T].rearrange("p (t n) -> p t n", t=NT),
                                          inc, ALU.mult)
                m.then_inc(sem("rw_bk"), 1)
                dve.wait_ge(sem("rw_g2_ps"), i + 1)
                dve.wait_ge(sem("rw_y"), 4)
                yy = y_r[:, :, P * i:P * i + P]
                dve.tensor_tensor(yy, yy, bank(4)[:, 0:T].rearrange("p (t n) -> p t n", t=NT), ALU.add)\
                   .then_inc(sem("rw_yadd"), 1)
            dve.wait_ge(sem("rw_yadd"), 6)
            ys = [y_r[:, t, :].rearrange("p (h d) -> p h d", h=12) for t in range(NT)]
            ycs = [yc[:, t, :].rearrange("p (h d) -> p h d", h=12) for t in range(NT)]
            for t in range(NT):
                m = dve.tensor_reduce(hss[:, 12 * t:12 * t + 12], ys[t], AX.X, ALU.add)
            step(m)
            step(dve.tensor_scalar(hss[:, 0:24], hss[:, 0:24], 1.0 / 64, None, ALU.mult))
            for t in range(NT):
                m = dve.tensor_tensor(ycs[t], ys[t], bc(hss[:, 12 * t:12 * t + 12].unsqueeze(2), [P, 12, 64]), ALU.subtract)
            step(m)
            for t in range(NT):
                m = dve.tensor_tensor(ys[t], ycs[t], ycs[t], ALU.mult)
            step(m)
            for t in range(NT):
                m = dve.tensor_reduce(hss[:, 12 * t:12 * t + 12], ys[t], AX.X, ALU.add)
            step(m)
            step(dve.tensor_scalar(hvar[:, 0:24], hss[:, 0:24], 1.0 / 64, LNX_EPS, ALU.mult, ALU.add))
            dve.reciprocal(hvar[:, 0:24], hvar[:, 0:24]).then_inc(sem("rw_yvar"), 1)
            dve.wait_ge(sem("rw_yrstd"), 1)
            for t in range(NT):
                m = dve.tensor_tensor(ycs[t], ycs[t], bc(hrstd[:, 12 * t:12 * t + 12].unsqueeze(2), [P, 12, 64]), ALU.mult)
            step(m)
            for o, op in ((1536, ALU.mult), (2304, ALU.add)):
                for t in range(NT):
                    m = dve.tensor_tensor(yc[:, t, :], yc[:, t, :], par[:, o:o + 768], op)
                step(m)
            for t in range(NT):
                m = dve.tensor_tensor(ys[t], v_tok[:, t, :].rearrange("p (h d) -> p h d", h=12),
                                      bc(bonus[:, 12 * t:12 * t + 12].unsqueeze(2), [P, 12, 64]), ALU.mult)
            step(m)
            step(dve.tensor_tensor(y_r, y_r, yc, ALU.add))
            dve.wait_ge(sem("rw_gate"), 1)
            step(dve.tensor_tensor(y_r, y_r, gate, ALU.mult))
            dve.memset(tiny[:, 161:162], 0.0).then_inc(sem("rwkv_over"), 1)
            dve.memset(tiny[:, 160:161], 0.0).then_inc(sem("rw_out"), 1)
            transposes("a_mix")
            gemm("a_out")
            norm("n_post0")
            swiglu("post0")
            norm("n_kv")
            gemm("kv")
            for e in moved("kv", 2):
                dve.wait_ge(sem(e[0]), e[1])
            dve.wait_ge(sem("norm_T"), 4 * (NORMS.index("n_kv") + 1))
            heads(4, [kd[:, t, :].rearrange("p (h d) -> p h d", h=12) for t in range(NT)], 64, [(0, 12, 7, 1.0)])
            dve.memset(tiny[:, 160:161], 0.0).then_inc(sem("heads_ok"), 1)
            transposes("kd")
            norm("n_pre1")
            swiglu("pre1")
            norm("n_mem1")
            gemm("mem1")
            mem_keys(5, 1)
            norm("n_mix1")
            gemm("b_q")
            for e in moved("b_q", 1):
                dve.wait_ge(sem(e[0]), e[1])
            dve.wait_ge(sem("norm_T"), 4 * (NORMS.index("n_mix1") + 1))
            heads(6, [q_d[:, t, :].rearrange("p (h d) -> p h d", h=16) for t in range(NT)], 64,
                  [(0, 12, 6, 0.125), (12, 16, 3, 0.125)])
            dve.memset(tiny[:, 160:161], 0.0).then_inc(sem("heads_ok"), 1)
            transposes("dil_q")
            attention("mem1")
            attention("dil")
            transposes("b_mix")
            gemm("b_out")
            norm("n_post1")
            swiglu("post1")


_WEIGHTS = ["x", "c", "ada_w", "ada_b", "even_w_in", "even_w_out", "odd_w_in", "odd_w_out", "router_w", "exp_w_gate",
            "exp_w_up", "exp_w_down", "mem_2", "ffn_pre_w_in_2", "ffn_pre_w_out_2", "ffn_post_w_in_2",
            "ffn_post_w_out_2", "mem_w_kv_2", "a_w_in_2", "a_w_up_2", "a_a_up_2", "a_g_up_2", "a_w_out_2", "b_w_q_2",
            "b_w_out_2", "kv_w_2", "rel_bias_2", "a_lnx_g_2", "a_lnx_b_2", "router_b"]


def kernel(**inputs):
    import concourse.bacc as _bacc
    from concourse.bass_utils import run_bass_kernel_spmd as _run

    n = {k: np.ascontiguousarray(v) for k, v in inputs.items()}
    arrays = {k: n[k] for k in _WEIGHTS}

    def cols(v):
        return v.reshape(-1, P).T

    gains = [n["norm1_g"][0], n["norm1_g"][1], n["norm2_g"][0], n["norm2_g"][1], n["ffn_pre_norm_2"][0],
             n["ffn_pre_norm_2"][1], n["mix_norm_2"][0], n["mix_norm_2"][1], n["ffn_post_norm_2"][0],
             n["ffn_post_norm_2"][1], n["mem_norm_2"][0], n["mem_norm_2"][1], n["kv_norm_2"]]
    arrays["gain_cols"] = np.ascontiguousarray(np.concatenate([cols(g) for g in gains], 1))
    arrays["rwkv_cols"] = np.ascontiguousarray(np.concatenate(
        [cols(v.reshape(-1)) for v in (n["a_shift_mu_2"], n["a_w0_2"], n["a_a0_2"], n["a_kk_scale_2"], n["a_k_a_2"],
                                       n["a_r_k_2"])], 1))
    arrays["gains64"] = np.ascontiguousarray(np.concatenate(
        [n["att_q_norm_g"].reshape(-1), n["att_k_norm_g"].reshape(-1), n["mem_q_norm_2"].reshape(-1),
         n["mem_k_norm_2"].reshape(-1), n["b_q_norm_2"].reshape(-1), n["kv_k_norm_2"].reshape(-1)]))
    rel = n["att_rel_bias"][0].T
    arrays["rel_t"] = np.ascontiguousarray(np.concatenate([rel, np.zeros((256 - rel.shape[0], 8), rel.dtype)], 0))
    arrays.update(constants())

    nc = _bacc.Bacc("TRN2", target_bir_lowering=False, num_devices=1)
    ins = {k: nc.dram_tensor(f"in_{k}", v.shape, mybir.dt.from_np(v.dtype), kind="ExternalInput").ap()
           for k, v in arrays.items()}
    out = nc.dram_tensor("out_x", (1, T, D), F32, kind="ExternalOutput").ap()
    build(nc, ins, out)
    r = _run(nc, [{f"in_{k}": v for k, v in arrays.items()}], core_ids=[0])
    return r.results[0]["out_x"]
```

```python
from contextlib import ExitStack
import math

import numpy as np
import concourse.bass as bass
from concourse import mybir

F32 = mybir.dt.float32
F32R = mybir.dt.float32r
BF16 = mybir.dt.bfloat16
U32 = mybir.dt.uint32
ALU = mybir.AluOpType
ACT = mybir.ActivationFunctionType
AX = mybir.AxisListType

P = 128
T = 256
NT = T // P
D = 1024
KD = D // P
EPS = 1e-6
LNX_EPS = 64e-5
NEG = -1e30
RAW = 3
PIECE = 2048
CHUNK = 64
EVEN_W = 3584
ODD_W = 3072
A_W = 2816
SHIFT_TILES = 20
NE = 16
DFF = 2816
HC = 256
MOE_CHUNKS = NE * 512 // HC
FFN_CHUNKS = DFF // HC
ADA_W = 6 * D
ADA_HALF = ADA_W // 2
ADA_PIECES = KD * ADA_W // PIECE
ADA_PER_ROW = ADA_W // PIECE
ADA_HALVES = 2 * KD
DECAY = math.exp(-0.5)


def constants():
    f = np.float32
    i = np.arange(P)
    c = {}
    same = (i[:, None] // CHUNK) == (i[None, :] // CHUNK)
    jj, tt = i[:, None], i[None, :]
    lower = np.array([[float(j < e) for j in range(4)] for e in range(4)]).reshape(1, 16)
    keep = np.concatenate([
        np.eye(P), np.ones((P, P)), np.where(jj >= tt, -1.0, 0.0), -np.ones((P, P)),
        (jj <= tt) & same, same, (i < 64)[:, None], (i >= 64)[:, None], np.repeat(lower, P, 0)], 1).astype(f)
    lv = [((jj >> (l + 1)) == (tt >> (l + 1))) & (((jj >> l) & 1) == 0) & (((tt >> l) & 1) == 1)
          for l in range(6)]
    rw_masks = np.concatenate(lv[1:] + [lv[0], lv[0].T, (jj < tt) & same], 1).astype(f)
    tok = np.arange(T)
    dec = []
    for h in range(4):
        lg = np.log(1.0 - 2.0 ** (-5.0 - h))
        m = np.exp(lg * np.abs(tok[None, :] - tok[:, None])) * (128.0 ** -0.5)
        m = m * ((tok[:, None] // CHUNK) <= (tok[None, :] // CHUNK))
        dec.append(np.concatenate([m[:P], m[P:, P:]], 1))
    inv = (10000.0 ** (-np.arange(0, 128, 2, dtype=np.float32) / np.float32(128))).astype(f)
    ang = (tok.astype(f)[:, None] * inv[None, :]).astype(f)
    rope = np.concatenate([np.cos(ang).reshape(2, P, 64).transpose(1, 0, 2).reshape(P, 128),
                           np.sin(ang).reshape(2, P, 64).transpose(1, 0, 2).reshape(P, 128)], 1)
    am = np.where((tok[None, :] // CHUNK) <= (tok[:, None] // CHUNK), 0.0, NEG)
    even = np.concatenate([np.concatenate(dec, 1), rope, am[:P, :P][::-1], am[P:][::-1]], 1).astype(f)
    reset = np.ones((P, T), f)
    reset[:, ::CHUNK] = 0.0
    dist = 255 - np.arange(512)
    hot_rel = np.zeros((256, 512), f)
    hot_rel[np.clip(dist, -63, 128) + 63, np.arange(512)] = 1.0
    d = np.maximum(dist, 0)
    df = np.maximum(d, 1).astype(np.float64)
    large = np.minimum(16 + np.floor(np.log(df / 16) / math.log(128) * 16 + 1e-9).astype(int), 31)
    bucket = np.where(d < 16, d, large)
    hot_t5 = np.zeros((32, 512), f)
    hot_t5[bucket, np.arange(512)] = 1.0
    ban = np.zeros((12, 512), f)
    for g, dil in enumerate((1, 4, 16)):
        ok = (dist >= 0) & (dist % dil == 0)
        if g == 0:
            ok &= dist <= 128
        ban[4 * g:4 * g + 4] = np.where(ok, 0.0, NEG)
    return {"c_keep": keep, "c_rw_masks": rw_masks, "c_even": even, "c_anti": np.eye(P, dtype=f)[::-1].copy(), "c_reset": reset, "c_hot_rel": hot_rel,
            "c_hot_t5": hot_t5, "c_ban": ban}


class Plan:

    def __init__(self):
        self.pieces = []
        self.held = [None] * RAW
        self.loads = [0] * RAW
        self.slot = 0
        self.gemms = {}
        self.done_at = []
        self.swi = {}
        self.gemm_chunks = self.gemm_pieces = self.swi_chunks = self.split = 0

    def add(self, kind, what, free):
        s = self.slot
        self.loads[s] += 1
        self.pieces.append(dict(kind=kind, what=what, slot=s, after=[self.held[s]], landed=16 * self.loads[s]))
        self.held[s] = free
        self.slot = (s + 1) % RAW

    def rwkv(self):
        self.pieces.append(dict(kind="rwkv", what=0, slot=0, after=[self.held[0], self.held[1]], landed=0))
        self.held[0] = self.held[1] = ("rwkv_over", 1)
        self.slot = 2

    def gemm(self, name, width, cols=256):
        g = dict(base=self.gemm_chunks, n=-(-width // 512), width=width, first=len(self.pieces), cols=cols)
        for o in range(0, width, cols):
            self.gemm_pieces += 1
            self.add("gemm", (name, o), ("gemm_done", self.gemm_pieces))
            if (o + cols) % 512 == 0 or o + cols >= width:
                self.done_at.append(self.gemm_pieces)
        self.gemm_chunks += g["n"]
        self.gemms[name] = g

    def swiglu(self, name, n):
        self.swi[name] = dict(base=self.swi_chunks, n=n, first=len(self.pieces), no=len(self.swi), split=self.split)
        order = [("gate", 0), ("up", 0)]
        for c in range(1, n):
            order += [("gate", c), ("up", c), ("down", c - 1)]
        order.append(("down", n - 1))
        for kind, c in order:
            self.split += 1
            self.add(kind, (name, c), ("w_lo", self.split))
        self.swi_chunks += n


def plan():
    p = Plan()
    for b in range(ADA_PIECES):
        p.add("ada", b, ("ada_used", b + 1))
    p.gemm("even_in", EVEN_W)
    p.gemm("even_out", D)
    p.swiglu("moe0", MOE_CHUNKS)
    p.gemm("odd_in", ODD_W)
    p.gemm("odd_out", D)
    p.swiglu("moe1", MOE_CHUNKS)
    p.swiglu("pre0", FFN_CHUNKS)
    p.gemm("mem0", 512)
    p.gemm("a_in", A_W)
    p.rwkv()
    p.gemm("a_out", D)
    p.swiglu("post0", FFN_CHUNKS)
    p.gemm("kv", 1536)
    p.swiglu("pre1", FFN_CHUNKS)
    p.gemm("mem1", 512)
    p.gemm("b_q", D)
    p.gemm("b_out", D, 512)
    p.swiglu("post1", FFN_CHUNKS)
    return p


PL = plan()
SWIGLUS = list(PL.swi)

HT, XN, PROJ, ROWS, WORK = 0, 2048, 4096, 11264, 15360
POOL = 24576
NORMS = ["n_even", "n_moe0", "n_odd", "n_moe1", "n_pre0", "n_mem0", "n_mix0", "n_post0", "n_kv", "n_pre1",
         "n_mem1", "n_mix1", "n_post1"]
JOB_BASE = {"att": 0, "mem0": 16, "mem1": 24, "dil": 32}


def build(nc, a, out):
    ctx = ExitStack()
    with ctx:
        def sb(name, shape, dt=F32):
            return ctx.enter_context(nc.sbuf_tensor(name, shape, dt))

        sems = {}

        def sem(name):
            if name not in sems:
                sems[name] = ctx.enter_context(nc.semaphore(name))
            return sems[name]

        scratch_bias = nc.dram_tensor("bias_rows", [20, 512], F32, kind="Internal").ap()

        ring = sb("ring", [P, RAW * PIECE])
        w_hi = sb("w_hi", [P, RAW, PIECE], F32R)
        w_lo = sb("w_lo", [P, RAW, PIECE], F32R)
        h_hi = sb("h_hi", [P, KD, T], F32R)
        h_lo = sb("h_lo", [P, KD, T], F32R)
        hid_hi = sb("hid_hi", [P, 2, 2, HC], F32R)
        hid_lo = sb("hid_lo", [P, 2, 2, HC], F32R)
        pool = sb("pool", [P, POOL])
        x = sb("x", [P, NT, D])
        keep = sb("keep", [P, a["c_keep"].shape[1]])
        gcols = sb("gcols", [P, 13, KD])
        rcols = sb("rcols", [P, 50])
        omu = sb("omu", [P, SHIFT_TILES])
        mcols = sb("mcols", [P, 2, 4, KD])
        mgain = sb("mgain", [P, 4, KD])
        cact = sb("cact", [P, KD])
        tiny = sb("tiny", [P, 162])
        zbf = sb("zbf", [P, P], BF16)
        gains64 = sb("gains64", [P, 8, 64])
        router_w = sb("router_w", [P, KD, NE])
        router_b = sb("router_b", [P, NE])
        psum = ctx.enter_context(nc.psum_tensor("psum", [P, 8, 512], F32))

        def bank(b, n=1):
            return psum[:, b, :] if n == 1 else psum[:, b:b + n, :].rearrange("p b n -> p (b n)")

        def view(off, *dims):
            n = int(np.prod(dims))
            v = pool[:, off:off + n]
            if len(dims) == 2:
                return v.rearrange("p (a b) -> p a b", a=dims[0])
            if len(dims) == 3:
                return v.rearrange("p (a b c) -> p a b c", a=dims[0], b=dims[1])
            return v

        off = 0
        K = {}
        for nm, w in (("ident", 128), ("ones", 128), ("neg_from", 128), ("neg_ones", 128), ("chunk_incl", 128),
                      ("head_ones", 128), ("head_cols", 2), ("lower", 16)):
            K[nm] = keep[:, off:off + w]
            off += w
        ident = K["ident"]

        hT = view(HT, KD, T)
        xn = view(XN, NT, D)
        acc = view(PROJ, ADA_W)
        grow = [[view(ROWS + 2048 * l + 1024 * j, D) for j in range(2)] for l in range(2)]

        def piece(n):
            s = PL.pieces[n]["slot"]
            return ring[:, s * PIECE:(s + 1) * PIECE]

        rwkv_par = ring[:, 0:2 * PIECE]

        def bc(ap, shape):
            return ap.to_broadcast(shape)

        csilu = cact
        ss = tiny[:, 0:2]
        var = tiny[:, 2:4]
        rstd = tiny[:, 4:6]
        hss = tiny[:, 8:40]
        hvar = tiny[:, 40:72]
        hrstd = tiny[:, 72:104]
        nmax = tiny[:, 104:106]
        esum = tiny[:, 106:110]
        erec = tiny[:, 6:8]
        mx = tiny[:, 110:112]
        pend = tiny[:, 112:136].rearrange("p (i c) -> p i c", c=4)
        bonus = tiny[:, 136:160]

        memx = view(ROWS, NT, D)
        NSRC = {n: (memx if n.startswith("n_mem") else x[:, :, :]) for n in NORMS}
        NGAIN = {"n_even": mgain[:, 0, :], "n_moe0": mgain[:, 1, :], "n_odd": mgain[:, 2, :],
                 "n_moe1": mgain[:, 3, :], "n_pre0": gcols[:, 4, :], "n_pre1": gcols[:, 5, :],
                 "n_mix0": gcols[:, 6, :], "n_mix1": gcols[:, 7, :], "n_post0": gcols[:, 8, :],
                 "n_post1": gcols[:, 9, :], "n_mem0": gcols[:, 10, :], "n_mem1": gcols[:, 11, :],
                 "n_kv": gcols[:, 12, :]}
        NSHIFT = {"n_even": mcols[:, 0, 0, :], "n_moe0": mcols[:, 0, 2, :], "n_odd": mcols[:, 1, 0, :],
                  "n_moe1": mcols[:, 1, 2, :]}
        XSEEN = {"n_even": 0, "n_moe0": 1, "n_odd": 2, "n_moe1": 3, "n_pre0": 4, "n_mem0": 0, "n_mix0": 5,
                 "n_post0": 6, "n_kv": 7, "n_pre1": 7, "n_mem1": 0, "n_mix1": 8, "n_post1": 9}

        proj_e = view(PROJ, NT, EVEN_W)
        decay_t = view(WORK, 4, 384)
        rope_c = view(WORK + 1536, NT, 64)
        rope_s = view(WORK + 1664, NT, 64)
        att_ban = view(WORK + 1792, 384)
        qk_t = view(WORK + 2176, 8, T)
        ret_s = view(WORK + 4224, 2, 384)
        att_p = view(WORK + 4992, 2, 768)
        att_pt = view(WORK + 6528, 768)
        anti = view(WORK + 7296, P)
        rot_a = view(WORK + 4992, 2, 512)
        rot_b = view(WORK + 6016, 2, 512)

        def bias_att(h, t):
            o = HT + 384 * h if h < 5 else ROWS + 2048 + 384 * (h - 5)
            return view(o, P) if t == 0 else view(o + P, T)

        qf = view(PROJ, KD, T)
        kf = view(PROJ + 2048, KD, T)
        v_o = view(PROJ + 4096, NT, D)
        SBW = WORK
        sb_abs = [view(SBW + 1536 * i, 384) for i in range(2)]
        sb_sp = [view(SBW + 1536 * i + 384, 384) for i in range(2)]
        sb_a = [view(SBW + 1536 * i + 768, 384) for i in range(2)]
        sb_zero = view(SBW + 3072, P)
        spread = keep[:, 0:256].bitcast(BF16)
        comb_b = view(WORK, NE, T)
        hid = [view(WORK + 4096, 2, HC), view(WORK + 4608, 2, HC)]
        comb_t = view(WORK + 5120, T)[0:NE, :]
        ada1 = view(WORK + 6144, ADA_HALF)
        rt = view(WORK + 5376, 512)
        rt_sc, comb_tok = rt[:, 0:32], rt[:, 448:480]
        mem_kt = view(ROWS + 3072, 2, T)
        mem_v = view(ROWS + 3584, NT, 256)
        mem_kv = view(WORK, NT, 512)
        q_mem_a = view(PROJ + 5120, NT, 256)
        F = view(PROJ, SHIFT_TILES, T)
        sh_tmp = [view(PROJ + 5632 + 260 * i, 260) for i in range(4)]
        W = [view(WORK + 1536 * i, 6, T) for i in range(6)]
        Wf = [view(WORK + 1536 * i, 1536) for i in range(6)]
        Fr, Fk, Fv = F[:, 0:6, :], F[:, 6:12, :], F[:, 12:18, :]
        rw_reset = view(XN, T)
        v_tok, b_tok, k_tok = (view(WORK + 1536 * i, NT, 768) for i in range(3))
        TT = view(ROWS, 6, 4, P)
        U = view(WORK + 6144, NT, 768)
        gate = view(HT, NT, 768)
        t_lt = view(PROJ + 3072, 4, P)
        t_t = view(PROJ + 3584, 4, P)
        t_x = view(PROJ + 4096, 4, P)
        t_lm = view(PROJ + 4608, 4, P)
        Z = view(PROJ + 3072, 768)
        SA = view(PROJ + 5632, NT, 768)
        state = view(ROWS + 3072, 6, P)
        bm = view(PROJ + 4608, 4, P)
        km = view(HT + 1536, 4, P)
        y_r = xn[:, :, 0:768]
        yc = view(PROJ + 3072, NT, 768)
        kd_t = view(PROJ, 6, T)
        v_d = view(PROJ + 1536, NT, 768)
        kd = view(WORK, NT, 768)
        q_d = view(PROJ + 3072, NT, D)
        qd_t = view(PROJ + 5120, 8, T)

        def bias_dil(g, h, t):
            o = WORK + 384 * (4 * g + h)
            return view(o, P) if t == 0 else view(o + P, T)

        def job(kind, h, t):
            half = slice(64 * (h % 2), 64 * (h % 2) + 64)
            qs = slice(P * t, P * t + P)
            if kind == "att":
                n = P * (t + 1)
                return ([dict(q=qk_t[half, h // 2, qs], k=qk_t[half, 4 + h // 2, 0:n], n=n,
                              bias=bias_att(h, t),
                              v=[proj_e[:, kt, 3072 + 64 * h:3136 + 64 * h] for kt in range(t + 1)])],
                        xn[:, t, 512 + 64 * h:576 + 64 * h])
            if kind in ("mem0", "mem1"):
                q = qk_t[half, h // 2, qs] if kind == "mem0" else qd_t[half, 6 + h // 2, qs]
                o = xn[:, t, 768 + 64 * h:832 + 64 * h] if kind == "mem0" else \
                    xn[:, t, 256 + 64 * h:320 + 64 * h]
                return ([dict(q=q, k=mem_kt[half, h // 2, :], n=T, bias=None,
                              v=[mem_v[:, kt, 64 * h:64 * h + 64] for kt in range(NT)])], o)
            n = P * (t + 1)
            segs = []
            for g in range(3):
                hh = 4 * g + h
                segs.append(dict(q=qd_t[half, hh // 2, qs], k=kd_t[half, hh // 2, 0:n], n=n,
                                 bias=bias_dil(g, h, t),
                                 v=[v_d[:, kt, 64 * hh:64 * hh + 64] for kt in range(t + 1)]))
            return segs, xn[:, t, 64 * h:64 * h + 64]

        JOBS = {"att": [("att", h, t) for h in range(8) for t in range(NT)],
                "mem0": [("mem0", h, t) for h in range(4) for t in range(NT)],
                "mem1": [("mem1", h, t) for h in range(4) for t in range(NT)],
                "dil": [("dil", h, t) for h in range(4) for t in range(NT)]}

        def gemm_dst(name, c):
            lo = 512 * c
            hi = min(lo + 512, PL.gemms[name]["width"])
            if name == "even_in":
                return "copy", proj_e[:, :, lo:hi]
            if name == "odd_in":
                if c < 2:
                    return "feat", qf[:, 4 * c:4 * c + 4, :]
                if c < 4:
                    return "feat", kf[:, 4 * c - 8:4 * c - 4, :]
                return "copy", v_o[:, :, lo - 2048:hi - 2048]
            if name in ("mem0", "mem1"):
                return "copy", mem_kv[:, :, :]
            if name == "a_in":
                return ("copy", q_mem_a[:, :, :]) if c == 5 else ("shift", c)
            if name == "kv":
                return "kv", c
            if name == "b_q":
                return "copy", q_d[:, :, lo:hi]
            if name in ("even_out", "odd_out"):
                return "resid_g", (0 if name == "even_out" else 1, c)
            return "resid", c

        KV_PARTS = {0: [(0, 512, kd, 0)], 1: [(0, 256, kd, 512), (256, 512, v_d, 0)], 2: [(0, 512, v_d, 256)]}

        X_AFTER = {"even_out": 1, "odd_out": 3, "a_out": 6, "b_out": 9}
        EVAC = []
        nact = ndve = 0
        for name, g in PL.gemms.items():
            for c in range(g["n"]):
                kind = gemm_dst(name, c)[0]
                if kind in ("copy", "feat", "kv"):
                    nact += 1
                    ndve += 1
                    EVAC.append([("ev_act", nact), ("ev_dve", ndve)])
                elif kind == "shift":
                    EVAC.append([("shift_mixed", 4 * c + 4)])
                else:
                    EVAC.append([("x_new", X_AFTER[name])] if c else
                                [("resid_first", list(X_AFTER).index(name) + 1)])

        def moved(name, c):
            return EVAC[PL.gemms[name]["base"] + c]

        block = ctx.enter_context(nc.Block())

        @block.sync
        def _(sp):
            def source(kind, name, c):
                layer = int(name[-1])
                w_in = a[f"ffn_{name[:-1]}_w_in_2"][layer].rearrange("(k p) n -> p k n", p=P)
                w_out = a[f"ffn_{name[:-1]}_w_out_2"][layer].rearrange("(k p) n -> p k n", p=P)
                return {"gate": w_in[:, :, HC * c:HC * c + HC], "up": w_in[:, :, DFF + HC * c:DFF + HC * c + HC],
                        "down": w_out[:, 2 * c:2 * c + 2, :]}[kind]

            def expert(kind, layer, e, half):
                w = a[{"gate": "exp_w_gate", "up": "exp_w_up", "down": "exp_w_down"}[kind]][layer, e]
                w = w.rearrange("(k p) n -> p k n", p=P)
                return w[:, 2 * half:2 * half + 2, :] if kind == "down" else w[:, :, HC * half:HC * half + HC]

            def load(n, src, k):
                s = PL.pieces[n]["slot"]
                sp.dma_start(piece(n).rearrange("p (k n) -> p k n", k=k), src).then_inc(sem(f"landed{s}"), 16)

            def static_piece(n):
                pc = PL.pieces[n]
                kind, what = pc["kind"], pc["what"]
                for e in pc["after"]:
                    if e is not None:
                        sp.wait_ge(sem(e[0]), e[1])
                if kind == "ada":
                    src = a["ada_w"][0].rearrange("(p t) n -> p (t n)", t=KD)
                    load(n, src[:, what * PIECE:(what + 1) * PIECE].unsqueeze(1), 1)
                elif kind == "gemm":
                    name, o = what
                    g = PL.gemms[name]
                    src = {"even_in": a["even_w_in"][0], "even_out": a["even_w_out"][0], "odd_in": a["odd_w_in"][0],
                           "odd_out": a["odd_w_out"][0], "mem0": a["mem_w_kv_2"][0], "mem1": a["mem_w_kv_2"][1],
                           "a_in": a["a_w_in_2"][0], "a_out": a["a_w_out_2"][0], "kv": a["kv_w_2"],
                           "b_q": a["b_w_q_2"][0], "b_out": a["b_w_out_2"][0]}[name]
                    load(n, src.rearrange("(k p) n -> p k n", p=P)[:, :, o:o + g["cols"]], PIECE // g["cols"])
                elif kind == "rwkv":
                    for m, (o, src) in enumerate((
                            (0, a["a_w_up_2"][0]), (0, a["a_a_up_2"][0]), (768, a["a_g_up_2"][0]),
                            (1536, a["a_lnx_g_2"][0].partition_broadcast(P)),
                            (2304, a["a_lnx_b_2"][0].partition_broadcast(P)), (3072, a["c_rw_masks"]))):
                        rows = rwkv_par[64:P] if m == 1 else rwkv_par[0:src.shape[0]]
                        sp.dma_start(rows[:, o:o + src.shape[1]], src).then_inc(sem("rwkv_in"), 16)
                else:
                    name, c = what
                    src = expert(kind, int(name[-1]), c // 2, c % 2) if name.startswith("moe") else \
                        source(kind, name, c)
                    load(n, src, 2 if kind == "down" else KD)

            ada_1 = a["ada_w"][1].rearrange("(p t) (h n) -> p t h n", t=KD, h=2)

            def ada_half(t, h, before):
                src = ada_1[:, t, h, :]
                sp.wait_ge(sem("ada_used"), ADA_PIECES + before)
                sp.dma_start(ada1, src).then_inc(sem("ada1_landed"), 16)

            def moe(name):
                s = PL.swi[name]
                layer, first = int(name[-1]), s["first"]
                loops = (s["n"] - 1) // 4
                for n in range(first, first + 14):
                    static_piece(n)
                if layer == 0:
                    sp.wait_ge(sem("moe_ready"), 1)
                    ada_half(0, 0, 0)
                with sp.Fori(0, loops - 1) as i:
                    for q in range(4):
                        r = 2 + 3 * q
                        for j, (kind, e, half) in enumerate((("gate", 2 * i + 2 + (q + 1) // 2, (q + 1) % 2),
                                                             ("up", 2 * i + 2 + (q + 1) // 2, (q + 1) % 2),
                                                             ("down", 2 * (i + 1) + q // 2, q % 2))):
                            src = expert(kind, layer, e, half)
                            sp.wait_ge(sem("w_lo"), s["split"] + 12 * i + 12 + r + j - 2)
                            load(first + r + j, src, 2 if kind == "down" else KD)
                        if layer == 0 and q == 0:
                            ada_half(i, 1, 2 * i + 1)
                        if layer == 0 and q == 2:
                            ada_half(i + 1, 0, 2 * i + 2)
                for n in range(first + 12 * loops + 2, first + 3 * s["n"]):
                    static_piece(n)
                    at = n - first - 12 * loops - 2
                    if layer == 0 and at == 2:
                        ada_half(loops - 1, 1, 2 * loops - 1)
                    if layer == 0 and at == 8:
                        ada_half(loops, 0, 2 * loops)
                if layer == 0:
                    ada_half(loops, 1, 2 * loops + 1)

            n = 0
            while n < len(PL.pieces):
                kind, what = PL.pieces[n]["kind"], PL.pieces[n]["what"]
                if kind == "gate" and what[0].startswith("moe"):
                    moe(what[0])
                    n += 3 * PL.swi[what[0]]["n"]
                else:
                    static_piece(n)
                    n += 1
            sp.wait_ge(sem("x_new"), 10)
            sp.dma_start(out.rearrange("a (t p) d -> p (a t) d", p=P), x[:, :, :]).then_inc(sem("stored"), 16)
            sp.wait_ge(sem("stored"), 16)

        @block.gpsimd
        def _(pl):
            pl.dma_start(cact[:, :], a["c"].rearrange("a (p t) -> p (a t)", t=KD)).then_inc(sem("c_in"), 16)
            pl.dma_start(x[:, :, :], a["x"].rearrange("a (t p) d -> p (a t) d", p=P)).then_inc(sem("x_in"), 16)
            pl.dma_start(keep[:, :], a["c_keep"]).then_inc(sem("keep_in"), 16)
            pl.dma_start(gcols[:, :, :], a["gain_cols"].rearrange("p (n k) -> p n k", k=KD)).then_inc(sem("cols_in"), 16)
            pl.dma_start(rcols[:, :], a["rwkv_cols"]).then_inc(sem("cols_in"), 16)
            pl.dma_start(gains64[:, :, :], a["gains64"].partition_broadcast(P).rearrange("p (n d) -> p n d", d=64))\
              .then_inc(sem("cols_in"), 16)
            pl.dma_start(router_b[:, :], a["router_b"].partition_broadcast(P)).then_inc(sem("cols_in"), 16)
            pl.dma_start(router_w[:, :, :], a["router_w"].rearrange("(k p) n -> p k n", p=P)).then_inc(sem("cols_in"), 16)
            pl.memset(acc, 0.0).then_inc(sem("acc_zero"), 1)
            pl.memset(zbf[:, :], 0.0).then_inc(sem("zbf_zero"), 1)
            pl.wait_ge(sem("acc_zero"), 1)
            pl.dma_start(acc[0:1, :], a["ada_b"][0:1, :]).then_inc(sem("ada_b_in"), 16)
            hot = view(WORK + 2176, 4, 512)
            pl.dma_start(hot[:, 0:2, :], a["c_hot_rel"].rearrange("(k p) n -> p k n", p=P)).then_inc(sem("hot_in"), 16)
            pl.dma_start(hot[0:32, 2, :], a["c_hot_t5"]).then_inc(sem("hot_in"), 16)
            pl.dma_start(hot[0:12, 3, :], a["c_ban"]).then_inc(sem("hot_in"), 16)
            pl.dma_start(view(WORK + 4224, 2, 8), a["rel_t"].rearrange("(k p) n -> p k n", p=P)).then_inc(sem("hot_in"), 16)
            pl.dma_start(view(WORK + 4240, 12)[0:32, :], a["rel_bias_2"]).then_inc(sem("hot_in"), 16)
            pl.dma_start(view(WORK, 2176), a["c_even"]).then_inc(sem("even_in"), 16)
            pl.wait_ge(sem("bias_rows"), 2)
            pl.dma_start(scratch_bias[0:8, :], view(WORK + 4256, 512)[0:8, :]).then_inc(sem("bias_out"), 16)
            pl.dma_start(scratch_bias[8:20, :], view(WORK + 4768, 512)[0:12, :]).then_inc(sem("bias_out"), 16)
            pl.wait_ge(sem("bias_out"), 32)

            def toeplitz(dst, row, t):
                n = P * (t + 1)
                src = bass.AP(tensor=scratch_bias.tensor, offset=row * 512 + 128 - P * t, ap=[[1, P], [1, n]])
                return pl.dma_start(dst, src)

            pl.wait_ge(sem("gemm_done"), PL.done_at[PL.gemms["even_in"]["base"] + 6])
            for h in range(8):
                for t in range(NT):
                    toeplitz(bias_att(h, t), h, t).then_inc(sem("bias_in"), 16)
            pl.dma_start(anti, a["c_anti"]).then_inc(sem("anti_in"), 16)
            pl.wait_ge(sem("bias_in"), 256)
            pl.wait_ge(sem("even_in"), 16)
            for h in range(8):
                for t in range(NT):
                    b_ = bias_att(h, t)
                    pl.tensor_tensor(b_, b_, att_ban[:, 0:P] if t == 0 else att_ban[:, P:384], ALU.add)\
                      .then_inc(sem("bias_banned"), 1)
            pl.wait_ge(sem("x_new"), 1)
            pl.memset(acc, 0.0).then_inc(sem("acc_zero"), 1)
            pl.wait_ge(sem("acc_zero"), 2)
            pl.dma_start(acc[0:1, :], a["ada_b"][1:2, :]).then_inc(sem("ada_b_in"), 16)
            pl.wait_ge(sem("x_new"), 4)
            pl.dma_start(memx, a["mem_2"].rearrange("a (t p) d -> p (a t) d", p=P)).then_inc(sem("mem_in"), 16)
            pl.wait_ge(sem("norm_T"), 4 * (NORMS.index("n_mix0") + 1))
            pl.wait_ge(sem("heads_ok"), 3)
            pl.dma_start(rw_reset, a["c_reset"]).then_inc(sem("reset_in"), 16)
            pl.wait_ge(sem("x_new"), 7)
            pl.dma_start(memx, a["mem_2"].rearrange("a (t p) d -> p (a t) d", p=P)).then_inc(sem("mem_in"), 16)
            pl.wait_ge(sem("x_new"), 8)
            pl.wait_ge(sem("heads_ok"), 5)
            pl.wait_ge(sem("gemm_done"), PL.done_at[PL.gemms["b_q"]["base"]])
            for g in range(3):
                for h in range(4):
                    for t in range(NT):
                        toeplitz(bias_dil(g, h, t), 8 + 4 * g + h, t).then_inc(sem("bias2_in"), 16)
            pl.dma_start(anti, a["c_anti"]).then_inc(sem("bias2_in"), 16)

        def flat(v):
            return v if len(v.shape) == 2 else v.rearrange("p a b -> p (a b)")

        def blocks_tok(src, tiles, dst):
            s = [src(j, t) for j in range(tiles) for t in range(NT)]
            return [(s[4 * b:4 * b + 4], dst(2 * b, min(2, tiles - 2 * b))) for b in range(-(-tiles // 2))]

        def blocks_feat(srcv, dst):
            s = [srcv[:, i, P * t:P * t + P] for t in range(NT) for i in range(6)]
            return [(s[4 * b:4 * b + 4], dst[:, 512 * b:512 * b + 512]) for b in range(3)]

        def into(v):
            return lambda j, n: flat(v[:, j:j + n, :])

        TRS = {
            "ret_qk": blocks_tok(lambda j, t: proj_e[:, t, P * j:P * j + P], 8, into(qk_t)),
            "att_qk": blocks_tok(lambda j, t: proj_e[:, t, 2048 + P * j:2048 + P * j + P], 8, into(qk_t)),
            "even_mix": blocks_tok(lambda j, t: xn[:, t, P * j:P * j + P], 8, into(hT)),
            "odd_mix": blocks_tok(lambda j, t: xn[:, t, P * j:P * j + P], 8, into(hT)),
            "mem0_k": blocks_tok(lambda j, t: mem_kv[:, t, P * j:P * j + P], 2, into(mem_kt)),
            "mem0_q": blocks_tok(lambda j, t: q_mem_a[:, t, P * j:P * j + P], 2, into(qk_t)),
            "rw_v": blocks_feat(Fv, flat(v_tok)),
            "rw_b": blocks_feat(W[5], flat(b_tok)),
            "rw_k": blocks_feat(Fk, flat(k_tok)),
            "a_mix": blocks_tok(lambda j, t: xn[:, t, P * j:P * j + P], 8, into(hT)),
            "kd": blocks_tok(lambda j, t: kd[:, t, P * j:P * j + P], 6, into(kd_t)),
            "mem1_k": blocks_tok(lambda j, t: mem_kv[:, t, P * j:P * j + P], 2, into(mem_kt)),
            "dil_q": blocks_tok(lambda j, t: q_d[:, t, P * j:P * j + P], 8, into(qd_t)),
            "b_mix": blocks_tok(lambda j, t: xn[:, t, P * j:P * j + P], 4, into(hT)),
        }
        TR_BASE, n = {}, 0
        for nm, bl in TRS.items():
            TR_BASE[nm] = n
            n += len(bl)

        def tr_counts(nm):
            e = TR_BASE[nm] + len(TRS[nm])
            return (e + 1) // 2, e // 2

        @block.tensor
        def _(pe):
            def landed(n):
                pe.wait_ge(sem(f"landed{PL.pieces[n]['slot']}"), PL.pieces[n]["landed"])

            def transposes(nm, *ready):
                for r in ready:
                    pe.wait_ge(sem(r[0]), r[1])
                for i, (srcs, _) in enumerate(TRS[nm]):
                    B = TR_BASE[nm] + i
                    e = B - 4
                    if e >= 0:
                        pe.wait_ge(sem("tr_act" if e % 2 == 0 else "tr_dve"), e // 2 + 1)
                    for k, src in enumerate(srcs):
                        m = pe.transpose(bank(4 + B % 4)[:, P * k:P * k + P], src, ident)
                    m.then_inc(sem("tr_done"), 1)

            def transposed(nm):
                na, nd = tr_counts(nm)
                if na > 0:
                    pe.wait_ge(sem("tr_act"), na)
                if nd > 0:
                    pe.wait_ge(sem("tr_dve"), nd)

            def norm(nm):
                n = NORMS.index(nm)
                pe.wait_ge(sem("norm_xn"), 2 * (n + 1))
                for b in range(4):
                    for k in range(2):
                        for t in range(NT):
                            j = 2 * b + k
                            m = pe.transpose(bank(b)[:, T * k + P * t:T * k + P * t + P],
                                             xn[:, t, P * j:P * j + P], ident)
                    m.then_inc(sem("norm_T"), 1)
                pe.wait_ge(sem("norm_act"), 4 * (n + 1))
                pe.wait_ge(sem("norm_dve"), 4 * (n + 1))

            def gemm(nm):
                g = PL.gemms[nm]
                for c in range(g["n"]):
                    G = g["base"] + c
                    kind = gemm_dst(nm, c)[0]
                    if G >= 4:
                        for e in EVAC[G - 4]:
                            pe.wait_ge(sem(e[0]), e[1])
                    pair, cols = 2 * (G % 4), g["cols"]
                    ks = PIECE // cols
                    for o in range(512 * c, min(512 * c + 512, g["width"]), cols):
                        no = g["first"] + o // cols
                        landed(no)
                        wt = piece(no).rearrange("p (k n) -> p k n", k=ks)
                        lo = o - 512 * c
                        if kind in ("feat", "shift"):
                            for f in range(2):
                                dst = bank(pair + lo // 256)[:, T * f:T * f + T]
                                for k in range(ks):
                                    m = pe.matmul(dst, wt[:, k, P * f:P * f + P], hT[:, k, :], start=k == 0, stop=k == ks - 1)
                        else:
                            for t in range(NT):
                                for k in range(ks):
                                    m = pe.matmul(bank(pair + t)[:, lo:lo + cols], hT[:, k, P * t:P * t + P], wt[:, k, :],
                                                  start=k == 0, stop=k == ks - 1)
                        m.then_inc(sem("gemm_done"), 1)

            def swiglu(nm):
                s = PL.swi[nm]
                G0, U0 = s["base"], s["split"]

                def zero_products(start):
                    for b in range(4):
                        m = pe.matmul(bank(b), zbf[:, :], spread, start=start, stop=not start, skip_group_check=True)
                    if not start:
                        m.then_inc(sem("sums_done"), 1)

                def gate_up(c, q, n, j, r):
                    pe.wait_ge(sem("w_lo"), U0 + n + 1)
                    pe.wait_ge(sem("silu_done" if j == 0 else "hid_ready"), max(G0 + c, 1) if isinstance(c, int) else G0 + c)
                    wh, wl = (w[:, r, :].rearrange("p (k n) -> p k n", k=KD) for w in (w_hi, w_lo))
                    for f in range(2):
                        for k in range(KD):
                            o, fs = bank(4 + 2 * (q % 2) + j)[:, T * f:T * f + T], slice(P * f, P * f + P)
                            pe.matmul(o, wh[:, k, fs], h_hi[:, k, :], start=k == 0, stop=False)
                            pe.matmul(o, wh[:, k, fs], h_lo[:, k, :], start=False, stop=False)
                            m = pe.matmul(o, wl[:, k, fs], h_hi[:, k, :], start=False, stop=k == KD - 1)
                    m.then_inc(sem("w_used"), 1)

                def down(c, q, n, r):
                    pe.wait_ge(sem("w_lo"), U0 + n + 1)
                    pe.wait_ge(sem("hid_ready"), G0 + c + 2)
                    wh, wl = (w[:, r, :].rearrange("p (k n) -> p k n", n=D) for w in (w_hi, w_lo))
                    hh, hl = hid_hi[:, q % 2], hid_lo[:, q % 2]
                    for f in range(2):
                        for t in range(NT):
                            ts = slice(P * t, P * t + P)
                            for h in range(2):
                                o, hs = bank(2 * t + h), slice(512 * h, 512 * h + 512)
                                for lhs, rhs in ((hh, wh), (hh, wl), (hl, wh)):
                                    m = pe.matmul(o, lhs[:, f, ts], rhs[:, f, hs], start=False, stop=False,
                                                  skip_group_check=True)
                    m.then_inc(sem("w_used"), 1)

                if XSEEN["n_" + nm] > 0:
                    pe.wait_ge(sem("x_new"), XSEEN["n_" + nm])
                zero_products(True)
                pe.wait_ge(sem("h_split_lo"), 4 * (s["no"] + 1))
                gate_up(0, 0, 0, 0, 0)
                gate_up(0, 0, 1, 1, 1)
                loops = (s["n"] - 1) // 4
                with pe.Fori(0, loops) as i:
                    for q in range(4):
                        gate_up(4 * i + q + 1, (q + 1) % 4, 12 * i + 3 * q + 2, 0, 2)
                        gate_up(4 * i + q + 1, (q + 1) % 4, 12 * i + 3 * q + 3, 1, 0)
                        down(4 * i + q, q, 12 * i + 3 * q + 4, 1)
                for c in range(4 * loops + 1, s["n"]):
                    gate_up(c, c % 4, 3 * c - 1, 0, 2)
                    gate_up(c, c % 4, 3 * c, 1, 0)
                    down(c - 1, (c - 1) % 4, 3 * c + 1, 1)
                last = s["n"] - 1
                down(last, last % 4, 3 * last + 2, 2)
                zero_products(False)

            def attention(kind, *ready):
                for r in ready:
                    pe.wait_ge(sem(r[0]), r[1])
                jobs, base = JOBS[kind], JOB_BASE[kind]
                for j in range(len(jobs) + 2):
                    J = base + j
                    if j < len(jobs):
                        if J > 1:
                            pe.wait_ge(sem("att_exp"), J - 1)
                        lg = psum[:, 2 * (j % 2):2 * (j % 2) + 2, :].rearrange("p b n -> p (b n)")
                        for k, sg in enumerate(job(*jobs[j])[0]):
                            o = lg[:, T * k:T * k + sg["n"]]
                            if sg["bias"] is not None:
                                pe.matmul(o, anti, sg["bias"], start=True, stop=False)
                            m = pe.matmul(o, sg["q"], sg["k"], start=sg["bias"] is None, stop=True)
                        m.then_inc(sem("att_scores"), 1)
                    if 0 <= j - 2:
                        J2 = J - 2
                        pe.wait_ge(sem("att_pts"), J2 + 1)
                        if J2 > 1:
                            pe.wait_ge(sem("att_o"), J2 - 1)
                        vs = [v for sg in job(*jobs[j - 2])[0] for v in sg["v"]]
                        for k, v in enumerate(vs):
                            m = pe.matmul(bank(6 + j % 2)[:, 0:64], att_pt[:, P * k:P * k + P], v,
                                          start=k == 0, stop=k == len(vs) - 1)
                        m.then_inc(sem("att_pv"), 1)
                    if 0 <= j - 1 < len(jobs):
                        J1 = J - 1
                        pe.wait_ge(sem("att_exp"), J1 + 1)
                        if J1 > 0:
                            pe.wait_ge(sem("att_pts"), J1)
                        k = 0
                        for sg_i, sg in enumerate(job(*jobs[j - 1])[0]):
                            for kt in range(len(sg["v"])):
                                o = T * sg_i + P * kt
                                m = pe.transpose(bank(4, 2)[:, P * k:P * k + P],
                                                 att_p[:, (j - 1) % 2, o:o + P], ident)
                                k += 1
                        m.then_inc(sem("att_pt"), 1)

            def modulation(layer):
                for j, part in enumerate((0, 1, 3, 4)):
                    for k in range(KD):
                        o = D * part + P * k
                        m = pe.matmul(bank(4)[:, KD * j + k:KD * j + k + 1], acc[:, o:o + P], K["ones"][:, 0:1],
                                      start=True, stop=True)
                m.then_inc(sem("mod_cols"), 1)
                for j, part in enumerate((2, 5)):
                    for h in range(2):
                        o = D * part + 512 * h
                        m = pe.matmul(bank(2 * j + h), K["ones"], acc[:, o:o + 512], start=True, stop=True)
                m.then_inc(sem("mod_rows"), 1)

            pe.wait_ge(sem("keep_in"), 16)
            pe.wait_ge(sem("hot_in"), 80)
            hot = view(WORK + 2176, 4, 512)
            for k in range(2):
                m = pe.matmul(bank(6)[0:8, :], view(WORK + 4224, 2, 8)[:, k, :], hot[:, k, :], start=k == 0, stop=k == 1)
            m.then_inc(sem("bias_ps"), 1)
            pe.matmul(bank(7)[0:12, :], view(WORK + 4240, 12)[0:32, :], hot[0:32, 2, :], start=True, stop=True)\
              .then_inc(sem("bias_ps"), 1)
            pe.wait_ge(sem("ada_used"), ADA_PIECES)
            modulation(0)
            norm("n_even")
            pe.wait_ge(sem("mod_moved"), 1)
            gemm("even_in")
            pe.wait_ge(sem("rotated"), 1)
            transposes("ret_qk")
            transposed("ret_qk")
            for h in range(5):
                if h < 4:
                    if h > 1:
                        pe.wait_ge(sem("ret_decayed"), h - 1)
                    o = bank(h % 2)
                    pe.matmul(o[:, 0:T], qk_t[:, 4 + h, 0:P], qk_t[:, h, :], start=True, stop=True)
                    pe.matmul(o[:, T:T + P], qk_t[:, 4 + h, P:T], qk_t[:, h, P:T], start=True, stop=True)\
                      .then_inc(sem("ret_scores"), 1)
                if h >= 1:
                    g = h - 1
                    pe.wait_ge(sem("ret_decayed"), g + 1)
                    if g > 1:
                        pe.wait_ge(sem("ret_moved"), g - 1)
                    o = bank(2 + g % 2)
                    v = proj_e[:, :, D + P * g:D + P * g + P]
                    s = ret_s[:, g % 2, :]
                    pe.matmul(o[:, 0:P], s[:, 0:P], v[:, 0, :], start=True, stop=True)
                    pe.matmul(o[:, P:T], s[:, P:T], v[:, 0, :], start=True, stop=False)
                    pe.matmul(o[:, P:T], s[:, T:T + P], v[:, 1, :], start=False, stop=True)\
                      .then_inc(sem("ret_pv"), 1)
            transposes("att_qk", ("heads_ok", 1))
            transposed("att_qk")
            attention("att", ("bias_banned", 16), ("anti_in", 16))
            transposes("even_mix", ("att_o", 16), ("even_mixed", 1))
            transposed("even_mix")
            gemm("even_out")

            def router(layer):
                pe.wait_ge(sem("x_new"), 1 + 2 * layer)
                for t in range(NT):
                    for k in range(KD):
                        m = pe.matmul(bank(4)[:, NE * t:NE * t + NE], hT[:, k, P * t:P * t + P], router_w[:, k, :],
                                      start=k == 0, stop=k == KD - 1)
                m.then_inc(sem("router_ps"), 1)
                pe.wait_ge(sem("comb_tok"), layer + 1)
                for t in range(NT):
                    m = pe.transpose(bank(5)[0:NE, P * t:P * t + P], comb_tok[:, NE * t:NE * t + NE], ident)
                m.then_inc(sem("comb_T_ps"), 1)
                pe.wait_ge(sem("comb_T"), layer + 1)
                for e in range(NE):
                    m = pe.matmul(bank(e // 2)[:, T * (e % 2):T * (e % 2) + T],
                                  bc(ident[0:NE, e:e + 1], [NE, P]), comb_t, start=True, stop=True)
                    if e % 2:
                        m.then_inc(sem("comb_ps"), 1)
                pe.wait_ge(sem("comb_act"), 4 * (layer + 1))
                pe.wait_ge(sem("comb_dve"), 4 * (layer + 1))

            norm("n_moe0")
            router(0)
            swiglu("moe0")
            pe.wait_ge(sem("ada_used"), ADA_PIECES + ADA_HALVES)
            pe.wait_ge(sem("x_new"), 2)
            modulation(1)
            norm("n_odd")
            gemm("odd_in")
            for e in moved("odd_in", 5):
                pe.wait_ge(sem(e[0]), e[1])
            for s_ in range(18):
                if s_ < 16:
                    h = s_
                    half = slice(64 * (h % 2), 64 * (h % 2) + 64)
                    kk, qq = kf[half, h // 2, :], qf[half, h // 2, :]
                    if h > 1:
                        pe.wait_ge(sem("sb_soft"), h - 1)
                    if h > 1:
                        pe.wait_ge(sem("sb_exp"), h - 1)
                    for bk in (h % 2, 2 + h % 2):
                        last = bk >= 2
                        pe.matmul(bank(bk)[:, 0:P], kk[:, 0:P], qq[:, 0:P], start=True, stop=not last,
                                  skip_group_check=True)
                        pe.matmul(bank(bk)[:, P:T], kk[:, 0:P], qq[:, P:T], start=not last, stop=not last,
                                  skip_group_check=True)
                        m = pe.matmul(bank(bk)[:, T:T + P], kk[:, P:T], qq[:, P:T], start=not last, stop=not last,
                                      skip_group_check=True)
                        if not last:
                            m.then_inc(sem("sb_z"), 1)
                if 1 <= s_ <= 16:
                    h = s_ - 1
                    pe.wait_ge(sem("sb_masked"), h + 1)
                    o, sp_ = bank(2 + h % 2), sb_sp[h % 2]
                    pe.matmul(o[:, 0:P], K["neg_from"], sp_[:, 0:P], start=False, stop=False, skip_group_check=True)
                    pe.matmul(o[:, P:T], K["neg_from"], sp_[:, P:T], start=False, stop=False, skip_group_check=True)
                    pe.matmul(o[:, P:T], K["neg_ones"], sp_[:, T:T + P], start=False, stop=False,
                              skip_group_check=True)
                    pe.matmul(o[:, T:T + P], K["neg_from"], sp_[:, T:T + P], start=False, stop=True,
                              skip_group_check=True).then_inc(sem("sb_sums"), 1)
                if s_ >= 2:
                    h = s_ - 2
                    pe.wait_ge(sem("sb_weights"), h + 1)
                    if h > 1:
                        pe.wait_ge(sem("sb_out"), h - 1)
                    o, av = bank(4 + h % 2), sb_a[h % 2]
                    v = v_o[:, :, 64 * h:64 * h + 64]
                    pe.matmul(o[:, 0:64], av[:, 0:P], v[:, 0, :], start=True, stop=True)
                    pe.matmul(o[:, 64:128], av[:, P:T], v[:, 0, :], start=True, stop=False)
                    pe.matmul(o[:, 64:128], av[:, T:T + P], v[:, 1, :], start=False, stop=True)\
                      .then_inc(sem("sb_pv"), 1)
            transposes("odd_mix", ("sb_out", 16))
            transposed("odd_mix")
            gemm("odd_out")
            norm("n_moe1")
            router(1)
            swiglu("moe1")
            norm("n_pre0")
            swiglu("pre0")
            norm("n_mem0")
            gemm("mem0")
            transposes("mem0_k", ("heads_ok", 2))
            norm("n_mix0")
            gemm("a_in")
            pe.wait_ge(sem("shift_mixed"), SHIFT_TILES)
            transposes("mem0_q", ("heads_ok", 3))
            transposed("mem0_q")
            attention("mem0")
            pe.wait_ge(sem("att_o"), 24)
            pe.wait_ge(sem("rwkv_in"), 96)
            par = rwkv_par
            pe.wait_ge(sem("rw_low"), 2)
            for i in range(6):
                m = pe.matmul(bank(i // 2)[:, T * (i % 2):T * (i % 2) + T], par[0:64, P * i:P * i + P],
                              F[0:64, 18, :], start=True, stop=True)
            m.then_inc(sem("rw_w_ps"), 1)
            for i in range(6):
                m = pe.matmul(bank(3 + i // 2)[:, T * (i % 2):T * (i % 2) + T], par[64:P, P * i:P * i + P],
                              F[64:P, 18, :], start=True, stop=True)
            m.then_inc(sem("rw_a_ps"), 1)
            pe.wait_ge(sem("rw_sig"), 1)
            for n in range(6):
                t, s = n // 3, n % 3
                m = pe.matmul(bank((6 + n // 2) % 8)[:, T * (n % 2):T * (n % 2) + T], F[:, 19, P * t:P * t + P],
                              par[:, 768 + T * s:768 + T * s + T], start=True, stop=True)
            m.then_inc(sem("rw_g_ps"), 1)
            pe.wait_ge(sem("rw_sq"), 1)
            pe.wait_ge(sem("rw_sig"), 2)
            for i in range(6):
                m = pe.matmul(bank(3 + i // 2)[:, T * (i % 2):T * (i % 2) + T], K["head_ones"], W[4][:, i, :],
                              start=True, stop=True)
            m.then_inc(sem("rw_ss_ps"), 1)
            pe.wait_ge(sem("rw_rk"), 1)
            for t in range(NT):
                for i in range(6):
                    m = pe.matmul(bank(1)[:, 12 * t + 2 * i:12 * t + 2 * i + 2], W[4][:, i, P * t:P * t + P],
                                  K["head_cols"], start=True, stop=True)
            m.then_inc(sem("rw_bonus_ps"), 1)
            pe.wait_ge(sem("rw_gate"), 1)
            pe.wait_ge(sem("rw_ss"), 1)
            pe.wait_ge(sem("rw_bonus"), 1)
            transposes("rw_v", ("rw_scaled", 1))
            transposes("rw_b")
            transposes("rw_k")
            transposed("rw_k")
            for i in range(6):
                if i > 0:
                    pe.wait_ge(sem("rw_u"), i)
                if i > 0:
                    pe.wait_ge(sem("rw_t"), i)
                halves = [slice(64 * e, 64 * e + 64) for e in range(2)]
                for e in range(2):
                    for t in range(NT):
                        tk = slice(P * t, P * t + P)
                        bT, kkT, kT = W[5][halves[e], i, tk], W[3][halves[e], i, tk], Fk[halves[e], i, tk]
                        pe.matmul(bank(e)[:, P * t:P * t + P], bT, kkT, start=True, stop=True)
                        pe.matmul(bank(e)[:, T + P * t:T + P * t + P], kkT, bT, start=True, stop=True)
                        m = pe.matmul(bank(2 + e)[:, P * t:P * t + P], kT, kkT, start=True, stop=True)
                m.then_inc(sem("rw_l_ps"), 1)
                for l in range(5):
                    pe.wait_ge(sem("rw_lm"), 5 * i + l + 1)
                    for m4 in range(4):
                        m = pe.matmul(bank(4)[:, P * m4:P * m4 + P], t_lm[:, m4, :], t_t[:, m4, :], start=True, stop=True)
                    m.then_inc(sem("rw_x_ps"), 1)
                    pe.wait_ge(sem("rw_x"), 5 * i + l + 1)
                    for m4 in range(4):
                        pe.matmul(bank(5)[:, P * m4:P * m4 + P], TT[:, i, m4, :], t_x[:, m4, :], start=True, stop=True)
                        m = pe.matmul(bank(6)[:, P * m4:P * m4 + P], t_x[:, m4, :], TT[:, i, m4, :], start=True, stop=True)
                    m.then_inc(sem("rw_tx_ps"), 1)
                pe.wait_ge(sem("rw_m"), i + 1)
                for e in range(2):
                    for t in range(NT):
                        m = pe.matmul(bank(7)[:, P * t + 64 * e:P * t + 64 * e + 64], t_lm[:, 2 * e + t, :],
                                      v_tok[:, t, P * i + 64 * e:P * i + 64 * e + 64], start=True, stop=True)
                m.then_inc(sem("rw_u_ps"), 1)
            pe.wait_ge(sem("rw_u"), 6)
            for c in range(4):
                t, q0 = c // 2, 64 * (c % 2)
                pe.wait_ge(sem("rw_state"), c + 1)
                if c > 0:
                    pe.wait_ge(sem("rw_y"), c)
                for i in range(6):
                    m = pe.matmul(bank(0, 2)[:, P * i:P * i + P], W[3][:, i, P * t:P * t + P], state[:, i, :],
                                  start=True, stop=True)
                m.then_inc(sem("rw_z_ps"), 1)
                for i in range(6):
                    m = pe.matmul(bank(2, 2)[:, P * i:P * i + P], Fr[:, i, P * t:P * t + P], state[:, i, :],
                                  start=True, stop=True)
                m.then_inc(sem("rw_y_ps"), 1)
                pe.wait_ge(sem("rw_z"), c + 1)
                for h in range(12):
                    m = pe.matmul(bank(4, 2)[:, 64 * h:64 * h + 64], TT[:, h // 2, 2 * (h % 2) + t, :],
                                  Z[:, 64 * h:64 * h + 64], start=True, stop=True)
                m.then_inc(sem("rw_sa_ps"), 1)
                pe.wait_ge(sem("rw_sa"), c + 1)
                rows = slice(q0, q0 + 64)
                for i in range(6):
                    cols = slice(P * i, P * i + P)
                    o = bank(6, 2)[:, cols]
                    pe.matmul(o, b_tok[rows, t, cols], SA[rows, t, cols], start=True, stop=False)
                    m = pe.matmul(o, k_tok[rows, t, cols], v_tok[rows, t, cols], start=False, stop=True)
                m.then_inc(sem("rw_new_ps"), 1)
            for i in range(6):
                if i > 0:
                    pe.wait_ge(sem("rw_bk"), i)
                pe.wait_ge(sem("rw_y"), 4)
                pe.wait_ge(sem("rw_z"), 4)
                for e in range(2):
                    half = slice(64 * e, 64 * e + 64)
                    for t in range(NT):
                        tk = slice(P * t, P * t + P)
                        pe.matmul(bank(e)[:, P * t:P * t + P], W[5][half, i, tk], Fr[half, i, tk], start=True, stop=True)
                        m = pe.matmul(bank(2 + e)[:, P * t:P * t + P], Fk[half, i, tk], Fr[half, i, tk],
                                      start=True, stop=True)
                m.then_inc(sem("rw_bk_ps"), 1)
                pe.wait_ge(sem("rw_bk"), i + 1)
                if i > 0:
                    pe.wait_ge(sem("rw_yadd"), i)
                for e in range(2):
                    for t in range(NT):
                        o = bank(4)[:, P * t + 64 * e:P * t + 64 * e + 64]
                        hs = slice(P * i + 64 * e, P * i + 64 * e + 64)
                        pe.matmul(o, bm[:, 2 * e + t, :], SA[:, t, hs], start=True, stop=False)
                        m = pe.matmul(o, km[:, 2 * e + t, :], v_tok[:, t, hs], start=False, stop=True)
                m.then_inc(sem("rw_g2_ps"), 1)
            transposes("a_mix", ("rw_out", 1))
            transposed("a_mix")
            gemm("a_out")
            norm("n_post0")
            swiglu("post0")
            norm("n_kv")
            gemm("kv")
            transposes("kd", ("heads_ok", 4))
            norm("n_pre1")
            swiglu("pre1")
            norm("n_mem1")
            gemm("mem1")
            transposes("mem1_k", ("heads_ok", 5))
            norm("n_mix1")
            gemm("b_q")
            transposes("dil_q", ("heads_ok", 6))
            transposed("dil_q")
            attention("mem1")
            attention("dil", ("bias2_in", 25 * 16))
            transposes("b_mix", ("att_o", 40))
            transposed("b_mix")
            gemm("b_out")
            norm("n_post1")
            swiglu("post1")

        @block.scalar
        def _(act):
            done = [0]

            def step(ins):
                done[0] += 1
                ins.then_inc(sem("act_step"), 1)
                act.wait_ge(sem("act_step"), done[0])

            def norm(nm):
                n = NORMS.index(nm)
                if nm == "n_even":
                    act.wait_ge(sem("x_in"), 16)
                elif nm == "n_mem0":
                    act.wait_ge(sem("mem_in"), 16)
                elif nm == "n_mem1":
                    act.wait_ge(sem("mem_in"), 32)
                if XSEEN[nm] > 0:
                    act.wait_ge(sem("x_new"), XSEEN[nm])
                if 2 * n > 0:
                    act.wait_ge(sem("norm_xn"), 2 * n)
                for t in range(NT):
                    act.activation(xn[:, t, :], NSRC[nm][:, t, :], ACT.Square, accum_out=ss[:, t:t + 1])\
                       .then_inc(sem("norm_ss"), 1)
                act.wait_ge(sem("norm_var"), n + 1)
                act.activation(rstd, var, ACT.Sqrt).then_inc(sem("norm_rstd"), 1)
                for j in (0, 1, 4, 5):
                    b = j // 2
                    act.wait_ge(sem("norm_T"), 4 * n + b + 1)
                    shift = NSHIFT[nm][:, j:j + 1] if nm in NSHIFT else 0.0
                    act.activation(hT[:, j, :], bank(b)[:, T * (j % 2):T * (j % 2) + T], ACT.Identity, bias=shift,
                                   scale=NGAIN[nm][:, j:j + 1]).then_inc(sem("norm_act"), 1)

            def gemm(nm):
                g = PL.gemms[nm]
                for c in range(g["n"]):
                    G = g["base"] + c
                    kind, dst = gemm_dst(nm, c)
                    if kind.startswith("resid"):
                        continue
                    act.wait_ge(sem("gemm_done"), PL.done_at[G])
                    ps = bank(2 * (G % 4))
                    if kind == "copy":
                        d = dst[:, 0, :]
                        act.activation(d, ps[:, 0:d.shape[1]], ACT.Copy).then_inc(sem("ev_act"), 1)
                    elif kind == "feat":
                        act.activation(flat(dst[:, 0:2, :]), ps, ACT.Copy,
                                       scale=0.125 if c < 2 else 1.0).then_inc(sem("ev_act"), 1)
                    elif kind == "kv":
                        for lo, hi, d, o in KV_PARTS[c]:
                            m = act.activation(d[:, 0, o:o + hi - lo], ps[:, lo:hi], ACT.Copy)
                        m.then_inc(sem("ev_act"), 1)
                    else:
                        for f in range(4):
                            n = 4 * c + f
                            if n > 3:
                                act.wait_ge(sem("shift_mixed"), n - 3)
                            tmp = sh_tmp[n % 4]
                            act.activation(tmp[:, 1:T + 1], bank(2 * (G % 4) + f // 2)[:, T * (f % 2):T * (f % 2) + T],
                                           ACT.Copy, scale=rcols[:, n:n + 1]).then_inc(sem("shift_mu"), 1)

            def transposes(nm):
                for i, (srcs, dst) in enumerate(TRS[nm]):
                    B = TR_BASE[nm] + i
                    if B % 2 == 0:
                        act.wait_ge(sem("tr_done"), B + 1)
                        act.activation(dst, bank(4 + B % 4)[:, 0:P * len(srcs)], ACT.Copy).then_inc(sem("tr_act"), 1)

            def heads(n):
                act.wait_ge(sem("heads_var"), n + 1)
                act.activation(hrstd, hvar, ACT.Sqrt).then_inc(sem("heads_rstd"), 1)

            def split_piece(nm, r, n, turn=0):
                s = PL.swi[nm]
                pc = PL.pieces[s["first"] + r]
                act.wait_ge(sem(f"landed{pc['slot']}"), pc["landed"] + 64 * turn)
                if not isinstance(n, int) or s["split"] + n > 2:
                    act.wait_ge(sem("w_used"), s["split"] + n - 2)
                act.activation(w_hi[:, r % 3, :], piece(s["first"] + r), ACT.Copy).then_inc(sem("w_split_hi"), 1)

            def before(nm):
                split_piece(nm, 0, 0)
                split_piece(nm, 1, 1)

            def split_h(nm):
                n = NORMS.index("n_" + nm)
                for b in (0, 2, 1, 3):
                    if b == 0:
                        act.wait_ge(sem("norm_act"), 4 * (n + 1))
                    if b == 1:
                        act.wait_ge(sem("norm_dve"), 4 * (n + 1))
                    act.activation(h_hi[:, 2 * b:2 * b + 2, :], hT[:, 2 * b:2 * b + 2, :], ACT.Copy)\
                       .then_inc(sem("h_split_hi"), 1)

            def swiglu(nm):
                s = PL.swi[nm]
                G0, U0 = s["base"], s["split"]

                def chunk(c, q, n, split):
                    act.wait_ge(sem("w_used"), U0 + n + 1)
                    act.wait_ge(sem("hid_ready"), max(G0 + c, 1) if isinstance(c, int) else G0 + c)
                    act.activation(flat(hid[q % 2]), bank(4 + 2 * (q % 2)), ACT.Silu).then_inc(sem("silu_done"), 1)
                    split(3)
                    split(4)
                    split(5)

                split_piece(nm, 2, 2)
                chunk(0, 0, 0, lambda j: split_piece(nm, j, j) if j < 5 else None)
                loops = (s["n"] - 1) // 4
                with act.Fori(0, loops) as i:
                    for q in range(4):
                        chunk(4 * i + q + 1, q + 1, 12 * i + 3 * q + 2,
                              lambda j: split_piece(nm, 3 * q + 2 + j, 12 * i + 3 * q + 2 + j, i))
                for c in range(4 * loops + 1, s["n"]):
                    chunk(c, c % 4, 3 * c - 1,
                          lambda j: split_piece(nm, 3 * c - 1 + j, 3 * c - 1 + j) if 3 * c - 1 + j < 3 * s["n"] else None)

            def attention(kind):
                jobs, base = JOBS[kind], JOB_BASE[kind]
                for j in range(len(jobs) + 1):
                    J = base + j
                    if j < len(jobs):
                        segs = job(*jobs[j])[0]
                        n = segs[0]["n"]
                        act.wait_ge(sem("att_logits"), J + 1)
                        if J > 1:
                            act.wait_ge(sem("att_pt"), J - 1)
                        src = bank(2 * (j % 2), 2).rearrange("p (s n) -> p s n", n=T)[:, 0:len(segs), 0:n]
                        dst = att_p[:, j % 2, :].rearrange("p (s n) -> p s n", n=T)[:, 0:len(segs), 0:n]
                        act.activation(dst, src, ACT.Exp, bias=nmax[:, j % 2:j % 2 + 1],
                                       accum_out=esum[:, j % 4:j % 4 + 1]).then_inc(sem("att_exp"), 1)
                    if j >= 1:
                        J1 = J - 1
                        nb = sum(len(sg["v"]) for sg in job(*jobs[j - 1])[0])
                        act.wait_ge(sem("att_pt"), J1 + 1)
                        if J1 > 0:
                            act.wait_ge(sem("att_pv"), J1)
                        act.activation(att_pt[:, 0:P * nb], bank(4, 2)[:, 0:P * nb], ACT.Copy)\
                           .then_inc(sem("att_pts"), 1)

            act.wait_ge(sem("cols_in"), 80)
            act.wait_ge(sem("keep_in"), 16)

            act.wait_ge(sem("c_in"), 16)
            act.activation(csilu[:, :], cact[:, :], ACT.Silu).then_inc(sem("silu_done"), 1)

            def modulation(layer):
                act.wait_ge(sem("mod_rows"), layer + 1)
                for j in range(2):
                    act.activation(grow[layer][j], bank(2 * j, 2), ACT.Copy).then_inc(sem("mod_rows_in"), 1)

            modulation(0)
            norm("n_even")
            gemm("even_in")
            act.wait_ge(sem("ev_act"), 7)
            act.wait_ge(sem("ev_dve"), 7)
            act.activation(proj_e[:, :, 1536:2048], proj_e[:, :, 1536:2048], ACT.Silu).then_inc(sem("even_gate"), 1)
            transposes("ret_qk")
            for h in range(4):
                act.wait_ge(sem("ret_pv"), h + 1)
                act.activation(xn[:, :, P * h:P * h + P], bank(2 + h % 2)[:, 0:T].rearrange("p (t n) -> p t n", t=NT),
                               ACT.Copy).then_inc(sem("ret_moved"), 1)
            heads(0)
            heads(1)
            transposes("att_qk")
            attention("att")
            transposes("even_mix")

            def router(layer):
                act.wait_ge(sem("router_ps"), layer + 1)
                act.activation(rt_sc, bank(4)[:, 0:2 * NE], ACT.Sigmoid).then_inc(sem("router_sig"), 1)
                for b in range(0, 8, 2):
                    act.wait_ge(sem("comb_ps"), 8 * layer + b + 1)
                    act.activation(flat(comb_b[:, 2 * b:2 * b + 2, :]), bank(b), ACT.Copy).then_inc(sem("comb_act"), 1)

            before("moe0")
            norm("n_moe0")
            split_h("moe0")
            router(0)
            swiglu("moe0")
            act.wait_ge(sem("x_new"), 2)
            modulation(1)
            norm("n_odd")
            gemm("odd_in")
            for s_ in range(17):
                if s_ < 16:
                    h = s_
                    act.wait_ge(sem("sb_z"), h + 1)
                    if h > 1:
                        act.wait_ge(sem("sb_soft"), h - 1)
                    step(act.activation(sb_abs[h % 2], bank(h % 2)[:, 0:384], ACT.Abs))
                    step(act.activation(sb_abs[h % 2], sb_abs[h % 2], ACT.Exp, scale=-1.0))
                    act.activation(sb_abs[h % 2], sb_abs[h % 2], ACT.Ln, bias=1.0).then_inc(sem("sb_ln"), 1)
                if s_ >= 1:
                    h = s_ - 1
                    act.wait_ge(sem("sb_sums"), h + 1)
                    if h > 1:
                        act.wait_ge(sem("sb_pv"), h - 1)
                    act.activation(sb_a[h % 2], bank(2 + h % 2)[:, 0:384], ACT.Exp).then_inc(sem("sb_exp"), 1)
            transposes("odd_mix")
            before("moe1")
            norm("n_moe1")
            split_h("moe1")
            router(1)
            swiglu("moe1")
            before("pre0")
            norm("n_pre0")
            split_h("pre0")
            swiglu("pre0")
            norm("n_mem0")
            gemm("mem0")
            heads(2)
            transposes("mem0_k")
            norm("n_mix0")
            gemm("a_in")
            heads(3)
            transposes("mem0_q")
            attention("mem0")
            act.wait_ge(sem("shift_mixed"), SHIFT_TILES)
            act.activation(F[0:64, 18, :], F[0:64, 18, :], ACT.Tanh).then_inc(sem("rw_low"), 1)
            act.activation(F[:, 19, :], F[:, 19, :], ACT.Sigmoid).then_inc(sem("rw_low"), 1)
            act.wait_ge(sem("rw_w_ps"), 1)
            for i in range(6):
                m = act.activation(W[0][:, i, :], bank(i // 2)[:, T * (i % 2):T * (i % 2) + T], ACT.Sigmoid,
                                   bias=rcols[:, 20 + i:21 + i])
            m.then_inc(sem("rw_sig"), 1)
            act.wait_ge(sem("rw_a_ps"), 1)
            for i in range(6):
                m = act.activation(W[1][:, i, :], bank(3 + i // 2)[:, T * (i % 2):T * (i % 2) + T], ACT.Sigmoid,
                                   bias=rcols[:, 26 + i:27 + i])
            m.then_inc(sem("rw_sig"), 1)
            act.wait_ge(sem("rw_g_ps"), 1)
            for n in range(3):
                m = act.activation(flat(gate)[:, 512 * n:512 * n + 512], bank((6 + n) % 8), ACT.Copy)
            m.then_inc(sem("rw_gate"), 1)
            act.wait_ge(sem("rw_ssr"), 1)
            act.activation(Wf[5], Wf[5], ACT.Sqrt).then_inc(sem("rw_kkn"), 1)
            act.wait_ge(sem("rw_prev"), 1)
            act.activation(Wf[0], Wf[0], ACT.Exp, scale=-DECAY).then_inc(sem("rw_dec"), 1)
            act.wait_ge(sem("rw_decayed"), 1)
            act.activation(Wf[0], Wf[2], ACT.Exp, scale=DECAY).then_inc(sem("rw_dec"), 1)
            act.wait_ge(sem("rw_decayed"), 2)
            act.activation(Wf[0], Wf[2], ACT.Exp, scale=-DECAY).then_inc(sem("rw_dec"), 1)
            for nm in ("rw_v", "rw_b", "rw_k"):
                transposes(nm)
            for i in range(6):
                for l in range(5):
                    act.wait_ge(sem("rw_x_ps"), 5 * i + l + 1)
                    if 5 * i + l > 0:
                        act.wait_ge(sem("rw_tx_ps"), 5 * i + l)
                    act.activation(flat(t_x), bank(4), ACT.Copy).then_inc(sem("rw_x"), 1)
                act.wait_ge(sem("rw_u_ps"), i + 1)
                act.activation(U[:, :, P * i:P * i + P], bank(7)[:, 0:T].rearrange("p (t n) -> p t n", t=NT),
                               ACT.Copy).then_inc(sem("rw_u"), 1)
            for c in range(4):
                t, rows = c // 2, slice(64 * (c % 2), 64 * (c % 2) + 64)
                act.wait_ge(sem("rw_y_ps"), c + 1)
                act.activation(y_r[rows, t, :], bank(2, 2)[rows, 0:768], ACT.Copy).then_inc(sem("rw_y"), 1)
            act.wait_ge(sem("rw_yvar"), 1)
            act.activation(hrstd, hvar, ACT.Sqrt).then_inc(sem("rw_yrstd"), 1)
            transposes("a_mix")
            before("post0")
            norm("n_post0")
            split_h("post0")
            swiglu("post0")
            norm("n_kv")
            gemm("kv")
            heads(4)
            transposes("kd")
            before("pre1")
            norm("n_pre1")
            split_h("pre1")
            swiglu("pre1")
            norm("n_mem1")
            gemm("mem1")
            heads(5)
            transposes("mem1_k")
            norm("n_mix1")
            gemm("b_q")
            heads(6)
            transposes("dil_q")
            attention("mem1")
            attention("dil")
            transposes("b_mix")
            before("post1")
            norm("n_post1")
            split_h("post1")
            swiglu("post1")

        @block.vector
        def _(dve):
            done = [0]

            def step(ins):
                done[0] += 1
                ins.then_inc(sem("dve_step"), 1)
                dve.wait_ge(sem("dve_step"), done[0])

            def norm(nm):
                n = NORMS.index(nm)
                dve.wait_ge(sem("norm_ss"), 2 * (n + 1))
                step(dve.tensor_scalar(var, ss, 1.0 / D, EPS, ALU.mult, ALU.add))
                dve.reciprocal(var, var).then_inc(sem("norm_var"), 1)
                dve.wait_ge(sem("norm_rstd"), n + 1)
                for t in range(NT):
                    dve.tensor_scalar(xn[:, t, :], NSRC[nm][:, t, :], rstd[:, t:t + 1], None, ALU.mult)\
                       .then_inc(sem("norm_xn"), 1)
                for j in (2, 3, 6, 7):
                    b = j // 2
                    dve.wait_ge(sem("norm_T"), 4 * n + b + 1)
                    if nm in NSHIFT:
                        m = dve.tensor_scalar(hT[:, j, :], bank(b)[:, T * (j % 2):T * (j % 2) + T], NGAIN[nm][:, j:j + 1],
                                              NSHIFT[nm][:, j:j + 1], ALU.mult, ALU.add)
                    else:
                        m = dve.tensor_scalar(hT[:, j, :], bank(b)[:, T * (j % 2):T * (j % 2) + T], NGAIN[nm][:, j:j + 1], None, ALU.mult)
                    m.then_inc(sem("norm_dve"), 1)

            def gemm(nm):
                g = PL.gemms[nm]
                for c in range(g["n"]):
                    G = g["base"] + c
                    kind, dst = gemm_dst(nm, c)
                    dve.wait_ge(sem("gemm_done"), PL.done_at[G])
                    pair = 2 * (G % 4)
                    ps = bank(pair + 1)
                    if kind == "copy":
                        d = dst[:, 1, :]
                        dve.tensor_copy(d, ps[:, 0:d.shape[1]]).then_inc(sem("ev_dve"), 1)
                    elif kind == "feat":
                        dve.tensor_scalar(flat(dst[:, 2:4, :]), ps, 0.125 if c < 2 else 1.0, None, ALU.mult)\
                           .then_inc(sem("ev_dve"), 1)
                    elif kind == "kv":
                        for lo, hi, d, o in KV_PARTS[c]:
                            m = dve.tensor_copy(d[:, 1, o:o + hi - lo], ps[:, lo:hi])
                        m.then_inc(sem("ev_dve"), 1)
                    elif kind == "shift":
                        for f in range(4):
                            n = 4 * c + f
                            dve.wait_ge(sem("shift_mu"), n - n % 2 + 2)
                            m = dve.scalar_tensor_tensor(
                                out=F[:, n, :], in0=bank(pair + f // 2)[:, T * (f % 2):T * (f % 2) + T],
                                scalar=omu[:, n:n + 1], in1=sh_tmp[n % 4][:, 0:T], op0=ALU.mult, op1=ALU.add)
                            m.then_inc(sem("shift_mixed"), 1)
                    else:
                        cols = slice(512 * c, 512 * c + 512)
                        both = psum[:, pair:pair + 2, :]
                        if kind == "resid_g":
                            row = grow[dst[0]][0][:, cols].unsqueeze(1)
                            step(dve.tensor_tensor(xn[:, :, cols], both, bc(row, [P, NT, 512]), ALU.mult))
                            m = dve.tensor_tensor(x[:, :, cols], x[:, :, cols], xn[:, :, cols], ALU.add)
                        else:
                            m = dve.tensor_tensor(x[:, :, cols], x[:, :, cols], both, ALU.add)
                        if c == 1:
                            m.then_inc(sem("x_new"), 1)
                        else:
                            m.then_inc(sem("resid_first"), 1)

            def transposes(nm):
                for i, (srcs, dst) in enumerate(TRS[nm]):
                    B = TR_BASE[nm] + i
                    if B % 2 == 1:
                        dve.wait_ge(sem("tr_done"), B + 1)
                        dve.tensor_copy(dst, bank(4 + B % 4)[:, 0:P * len(srcs)]).then_inc(sem("tr_dve"), 1)

            def heads(n, parts, width, gains, scale=1.0):
                col = 0
                for v in parts:
                    H = v.shape[1]
                    sq = pool[:, XN:XN + H * width].rearrange("p (h d) -> p h d", h=H) if n > 1 else \
                        pool[:, WORK + 4992:WORK + 4992 + H * width].rearrange("p (h d) -> p h d", h=H)
                    step(dve.tensor_tensor(sq, v, v, ALU.mult))
                    m = dve.tensor_reduce(hss[:, col:col + H], sq, AX.X, ALU.add)
                    step(m)
                    col += H
                if col < 32:
                    step(dve.memset(hss[:, col:32], 1.0))
                step(dve.tensor_scalar(hvar, hss, 1.0 / width, EPS, ALU.mult, ALU.add))
                dve.reciprocal(hvar, hvar).then_inc(sem("heads_var"), 1)
                dve.wait_ge(sem("heads_rstd"), n + 1)
                col = 0
                for v in parts:
                    H = v.shape[1]
                    m = dve.tensor_tensor(v, v, bc(hrstd[:, col:col + H].unsqueeze(2), [P, H, width]), ALU.mult)
                    col += H
                    step(m)
                    for lo, hi, g, s in gains:
                        vv = v[:, lo:hi, :]
                        step(dve.scalar_tensor_tensor(out=vv, in0=vv, scalar=s,
                                                      in1=bc(gains64[:, g, :].unsqueeze(1), [P, hi - lo, width]),
                                                      op0=ALU.mult, op1=ALU.mult))

            def attention(kind):
                jobs, base = JOBS[kind], JOB_BASE[kind]
                for j in range(len(jobs) + 2):
                    J = base + j
                    if j < len(jobs):
                        segs = job(*jobs[j])[0]
                        n = segs[0]["n"]
                        dve.wait_ge(sem("att_scores"), J + 1)
                        if J > 1:
                            dve.wait_ge(sem("att_exp"), J - 1)
                        lg = bank(2 * (j % 2), 2).rearrange("p (s n) -> p s n", n=T)
                        step(dve.tensor_reduce(mx[:, j % 2:j % 2 + 1], lg[:, 0:len(segs), 0:n], AX.XY, ALU.max))
                        dve.tensor_scalar(nmax[:, j % 2:j % 2 + 1], mx[:, j % 2:j % 2 + 1], -1.0, None, ALU.mult)\
                           .then_inc(sem("att_logits"), 1)
                    if j >= 2:
                        o = job(*jobs[j - 2])[1]
                        if J > 1:
                            dve.wait_ge(sem("att_pv"), J - 1)
                        step(dve.reciprocal(erec[:, j % 2:j % 2 + 1], esum[:, (j - 2) % 4:(j - 2) % 4 + 1]))
                        dve.tensor_scalar(o, bank(6 + j % 2)[:, 0:64], erec[:, j % 2:j % 2 + 1], None, ALU.mult)\
                           .then_inc(sem("att_o"), 1)

            def split_piece(nm, r, n):
                s = PL.swi[nm]
                dve.wait_ge(sem("w_split_hi"), s["split"] + n + 1)
                dve.tensor_tensor(w_lo[:, r % 3, :], piece(s["first"] + r), w_hi[:, r % 3, :].bitcast(F32),
                                  ALU.subtract).then_inc(sem("w_lo"), 1)

            def split_h(nm):
                for i, b in enumerate((0, 2, 1, 3)):
                    dve.wait_ge(sem("h_split_hi"), 4 * PL.swi[nm]["no"] + i + 1)
                    dve.tensor_tensor(h_lo[:, 2 * b:2 * b + 2, :], hT[:, 2 * b:2 * b + 2, :],
                                      h_hi[:, 2 * b:2 * b + 2, :].bitcast(F32), ALU.subtract)\
                       .then_inc(sem("h_split_lo"), 1)

            def swiglu(nm):
                s = PL.swi[nm]
                G0, U0 = s["base"], s["split"]
                moe = nm.startswith("moe")
                pp = 2 if moe else 1
                P0 = sum(PL.swi[k]["n"] * (2 if k.startswith("moe") else 1) for k in SWIGLUS[:s["no"]])

                def product(c, q, n, e):
                    dve.wait_ge(sem("silu_done"), G0 + c + 2)
                    dve.wait_ge(sem("w_used"), U0 + n + 1)
                    h = hid[q % 2]
                    dve.tensor_tensor(flat(h), flat(h), bank(5 + 2 * (q % 2)), ALU.mult).then_inc(sem("hid_prod"), 1)
                    if moe:
                        dve.wait_ge(sem("hid_prod"), P0 + pp * c + 1)
                        dve.tensor_tensor(h[:, :, :], h[:, :, :], bc(comb_b[:, e, :].unsqueeze(1), [P, 2, T]), ALU.mult)\
                           .then_inc(sem("hid_prod"), 1)
                    dve.wait_ge(sem("hid_prod"), P0 + pp * c + pp)
                    dve.tensor_copy(flat(hid_hi[:, q % 2]), flat(h)).then_inc(sem("hid_round"), 1)
                    dve.wait_ge(sem("hid_round"), G0 + c + 1)
                    dve.tensor_tensor(flat(hid_lo[:, q % 2]), flat(h), flat(hid_hi[:, q % 2]).bitcast(F32), ALU.subtract)\
                       .then_inc(sem("hid_ready"), 1)

                def ada_part(i, q):
                    dve.wait_ge(sem("ada1_landed"), 32 * i + 16 * q + 16)
                    half = acc[:, q * ADA_HALF:(q + 1) * ADA_HALF]
                    dve.scalar_tensor_tensor(out=half, in0=ada1, scalar=csilu[:, bass.ds(i, 1)], in1=half,
                                             op0=ALU.mult, op1=ALU.add).then_inc(sem("ada_used"), 1)

                if nm == "moe0":
                    dve.wait_ge(sem("ada_b_in"), 32)
                for r in (1, 2, 3):
                    split_piece(nm, r, r)
                product(0, 0, 1, 0)
                split_piece(nm, 4, 4)
                loops = (s["n"] - 1) // 4
                with dve.Fori(0, loops) as i:
                    for q in range(4):
                        r = 3 * q + 5
                        split_piece(nm, r, 12 * i + r)
                        product(4 * i + q + 1, q + 1, 12 * i + r - 2, 2 * i + (q + 1) // 2)
                        split_piece(nm, r + 1, 12 * i + r + 1)
                        split_piece(nm, r + 2, 12 * i + r + 2)
                        if nm == "moe0" and q % 2:
                            ada_part(i, q // 2)
                for c in range(4 * loops + 1, s["n"]):
                    if 3 * c + 2 < 3 * s["n"]:
                        split_piece(nm, 3 * c + 2, 3 * c + 2)
                    product(c, c % 4, 3 * c, c // 2)
                    for n in (3 * c + 3, 3 * c + 4):
                        if n < 3 * s["n"]:
                            split_piece(nm, n, n)
                    if nm == "moe0" and c == s["n"] - 2:
                        ada_part(loops, 0)
                if nm == "moe0":
                    ada_part(loops, 1)
                dve.wait_ge(sem("sums_done"), s["no"] + 1)
                for t in range(NT):
                    ps = bank(2 * t, 2)
                    if moe:
                        step(dve.tensor_tensor(xn[:, t, :], ps, grow[int(nm[-1])][1], ALU.mult))
                        m = dve.tensor_tensor(x[:, t, :], x[:, t, :], xn[:, t, :], ALU.add)
                    else:
                        m = dve.scalar_tensor_tensor(out=x[:, t, :], in0=ps, scalar=0.5, in1=x[:, t, :],
                                                     op0=ALU.mult, op1=ALU.add)
                    m.then_inc(sem("x_new" if t else "x_part"), 1)

            def mod_cols(layer):
                dve.wait_ge(sem("mod_cols"), layer + 1)
                step(dve.tensor_copy(mcols[:, layer].rearrange("p j k -> p (j k)"), bank(4)[:, 0:4 * KD]))
                for j in range(2):
                    m = dve.scalar_tensor_tensor(out=mgain[:, 2 * layer + j, :], in0=mcols[:, layer, 1 + 2 * j, :],
                                                 scalar=1.0, in1=gcols[:, layer + 2 * j, :], op0=ALU.add, op1=ALU.mult)
                m.then_inc(sem("mod_moved"), 1)

            dve.wait_ge(sem("bias_ps"), 2)
            dve.wait_ge(sem("hot_in"), 80)
            dve.tensor_copy(view(WORK + 4256, 512)[0:8, :], bank(6)[0:8, :]).then_inc(sem("bias_rows"), 1)
            dve.tensor_tensor(view(WORK + 4768, 512)[0:12, :], bank(7)[0:12, :], view(WORK + 2176, 4, 512)[0:12, 3, :],
                              ALU.add).then_inc(sem("bias_rows"), 1)
            dve.wait_ge(sem("cols_in"), 80)
            dve.tensor_scalar(omu[:, :], rcols[:, 0:SHIFT_TILES], -1.0, 1.0, ALU.mult, ALU.add).then_inc(sem("hid_ready"), 1)
            dve.wait_ge(sem("silu_done"), 1)
            dve.wait_ge(sem("ada_b_in"), 16)
            for b in range(ADA_PIECES):
                t, q = b // ADA_PER_ROW, b % ADA_PER_ROW
                dve.wait_ge(sem(f"landed{PL.pieces[b]['slot']}"), PL.pieces[b]["landed"])
                part = acc[:, q * PIECE:(q + 1) * PIECE]
                if b >= ADA_PER_ROW:
                    dve.wait_ge(sem("ada_used"), b - ADA_PER_ROW + 1)
                dve.scalar_tensor_tensor(out=part, in0=piece(b), scalar=csilu[:, t:t + 1], in1=part,
                                         op0=ALU.mult, op1=ALU.add).then_inc(sem("ada_used"), 1)
            mod_cols(0)
            dve.wait_ge(sem("keep_in"), 16)
            norm("n_even")
            gemm("even_in")
            dve.wait_ge(sem("ev_act"), 7)
            dve.wait_ge(sem("ev_dve"), 7)
            dve.wait_ge(sem("even_in"), 16)
            dve.wait_ge(sem("bias_out"), 32)
            for t in range(NT):
                v = proj_e[:, t, 0:1024].rearrange("p (h d) -> p h d", h=8)
                x1, x2 = v[:, :, 0:64], v[:, :, 64:128]
                co = bc(rope_c[:, t, :].unsqueeze(1), [P, 8, 64])
                si = bc(rope_s[:, t, :].unsqueeze(1), [P, 8, 64])
                r = [z.rearrange("p (h d) -> p h d", h=8) for z in (rot_a[:, 0, :], rot_a[:, 1, :],
                                                                    rot_b[:, 0, :], rot_b[:, 1, :])]
                dve.tensor_tensor(r[0], x1, co, ALU.mult)
                dve.tensor_tensor(r[1], x2, si, ALU.mult)
                dve.tensor_tensor(r[2], x1, si, ALU.mult)
                step(dve.tensor_tensor(r[3], x2, co, ALU.mult))
                dve.tensor_tensor(x1, r[0], r[1], ALU.subtract)
                step(dve.tensor_tensor(x2, r[2], r[3], ALU.add))
            dve.memset(tiny[:, 160:161], 0.0).then_inc(sem("rotated"), 1)
            transposes("ret_qk")
            for h in range(4):
                dve.wait_ge(sem("ret_scores"), h + 1)
                if h > 1:
                    dve.wait_ge(sem("ret_pv"), h - 1)
                dve.tensor_tensor(ret_s[:, h % 2, :], bank(h % 2)[:, 0:384], decay_t[:, h, :], ALU.mult)\
                   .then_inc(sem("ret_decayed"), 1)
            dve.wait_ge(sem("norm_T"), 4)
            qk = [proj_e[:, t, 2048:3072].rearrange("p (h d) -> p h d", h=16) for t in range(NT)]
            heads(0, qk, 64, [(0, 8, 0, 0.125), (8, 16, 1, 1.0)])
            dve.memset(tiny[:, 160:161], 0.0).then_inc(sem("heads_ok"), 1)
            dve.wait_ge(sem("ret_moved"), 4)
            rr = [xn[:, t, 0:512].rearrange("p (h d) -> p h d", h=4) for t in range(NT)]
            heads(1, rr, P, [])
            dve.wait_ge(sem("even_gate"), 1)
            dve.tensor_tensor(xn[:, :, 0:512], xn[:, :, 0:512], proj_e[:, :, 1536:2048], ALU.mult)\
               .then_inc(sem("even_mixed"), 1)
            transposes("att_qk")
            attention("att")
            transposes("even_mix")
            gemm("even_out")

            def router(layer):
                dve.wait_ge(sem("router_sig"), layer + 1)
                sel, cmp_, eq = rt[:, 32:64], rt[:, 64:192], rt[:, 192:320]
                rank, pick, gs = rt[:, 320:352], rt[:, 352:384], rt[:, 384:392]
                gpick, tot = rt[:, 392:400], rt[:, 400:402]
                step(dve.tensor_tensor(sel.rearrange("p (t e) -> p t e", t=NT), rt_sc.rearrange("p (t e) -> p t e", t=NT),
                                       bc(router_b[:, :].unsqueeze(1), [P, NT, NE]), ALU.add))

                def ranks(v, groups, out_):
                    n = 16 * groups
                    v3 = v.rearrange("p (g e) -> p g e", e=4)
                    other = bc(v3.unsqueeze(2), [P, groups, 4, 4])
                    own = bc(v3.unsqueeze(3), [P, groups, 4, 4])
                    c4 = cmp_[:, 0:n].rearrange("p (g e j) -> p g e j", g=groups, e=4)
                    q4 = eq[:, 0:n].rearrange("p (g e j) -> p g e j", g=groups, e=4)
                    dve.tensor_tensor(c4, other, own, ALU.is_gt)
                    step(dve.tensor_tensor(q4, other, own, ALU.is_equal))
                    step(dve.tensor_tensor(eq[:, 0:n].rearrange("p (g k) -> p g k", g=groups),
                                           eq[:, 0:n].rearrange("p (g k) -> p g k", g=groups),
                                           bc(K["lower"].unsqueeze(1), [P, groups, 16]), ALU.mult))
                    step(dve.tensor_tensor(cmp_[:, 0:n], cmp_[:, 0:n], eq[:, 0:n], ALU.add))
                    step(dve.tensor_reduce(out_, cmp_[:, 0:n].rearrange("p (g j) -> p g j", j=4), AX.X, ALU.add))

                ranks(sel, 8, rank)
                step(dve.tensor_scalar(pick, rank, 1.5, None, ALU.is_lt))
                step(dve.tensor_tensor(sel, sel, pick, ALU.mult))
                step(dve.tensor_reduce(gs, sel.rearrange("p (g e) -> p g e", e=4), AX.X, ALU.add))
                ranks(gs, 2, gpick)
                step(dve.tensor_scalar(gpick, gpick, 0.5, None, ALU.is_lt))
                step(dve.tensor_tensor(pick.rearrange("p (g e) -> p g e", e=4), pick.rearrange("p (g e) -> p g e", e=4),
                                       bc(gpick.unsqueeze(2), [P, 8, 4]), ALU.mult))
                step(dve.tensor_tensor(pick, pick, rt_sc, ALU.mult))
                step(dve.tensor_reduce(tot, pick.rearrange("p (t e) -> p t e", t=NT), AX.X, ALU.add))
                step(dve.reciprocal(tot, tot))
                dve.tensor_tensor(comb_tok.rearrange("p (t e) -> p t e", t=NT), pick.rearrange("p (t e) -> p t e", t=NT),
                                  bc(tot.unsqueeze(2), [P, NT, NE]), ALU.mult).then_inc(sem("comb_tok"), 1)
                dve.wait_ge(sem("comb_T_ps"), layer + 1)
                dve.tensor_copy(comb_t, bank(5)[0:NE, 0:T]).then_inc(sem("comb_T"), 1)
                for b in range(1, 8, 2):
                    dve.wait_ge(sem("comb_ps"), 8 * layer + b + 1)
                    dve.tensor_copy(flat(comb_b[:, 2 * b:2 * b + 2, :]), bank(b)).then_inc(sem("comb_dve"), 1)

            split_piece("moe0", 0, 0)
            norm("n_moe0")
            split_h("moe0")
            router(0)
            dve.memset(tiny[:, 160:161], 0.0).then_inc(sem("moe_ready"), 1)
            swiglu("moe0")
            mod_cols(1)
            dve.wait_ge(sem("mod_rows_in"), 4)
            norm("n_odd")
            gemm("odd_in")
            step(dve.memset(sb_zero, 0.0))
            for s_ in range(18):
                if s_ < 16:
                    h = s_
                    dve.wait_ge(sem("sb_ln"), h + 1)
                    if h > 1:
                        dve.wait_ge(sem("sb_sums"), h - 1)
                    dve.scalar_tensor_tensor(out=sb_sp[h % 2], in0=bank(h % 2)[:, 0:384], scalar=0.0, in1=sb_abs[h % 2],
                                             op0=ALU.max, op1=ALU.add).then_inc(sem("sb_soft"), 1)
                    dve.wait_ge(sem("sb_soft"), h + 1)
                    diag = sb_sp[h % 2].rearrange("p (b n) -> p b n", b=3)
                    dve.copy_predicated(diag[:, 0, :], K["neg_from"].bitcast(U32), sb_zero)
                    dve.copy_predicated(diag[:, 2, :], K["neg_from"].bitcast(U32), sb_zero)\
                       .then_inc(sem("sb_masked"), 1)
                if 1 <= s_ <= 16:
                    h = s_ - 1
                    dve.wait_ge(sem("sb_exp"), h + 1)
                    diag = sb_a[h % 2].rearrange("p (b n) -> p b n", b=3)
                    dve.copy_predicated(diag[:, 0, :], K["neg_from"].bitcast(U32), sb_zero)
                    dve.copy_predicated(diag[:, 2, :], K["neg_from"].bitcast(U32), sb_zero)\
                       .then_inc(sem("sb_weights"), 1)
                if s_ >= 2:
                    h = s_ - 2
                    dve.wait_ge(sem("sb_pv"), h + 1)
                    dve.tensor_copy(xn[:, :, 64 * h:64 * h + 64],
                                    bank(4 + h % 2)[:, 0:128].rearrange("p (t d) -> p t d", t=NT))\
                       .then_inc(sem("sb_out"), 1)
            transposes("odd_mix")
            gemm("odd_out")
            split_piece("moe1", 0, 0)
            norm("n_moe1")
            split_h("moe1")
            router(1)
            swiglu("moe1")
            split_piece("pre0", 0, 0)
            norm("n_pre0")
            split_h("pre0")
            swiglu("pre0")
            norm("n_mem0")
            gemm("mem0")

            def mem_keys(n, q):
                for e in moved(f"mem{q}", 0):
                    dve.wait_ge(sem(e[0]), e[1])
                mk = [mem_kv[:, t, 0:256].rearrange("p (h d) -> p h d", h=4) for t in range(NT)]
                dve.wait_ge(sem("norm_T"), 4 * (NORMS.index(f"n_mem{q}") + 1))
                heads(n, mk, 64, [(0, 4, 4 + q, 1.0)])
                dve.tensor_copy(mem_v, mem_kv[:, :, 256:512]).then_inc(sem("heads_ok"), 1)
                transposes(f"mem{q}_k")

            mem_keys(2, 0)
            norm("n_mix0")
            for z in sh_tmp:
                m = dve.memset(z[:, 0:1], 0.0)
            step(m)
            gemm("a_in")
            dve.wait_ge(sem("shift_mixed"), SHIFT_TILES)
            dve.wait_ge(sem("rwkv_in"), 96)
            par = rwkv_par
            for e in moved("a_in", 5):
                dve.wait_ge(sem(e[0]), e[1])
            mq = [q_mem_a[:, t, :].rearrange("p (h d) -> p h d", h=4) for t in range(NT)]
            dve.wait_ge(sem("norm_T"), 4 * (NORMS.index("n_mix0") + 1))
            heads(3, mq, 64, [(0, 4, 2, 0.125)])
            dve.memset(tiny[:, 160:161], 0.0).then_inc(sem("heads_ok"), 1)
            transposes("mem0_q")
            attention("mem0")
            for i in range(6):
                m = dve.tensor_scalar(W[3][:, i, :], Fk[:, i, :], rcols[:, 32 + i:33 + i], None, ALU.mult)
            step(m)
            dve.tensor_tensor(Wf[4], Wf[3], Wf[3], ALU.mult).then_inc(sem("rw_sq"), 1)
            dve.wait_ge(sem("rw_sig"), 1)
            dve.wait_ge(sem("reset_in"), 16)
            for i in range(6):
                m = dve.tensor_tensor_scan(W[2][:, i, :], rw_reset, W[0][:, i, :], 0.0, ALU.mult, ALU.add)
            step(m)
            dve.tensor_tensor(Wf[0], Wf[2], Wf[0], ALU.subtract).then_inc(sem("rw_prev"), 1)
            dve.wait_ge(sem("rw_ss_ps"), 1)
            dve.tensor_scalar(Wf[5], bank(3, 3), 1e-24, None, ALU.max).then_inc(sem("rw_ss"), 1)
            dve.wait_ge(sem("rw_ss"), 1)
            dve.reciprocal(Wf[5], Wf[5]).then_inc(sem("rw_ssr"), 1)
            dve.wait_ge(sem("rw_sig"), 2)
            for i in range(6):
                m = dve.tensor_scalar(W[4][:, i, :], W[1][:, i, :], -1.0, rcols[:, 38 + i:39 + i], ALU.add, ALU.mult)
            step(m)
            step(dve.scalar_tensor_tensor(out=flat(Fk), in0=Wf[4], scalar=1.0, in1=flat(Fk), op0=ALU.add, op1=ALU.mult))
            for i in range(6):
                m = dve.scalar_tensor_tensor(out=W[4][:, i, :], in0=Fr[:, i, :], scalar=rcols[:, 44 + i:45 + i],
                                             in1=Fk[:, i, :], op0=ALU.mult, op1=ALU.mult)
            m.then_inc(sem("rw_rk"), 1)
            dve.wait_ge(sem("rw_kkn"), 1)
            step(dve.tensor_tensor(Wf[3], Wf[3], Wf[5], ALU.mult))
            step(dve.tensor_tensor(Wf[1], Wf[1], Wf[3], ALU.mult))
            dve.wait_ge(sem("rw_dec"), 1)
            dve.tensor_tensor(Wf[3], Wf[3], Wf[0], ALU.mult).then_inc(sem("rw_decayed"), 1)
            dve.wait_ge(sem("rw_dec"), 2)
            dve.tensor_tensor(Wf[5], Wf[1], Wf[0], ALU.mult)
            dve.tensor_tensor(flat(Fk), flat(Fk), Wf[0], ALU.mult).then_inc(sem("rw_decayed"), 1)
            dve.wait_ge(sem("rw_dec"), 3)
            dve.tensor_tensor(flat(Fr), flat(Fr), Wf[0], ALU.mult)
            for c in range(4):
                m = dve.tensor_copy(pend[:, :, c:c + 1], W[0][:, :, 64 * c + 63:64 * c + 64])
            step(m)
            dve.wait_ge(sem("rw_bonus_ps"), 1)
            dve.tensor_copy(bonus, bank(1)[:, 0:24]).then_inc(sem("rw_bonus"), 1)
            dve.memset(state, 0.0).then_inc(sem("rw_scaled"), 1)
            for nm in ("rw_v", "rw_b", "rw_k"):
                transposes(nm)
            levels = par[:, 3072:3712].rearrange("p (l n) -> p l n", l=5)
            lvl0_t, lvl0, strict = par[:, 3712:3840], par[:, 3840:3968], par[:, 3968:4096]

            def four(m_):
                return bc(m_.unsqueeze(1), [P, 4, P])

            for i in range(6):
                dve.wait_ge(sem("rw_l_ps"), i + 1)
                pv = psum[:, 0:2, 0:T].rearrange("p e (t n) -> p e t n", t=NT)
                lo_ = psum[:, 0:2, T:2 * T].rearrange("p e (t n) -> p e t n", t=NT)
                if i > 0:
                    dve.wait_ge(sem("rw_u_ps"), i)
                if i == 0:
                    dve.wait_ge(sem("tr_act"), tr_counts("rw_v")[0])
                    dve.wait_ge(sem("tr_act"), tr_counts("rw_k")[0])
                m = None
                lt4 = t_lt.rearrange("p (e t) n -> p e t n", e=2)
                x4 = t_lm.rearrange("p (e t) n -> p e t n", e=2)
                for e in range(2):
                    dve.tensor_tensor(lt4[:, e], pv[:, e], bc(strict.unsqueeze(1), [P, 2, P]), ALU.mult)
                    m = dve.tensor_tensor(x4[:, e], lo_[:, e], bc(lvl0.unsqueeze(1), [P, 2, P]), ALU.mult)
                step(m)
                step(dve.tensor_tensor(t_t, four(ident), t_lm, ALU.subtract))
                step(dve.tensor_tensor(t_lm, t_lt, four(lvl0_t), ALU.mult))
                step(dve.tensor_tensor(TT[:, i], four(ident), t_lm, ALU.subtract))
                for l in range(5):
                    dve.tensor_tensor(t_lm, t_lt, four(levels[:, l, :]), ALU.mult).then_inc(sem("rw_lm"), 1)
                    dve.wait_ge(sem("rw_tx_ps"), 5 * i + l + 1)
                    dve.tensor_tensor(flat(t_t), flat(t_t), bank(5), ALU.subtract)
                    step(dve.tensor_tensor(TT[:, i].rearrange("p m n -> p (m n)"), TT[:, i].rearrange("p m n -> p (m n)"),
                                           bank(6), ALU.subtract))
                for e in range(2):
                    m = dve.tensor_tensor(x4[:, e], psum[:, 2 + e, 0:T].rearrange("p (t n) -> p t n", t=NT),
                                          bc(strict.unsqueeze(1), [P, 2, P]), ALU.mult)
                m.then_inc(sem("rw_m"), 1)
                dve.wait_ge(sem("rw_m"), i + 1)
                dve.memset(tiny[:, 161:162], 0.0).then_inc(sem("rw_t"), 1)
            step(dve.memset(SA, 0.0))
            dve.memset(tiny[:, 161:162], 0.0).then_inc(sem("rw_state"), 1)
            for c in range(4):
                t, q0 = c // 2, 64 * (c % 2)
                rows = slice(q0, q0 + 64)
                dve.wait_ge(sem("rw_z_ps"), c + 1)
                dve.wait_ge(sem("rw_u"), 6)
                dve.tensor_tensor(Z, bank(0, 2)[:, 0:768], U[:, t, :], ALU.add).then_inc(sem("rw_z"), 1)
                dve.wait_ge(sem("rw_sa_ps"), c + 1)
                dve.tensor_scalar(SA[rows, t, :], bank(4, 2)[rows, 0:768], -1.0, None, ALU.mult)\
                   .then_inc(sem("rw_sa"), 1)
                dve.wait_ge(sem("rw_new_ps"), c + 1)
                dve.wait_ge(sem("rw_y_ps"), c + 1)
                for e in range(2):
                    hf = slice(64 * e, 64 * e + 64)
                    st = state[hf, :, hf]
                    new = bank(6, 2)[hf, 0:768].rearrange("p (i n) -> p i n", i=6)[:, :, hf]
                    m = dve.tensor_tensor(st, st, new, ALU.add)
                step(m)
                for e in range(2):
                    hf = slice(64 * e, 64 * e + 64)
                    st = state[hf, :, hf]
                    m = dve.tensor_tensor(st, st, bc(pend[hf, :, c:c + 1], [64, 6, 64]), ALU.mult)
                m.then_inc(sem("rw_state"), 1)
            for i in range(6):
                dve.wait_ge(sem("rw_bk_ps"), i + 1)
                if i > 0:
                    dve.wait_ge(sem("rw_g2_ps"), i)
                for e in range(2):
                    inc = bc(K["chunk_incl"].unsqueeze(1), [P, 2, P])
                    dve.tensor_tensor(bm[:, 2 * e:2 * e + 2, :], psum[:, e, 0:T].rearrange("p (t n) -> p t n", t=NT),
                                      inc, ALU.mult)
                    m = dve.tensor_tensor(km[:, 2 * e:2 * e + 2, :], psum[:, 2 + e, 0:T].rearrange("p (t n) -> p t n", t=NT),
                                          inc, ALU.mult)
                m.then_inc(sem("rw_bk"), 1)
                dve.wait_ge(sem("rw_g2_ps"), i + 1)
                dve.wait_ge(sem("rw_y"), 4)
                yy = y_r[:, :, P * i:P * i + P]
                dve.tensor_tensor(yy, yy, bank(4)[:, 0:T].rearrange("p (t n) -> p t n", t=NT), ALU.add)\
                   .then_inc(sem("rw_yadd"), 1)
            dve.wait_ge(sem("rw_yadd"), 6)
            ys = [y_r[:, t, :].rearrange("p (h d) -> p h d", h=12) for t in range(NT)]
            ycs = [yc[:, t, :].rearrange("p (h d) -> p h d", h=12) for t in range(NT)]
            for t in range(NT):
                m = dve.tensor_reduce(hss[:, 12 * t:12 * t + 12], ys[t], AX.X, ALU.add)
            step(m)
            step(dve.tensor_scalar(hss[:, 0:24], hss[:, 0:24], 1.0 / 64, None, ALU.mult))
            for t in range(NT):
                m = dve.tensor_tensor(ycs[t], ys[t], bc(hss[:, 12 * t:12 * t + 12].unsqueeze(2), [P, 12, 64]), ALU.subtract)
            step(m)
            for t in range(NT):
                m = dve.tensor_tensor(ys[t], ycs[t], ycs[t], ALU.mult)
            step(m)
            for t in range(NT):
                m = dve.tensor_reduce(hss[:, 12 * t:12 * t + 12], ys[t], AX.X, ALU.add)
            step(m)
            step(dve.tensor_scalar(hvar[:, 0:24], hss[:, 0:24], 1.0 / 64, LNX_EPS, ALU.mult, ALU.add))
            dve.reciprocal(hvar[:, 0:24], hvar[:, 0:24]).then_inc(sem("rw_yvar"), 1)
            dve.wait_ge(sem("rw_yrstd"), 1)
            for t in range(NT):
                m = dve.tensor_tensor(ycs[t], ycs[t], bc(hrstd[:, 12 * t:12 * t + 12].unsqueeze(2), [P, 12, 64]), ALU.mult)
            step(m)
            for o, op in ((1536, ALU.mult), (2304, ALU.add)):
                for t in range(NT):
                    m = dve.tensor_tensor(yc[:, t, :], yc[:, t, :], par[:, o:o + 768], op)
                step(m)
            for t in range(NT):
                m = dve.tensor_tensor(ys[t], v_tok[:, t, :].rearrange("p (h d) -> p h d", h=12),
                                      bc(bonus[:, 12 * t:12 * t + 12].unsqueeze(2), [P, 12, 64]), ALU.mult)
            step(m)
            step(dve.tensor_tensor(y_r, y_r, yc, ALU.add))
            dve.wait_ge(sem("rw_gate"), 1)
            step(dve.tensor_tensor(y_r, y_r, gate, ALU.mult))
            dve.memset(tiny[:, 161:162], 0.0).then_inc(sem("rwkv_over"), 1)
            dve.memset(tiny[:, 160:161], 0.0).then_inc(sem("rw_out"), 1)
            transposes("a_mix")
            gemm("a_out")
            split_piece("post0", 0, 0)
            norm("n_post0")
            split_h("post0")
            swiglu("post0")
            norm("n_kv")
            gemm("kv")
            for e in moved("kv", 2):
                dve.wait_ge(sem(e[0]), e[1])
            dve.wait_ge(sem("norm_T"), 4 * (NORMS.index("n_kv") + 1))
            heads(4, [kd[:, t, :].rearrange("p (h d) -> p h d", h=12) for t in range(NT)], 64, [(0, 12, 7, 1.0)])
            dve.memset(tiny[:, 160:161], 0.0).then_inc(sem("heads_ok"), 1)
            transposes("kd")
            split_piece("pre1", 0, 0)
            norm("n_pre1")
            split_h("pre1")
            swiglu("pre1")
            norm("n_mem1")
            gemm("mem1")
            mem_keys(5, 1)
            norm("n_mix1")
            gemm("b_q")
            for e in moved("b_q", 1):
                dve.wait_ge(sem(e[0]), e[1])
            dve.wait_ge(sem("norm_T"), 4 * (NORMS.index("n_mix1") + 1))
            heads(6, [q_d[:, t, :].rearrange("p (h d) -> p h d", h=16) for t in range(NT)], 64,
                  [(0, 12, 6, 0.125), (12, 16, 3, 0.125)])
            dve.memset(tiny[:, 160:161], 0.0).then_inc(sem("heads_ok"), 1)
            transposes("dil_q")
            attention("mem1")
            attention("dil")
            transposes("b_mix")
            gemm("b_out")
            split_piece("post1", 0, 0)
            norm("n_post1")
            split_h("post1")
            swiglu("post1")


_WEIGHTS = ["x", "c", "ada_w", "ada_b", "even_w_in", "even_w_out", "odd_w_in", "odd_w_out", "router_w", "exp_w_gate",
            "exp_w_up", "exp_w_down", "mem_2", "ffn_pre_w_in_2", "ffn_pre_w_out_2", "ffn_post_w_in_2",
            "ffn_post_w_out_2", "mem_w_kv_2", "a_w_in_2", "a_w_up_2", "a_a_up_2", "a_g_up_2", "a_w_out_2", "b_w_q_2",
            "b_w_out_2", "kv_w_2", "rel_bias_2", "a_lnx_g_2", "a_lnx_b_2", "router_b"]


def kernel(**inputs):
    import concourse.bacc as _bacc
    from concourse.bass_utils import run_bass_kernel_spmd as _run

    n = {k: np.ascontiguousarray(v) for k, v in inputs.items()}
    arrays = {k: n[k] for k in _WEIGHTS}

    def cols(v):
        return v.reshape(-1, P).T

    gains = [n["norm1_g"][0], n["norm1_g"][1], n["norm2_g"][0], n["norm2_g"][1], n["ffn_pre_norm_2"][0],
             n["ffn_pre_norm_2"][1], n["mix_norm_2"][0], n["mix_norm_2"][1], n["ffn_post_norm_2"][0],
             n["ffn_post_norm_2"][1], n["mem_norm_2"][0], n["mem_norm_2"][1], n["kv_norm_2"]]
    arrays["gain_cols"] = np.ascontiguousarray(np.concatenate([cols(g) for g in gains], 1))
    arrays["rwkv_cols"] = np.ascontiguousarray(np.concatenate(
        [cols(v.reshape(-1)) for v in (n["a_shift_mu_2"], n["a_w0_2"], n["a_a0_2"], n["a_kk_scale_2"], n["a_k_a_2"],
                                       n["a_r_k_2"])], 1))
    arrays["gains64"] = np.ascontiguousarray(np.concatenate(
        [n["att_q_norm_g"].reshape(-1), n["att_k_norm_g"].reshape(-1), n["mem_q_norm_2"].reshape(-1),
         n["mem_k_norm_2"].reshape(-1), n["b_q_norm_2"].reshape(-1), n["kv_k_norm_2"].reshape(-1)]))
    rel = n["att_rel_bias"][0].T
    arrays["rel_t"] = np.ascontiguousarray(np.concatenate([rel, np.zeros((256 - rel.shape[0], 8), rel.dtype)], 0))
    arrays.update(constants())

    nc = _bacc.Bacc("TRN2", target_bir_lowering=False, num_devices=1)
    ins = {k: nc.dram_tensor(f"in_{k}", v.shape, mybir.dt.from_np(v.dtype), kind="ExternalInput").ap()
           for k, v in arrays.items()}
    out = nc.dram_tensor("out_x", (1, T, D), F32, kind="ExternalOutput").ap()
    build(nc, ins, out)
    r = _run(nc, [{f"in_{k}": v for k, v in arrays.items()}], core_ids=[0])
    return r.results[0]["out_x"]
```

```python
from contextlib import ExitStack
import math

import numpy as np
import concourse.bass as bass
from concourse import mybir

F32 = mybir.dt.float32
F32R = mybir.dt.float32r
BF16 = mybir.dt.bfloat16
U32 = mybir.dt.uint32
ALU = mybir.AluOpType
ACT = mybir.ActivationFunctionType
AX = mybir.AxisListType

P = 128
T = 256
NT = T // P
D = 1024
KD = D // P
EPS = 1e-6
LNX_EPS = 64e-5
NEG = -1e30
RAW = 3
PIECE = 2048
CHUNK = 64
EVEN_W = 3584
ODD_W = 3072
A_W = 2816
SHIFT_TILES = 20
NE = 16
DFF = 2816
HC = 256
MOE_CHUNKS = NE * 512 // HC
FFN_CHUNKS = DFF // HC
ADA_W = 6 * D
ADA_HALF = ADA_W // 2
ADA_PIECES = KD * ADA_W // PIECE
ADA_PER_ROW = ADA_W // PIECE
ADA_HALVES = 2 * KD
EARLY = 3
DECAY = math.exp(-0.5)


def constants():
    f = np.float32
    i = np.arange(P)
    c = {}
    same = (i[:, None] // CHUNK) == (i[None, :] // CHUNK)
    jj, tt = i[:, None], i[None, :]
    lower = np.array([[float(j < e) for j in range(4)] for e in range(4)]).reshape(1, 16)
    keep = np.concatenate([
        np.eye(P), np.ones((P, P)), np.where(jj >= tt, -1.0, 0.0), -np.ones((P, P)),
        (jj <= tt) & same, same, (i < 64)[:, None], (i >= 64)[:, None], np.repeat(lower, P, 0)], 1).astype(f)
    lv = [((jj >> (l + 1)) == (tt >> (l + 1))) & (((jj >> l) & 1) == 0) & (((tt >> l) & 1) == 1)
          for l in range(6)]
    rw_masks = np.concatenate(lv[1:] + [lv[0], lv[0].T, (jj < tt) & same], 1).astype(f)
    tok = np.arange(T)
    dec = []
    for h in range(4):
        lg = np.log(1.0 - 2.0 ** (-5.0 - h))
        m = np.exp(lg * np.abs(tok[None, :] - tok[:, None])) * (128.0 ** -0.5)
        m = m * ((tok[:, None] // CHUNK) <= (tok[None, :] // CHUNK))
        dec.append(np.concatenate([m[:P], m[P:, P:]], 1))
    inv = (10000.0 ** (-np.arange(0, 128, 2, dtype=np.float32) / np.float32(128))).astype(f)
    ang = (tok.astype(f)[:, None] * inv[None, :]).astype(f)
    rope = np.concatenate([np.cos(ang).reshape(2, P, 64).transpose(1, 0, 2).reshape(P, 128),
                           np.sin(ang).reshape(2, P, 64).transpose(1, 0, 2).reshape(P, 128)], 1)
    am = np.where((tok[None, :] // CHUNK) <= (tok[:, None] // CHUNK), 0.0, NEG)
    even = np.concatenate([np.concatenate(dec, 1), rope, am[:P, :P][::-1], am[P:][::-1]], 1).astype(f)
    reset = np.ones((P, T), f)
    reset[:, ::CHUNK] = 0.0
    dist = 255 - np.arange(512)
    hot_rel = np.zeros((256, 512), f)
    hot_rel[np.clip(dist, -63, 128) + 63, np.arange(512)] = 1.0
    d = np.maximum(dist, 0)
    df = np.maximum(d, 1).astype(np.float64)
    large = np.minimum(16 + np.floor(np.log(df / 16) / math.log(128) * 16 + 1e-9).astype(int), 31)
    bucket = np.where(d < 16, d, large)
    hot_t5 = np.zeros((32, 512), f)
    hot_t5[bucket, np.arange(512)] = 1.0
    ban = np.zeros((12, 512), f)
    for g, dil in enumerate((1, 4, 16)):
        ok = (dist >= 0) & (dist % dil == 0)
        if g == 0:
            ok &= dist <= 128
        ban[4 * g:4 * g + 4] = np.where(ok, 0.0, NEG)
    return {"c_keep": keep, "c_rw_masks": rw_masks, "c_even": even, "c_anti": np.eye(P, dtype=f)[::-1].copy(), "c_reset": reset, "c_hot_rel": hot_rel,
            "c_hot_t5": hot_t5, "c_ban": ban}


class Plan:

    def __init__(self):
        self.pieces = []
        self.held = [None] * RAW
        self.loads = [0] * RAW
        self.slot = 0
        self.ada_order = []
        self.gemms = {}
        self.done_at = []
        self.swi = {}
        self.gemm_chunks = self.swi_chunks = self.split = 0

    def add(self, kind, what, free):
        s = self.slot
        self.loads[s] += 1
        self.pieces.append(dict(kind=kind, what=what, slot=s, after=[self.held[s]], landed=16 * self.loads[s]))
        self.held[s] = free
        self.slot = (s + 1) % RAW

    def rwkv(self):
        self.pieces.append(dict(kind="rwkv", what=0, slot=0, after=[self.held[0], self.held[1]], landed=0))
        self.held[0] = self.held[1] = ("rwkv_over", 1)
        self.slot = 2

    def ada(self, row, third):
        self.ada_order.append((len(self.pieces), row, third))
        self.add("ada", ADA_PER_ROW * row + third, ("ada_used", len(self.ada_order)))

    def gemm(self, name, width, cols=256, between=()):
        g = dict(base=self.gemm_chunks, n=-(-width // 512), width=width, pieces=[], cols=cols, split=self.split)
        between = list(between)
        for o in range(0, width, cols):
            self.split += 1
            g["pieces"].append(len(self.pieces))
            self.add("gemm", (name, o), ("w_lo", self.split))
            if between:
                self.ada(*between.pop(0))
            if (o + cols) % 512 == 0 or o + cols >= width:
                self.done_at.append(self.split)
        for part in between:
            self.ada(*part)
        self.gemm_chunks += g["n"]
        self.gemms[name] = g

    def swiglu(self, name, n):
        first = len(self.pieces)
        self.swi[name] = dict(base=self.swi_chunks, n=n, first=first, no=len(self.swi), split=self.split,
                              pieces=list(range(first, first + 3 * n)))
        order = [("gate", 0), ("up", 0)]
        for c in range(1, n):
            order += [("gate", c), ("up", c), ("down", c - 1)]
        order.append(("down", n - 1))
        for kind, c in order:
            self.split += 1
            self.add(kind, (name, c), ("w_lo", self.split))
        self.swi_chunks += n


def plan():
    p = Plan()
    for row in range(KD):
        p.ada(row, 0)
    p.gemm("even_in", EVEN_W, between=[(row, third) for row in range(KD) for third in (1, 2)])
    p.gemm("even_out", D)
    p.swiglu("moe0", MOE_CHUNKS)
    p.gemm("odd_in", ODD_W)
    p.gemm("odd_out", D)
    p.swiglu("moe1", MOE_CHUNKS)
    p.swiglu("pre0", FFN_CHUNKS)
    p.gemm("mem0", 512)
    p.gemm("a_in", A_W)
    p.rwkv()
    p.gemm("a_out", D)
    p.swiglu("post0", FFN_CHUNKS)
    p.gemm("kv", 1536)
    p.swiglu("pre1", FFN_CHUNKS)
    p.gemm("mem1", 512)
    p.gemm("b_q", D)
    p.gemm("b_out", D, 512)
    p.swiglu("post1", FFN_CHUNKS)
    return p


PL = plan()
SWIGLUS = list(PL.swi)
STAGES = {**PL.gemms, **PL.swi}
SPLITS = {"n_even": 4, "even_mix": 4, "n_moe0": 4, "n_odd": 4, "odd_mix": 4, "n_moe1": 4, "n_pre0": 4, "n_mem0": 4,
          "n_mix0": 4, "a_mix": 4, "n_post0": 4, "n_kv": 4, "n_pre1": 4, "n_mem1": 4, "n_mix1": 4, "b_mix": 2,
          "n_post1": 4}
SPLIT_BASE = {nm: sum(list(SPLITS.values())[:i]) for i, nm in enumerate(SPLITS)}
SPLIT_OF = {"even_in": "n_even", "even_out": "even_mix", "odd_in": "n_odd", "odd_out": "odd_mix", "mem0": "n_mem0",
            "a_in": "n_mix0", "a_out": "a_mix", "kv": "n_kv", "mem1": "n_mem1", "b_q": "n_mix1", "b_out": "b_mix"}

HT, XN, PROJ, ROWS, WORK = 0, 2048, 4096, 11264, 15360
POOL = 24576
NORMS = ["n_even", "n_moe0", "n_odd", "n_moe1", "n_pre0", "n_mem0", "n_mix0", "n_post0", "n_kv", "n_pre1",
         "n_mem1", "n_mix1", "n_post1"]
JOB_BASE = {"att": 0, "mem0": 16, "mem1": 24, "dil": 32}


def build(nc, a, out):
    ctx = ExitStack()
    with ctx:
        def sb(name, shape, dt=F32):
            return ctx.enter_context(nc.sbuf_tensor(name, shape, dt))

        sems = {}

        def sem(name):
            if name not in sems:
                sems[name] = ctx.enter_context(nc.semaphore(name))
            return sems[name]

        scratch_bias = nc.dram_tensor("bias_rows", [20, 512], F32, kind="Internal").ap()

        ring = sb("ring", [P, RAW * PIECE])
        w_hi = sb("w_hi", [P, RAW, PIECE], F32R)
        w_lo = sb("w_lo", [P, RAW, PIECE], F32R)
        h_hi = sb("h_hi", [P, KD, T], F32R)
        h_lo = sb("h_lo", [P, KD, T], F32R)
        hid_hi = sb("hid_hi", [P, 2, 2, HC], F32R)
        hid_lo = sb("hid_lo", [P, 2, 2, HC], F32R)
        pool = sb("pool", [P, POOL])
        x = sb("x", [P, NT, D])
        keep = sb("keep", [P, a["c_keep"].shape[1]])
        gcols = sb("gcols", [P, 13, KD])
        rcols = sb("rcols", [P, 50])
        omu = sb("omu", [P, SHIFT_TILES])
        mcols = sb("mcols", [P, 2, 4, KD])
        mgain = sb("mgain", [P, 4, KD])
        cact = sb("cact", [P, KD])
        tiny = sb("tiny", [P, 162])
        zbf = sb("zbf", [P, P], BF16)
        gains64 = sb("gains64", [P, 8, 64])
        router_w = sb("router_w", [P, KD, NE])
        router_b = sb("router_b", [P, NE])
        psum = ctx.enter_context(nc.psum_tensor("psum", [P, 8, 512], F32))

        def bank(b, n=1):
            return psum[:, b, :] if n == 1 else psum[:, b:b + n, :].rearrange("p b n -> p (b n)")

        def view(off, *dims):
            n = int(np.prod(dims))
            v = pool[:, off:off + n]
            if len(dims) == 2:
                return v.rearrange("p (a b) -> p a b", a=dims[0])
            if len(dims) == 3:
                return v.rearrange("p (a b c) -> p a b c", a=dims[0], b=dims[1])
            return v

        off = 0
        K = {}
        for nm, w in (("ident", 128), ("ones", 128), ("neg_from", 128), ("neg_ones", 128), ("chunk_incl", 128),
                      ("head_ones", 128), ("head_cols", 2), ("lower", 16)):
            K[nm] = keep[:, off:off + w]
            off += w
        ident = K["ident"]

        hT = view(HT, KD, T)
        xn = view(XN, NT, D)
        acc = view(PROJ, ADA_W)
        acc_0 = [view(PROJ, PIECE), view(ROWS, PIECE), view(ROWS + PIECE, PIECE)]
        grow = [[view(ROWS + 2048 * l + 1024 * j, D) for j in range(2)] for l in range(2)]

        def piece(n):
            s = PL.pieces[n]["slot"]
            return ring[:, s * PIECE:(s + 1) * PIECE]

        rwkv_par = ring[:, 0:2 * PIECE]

        def bc(ap, shape):
            return ap.to_broadcast(shape)

        csilu = cact
        ss = tiny[:, 0:2]
        var = tiny[:, 2:4]
        rstd = tiny[:, 4:6]
        hss = tiny[:, 8:40]
        hvar = tiny[:, 40:72]
        hrstd = tiny[:, 72:104]
        nmax = tiny[:, 104:106]
        esum = tiny[:, 106:110]
        erec = tiny[:, 6:8]
        mx = tiny[:, 110:112]
        pend = tiny[:, 112:136].rearrange("p (i c) -> p i c", c=4)
        bonus = tiny[:, 136:160]

        memx = view(ROWS, NT, D)
        NSRC = {n: (memx if n.startswith("n_mem") else x[:, :, :]) for n in NORMS}
        NGAIN = {"n_even": mgain[:, 0, :], "n_moe0": mgain[:, 1, :], "n_odd": mgain[:, 2, :],
                 "n_moe1": mgain[:, 3, :], "n_pre0": gcols[:, 4, :], "n_pre1": gcols[:, 5, :],
                 "n_mix0": gcols[:, 6, :], "n_mix1": gcols[:, 7, :], "n_post0": gcols[:, 8, :],
                 "n_post1": gcols[:, 9, :], "n_mem0": gcols[:, 10, :], "n_mem1": gcols[:, 11, :],
                 "n_kv": gcols[:, 12, :]}
        NSHIFT = {"n_even": mcols[:, 0, 0, :], "n_moe0": mcols[:, 0, 2, :], "n_odd": mcols[:, 1, 0, :],
                  "n_moe1": mcols[:, 1, 2, :]}
        XSEEN = {"n_even": 0, "n_moe0": 1, "n_odd": 2, "n_moe1": 3, "n_pre0": 4, "n_mem0": 0, "n_mix0": 5,
                 "n_post0": 6, "n_kv": 7, "n_pre1": 7, "n_mem1": 0, "n_mix1": 8, "n_post1": 9}

        proj_e = view(PROJ, NT, EVEN_W)
        decay_t = view(WORK, 4, 384)
        rope_c = view(WORK + 1536, NT, 64)
        rope_s = view(WORK + 1664, NT, 64)
        att_ban = view(WORK + 1792, 384)
        qk_t = view(WORK + 2176, 8, T)
        ret_s = view(WORK + 4224, 2, 384)
        att_p = view(WORK + 4992, 2, 768)
        att_pt = view(WORK + 6528, 768)
        anti = view(WORK + 7296, P)
        rot_a = view(WORK + 4992, 2, 512)
        rot_b = view(WORK + 6016, 2, 512)

        def bias_att(h, t):
            o = HT + 384 * h if h < 5 else ROWS + 2048 + 384 * (h - 5)
            return view(o, P) if t == 0 else view(o + P, T)

        qf = view(PROJ, KD, T)
        kf = view(PROJ + 2048, KD, T)
        v_o = view(PROJ + 4096, NT, D)
        SBW = WORK
        sb_abs = [view(SBW + 1536 * i, 384) for i in range(2)]
        sb_sp = [view(SBW + 1536 * i + 384, 384) for i in range(2)]
        sb_a = [view(SBW + 1536 * i + 768, 384) for i in range(2)]
        sb_zero = view(SBW + 3072, P)
        spread = keep[:, 0:256].bitcast(BF16)
        comb_b = view(WORK, NE, T)
        hid = [view(WORK + 4096, 2, HC), view(WORK + 4608, 2, HC)]
        comb_t = view(WORK + 5120, T)[0:NE, :]
        ada1 = view(WORK + 6144, ADA_HALF)
        rt = view(WORK + 5376, 512)
        rt_sc, comb_tok = rt[:, 0:32], rt[:, 448:480]
        mem_kt = view(ROWS + 3072, 2, T)
        mem_v = view(ROWS + 3584, NT, 256)
        mem_kv = view(WORK, NT, 512)
        q_mem_a = view(PROJ + 5120, NT, 256)
        F = view(PROJ, SHIFT_TILES, T)
        sh_tmp = [view(PROJ + 5632 + 260 * i, 260) for i in range(4)]
        W = [view(WORK + 1536 * i, 6, T) for i in range(6)]
        Wf = [view(WORK + 1536 * i, 1536) for i in range(6)]
        Fr, Fk, Fv = F[:, 0:6, :], F[:, 6:12, :], F[:, 12:18, :]
        rw_reset = view(XN, T)
        v_tok, b_tok, k_tok = (view(WORK + 1536 * i, NT, 768) for i in range(3))
        TT = view(ROWS, 6, 4, P)
        U = view(WORK + 6144, NT, 768)
        gate = view(HT, NT, 768)
        t_lt = [view(PROJ + 3072, 4, P), view(PROJ + 5632, 4, P)]
        t_t = [view(PROJ + 3584, 4, P), view(PROJ + 6144, 4, P)]
        t_x = [view(PROJ + 4096, 4, P), view(PROJ + 6656, 4, P)]
        t_lm = [view(PROJ + 4608, 4, P), view(XN, 4, P)]
        t_m = [view(PROJ + 5120, 4, P), view(XN + D, 4, P)]
        Z = view(PROJ + 3072, 768)
        SA = view(PROJ + 5632, NT, 768)
        state = view(ROWS + 3072, 6, P)
        bm = [view(PROJ + 4608, 4, P), view(PROJ + 3072, 4, P)]
        km = [view(HT + 1536, 4, P), view(PROJ + 3584, 4, P)]
        y_r = xn[:, :, 0:768]
        yc = view(PROJ + 3072, NT, 768)
        kd_t = view(PROJ, 6, T)
        v_d = view(PROJ + 1536, NT, 768)
        kd = view(WORK, NT, 768)
        q_d = view(PROJ + 3072, NT, D)
        qd_t = view(PROJ + 5120, 8, T)

        def bias_dil(g, h, t):
            o = WORK + 384 * (4 * g + h)
            return view(o, P) if t == 0 else view(o + P, T)

        def job(kind, h, t):
            half = slice(64 * (h % 2), 64 * (h % 2) + 64)
            qs = slice(P * t, P * t + P)
            if kind == "att":
                n = P * (t + 1)
                return ([dict(q=qk_t[half, h // 2, qs], k=qk_t[half, 4 + h // 2, 0:n], n=n,
                              bias=bias_att(h, t),
                              v=[proj_e[:, kt, 3072 + 64 * h:3136 + 64 * h] for kt in range(t + 1)])],
                        xn[:, t, 512 + 64 * h:576 + 64 * h])
            if kind in ("mem0", "mem1"):
                q = qk_t[half, h // 2, qs] if kind == "mem0" else qd_t[half, 6 + h // 2, qs]
                o = xn[:, t, 768 + 64 * h:832 + 64 * h] if kind == "mem0" else \
                    xn[:, t, 256 + 64 * h:320 + 64 * h]
                return ([dict(q=q, k=mem_kt[half, h // 2, :], n=T, bias=None,
                              v=[mem_v[:, kt, 64 * h:64 * h + 64] for kt in range(NT)])], o)
            n = P * (t + 1)
            segs = []
            for g in range(3):
                hh = 4 * g + h
                segs.append(dict(q=qd_t[half, hh // 2, qs], k=kd_t[half, hh // 2, 0:n], n=n,
                                 bias=bias_dil(g, h, t),
                                 v=[v_d[:, kt, 64 * hh:64 * hh + 64] for kt in range(t + 1)]))
            return segs, xn[:, t, 64 * h:64 * h + 64]

        JOBS = {"att": [("att", h, t) for h in range(8) for t in range(NT)],
                "mem0": [("mem0", h, t) for h in range(4) for t in range(NT)],
                "mem1": [("mem1", h, t) for h in range(4) for t in range(NT)],
                "dil": [("dil", h, t) for h in range(4) for t in range(NT)]}

        def gemm_dst(name, c):
            lo = 512 * c
            hi = min(lo + 512, PL.gemms[name]["width"])
            if name == "even_in":
                return "copy", proj_e[:, :, lo:hi]
            if name == "odd_in":
                if c < 2:
                    return "feat", qf[:, 4 * c:4 * c + 4, :]
                if c < 4:
                    return "feat", kf[:, 4 * c - 8:4 * c - 4, :]
                return "copy", v_o[:, :, lo - 2048:hi - 2048]
            if name in ("mem0", "mem1"):
                return "copy", mem_kv[:, :, :]
            if name == "a_in":
                return ("copy", q_mem_a[:, :, :]) if c == 5 else ("shift", c)
            if name == "kv":
                return "kv", c
            if name == "b_q":
                return "copy", q_d[:, :, lo:hi]
            if name in ("even_out", "odd_out"):
                return "resid_g", (0 if name == "even_out" else 1, c)
            return "resid", c

        KV_PARTS = {0: [(0, 512, kd, 0)], 1: [(0, 256, kd, 512), (256, 512, v_d, 0)], 2: [(0, 512, v_d, 256)]}

        X_AFTER = {"even_out": 1, "odd_out": 3, "a_out": 6, "b_out": 9}
        EVAC = []
        nact = ndve = 0
        for name, g in PL.gemms.items():
            for c in range(g["n"]):
                kind = gemm_dst(name, c)[0]
                if kind in ("copy", "feat", "kv"):
                    nact += 1
                    ndve += 1
                    EVAC.append([("ev_act", nact), ("ev_dve", ndve)])
                elif kind == "shift":
                    EVAC.append([("shift_mixed", 4 * c + 4)])
                else:
                    EVAC.append([("x_new", X_AFTER[name])] if c else
                                [("resid_first", list(X_AFTER).index(name) + 1)])

        def moved(name, c):
            return EVAC[PL.gemms[name]["base"] + c]

        block = ctx.enter_context(nc.Block())

        @block.sync
        def _(sp):
            def source(kind, name, c):
                layer = int(name[-1])
                w_in = a[f"ffn_{name[:-1]}_w_in_2"][layer].rearrange("(k p) n -> p k n", p=P)
                w_out = a[f"ffn_{name[:-1]}_w_out_2"][layer].rearrange("(k p) n -> p k n", p=P)
                return {"gate": w_in[:, :, HC * c:HC * c + HC], "up": w_in[:, :, DFF + HC * c:DFF + HC * c + HC],
                        "down": w_out[:, 2 * c:2 * c + 2, :]}[kind]

            def expert(kind, layer, e, half):
                w = a[{"gate": "exp_w_gate", "up": "exp_w_up", "down": "exp_w_down"}[kind]][layer, e]
                w = w.rearrange("(k p) n -> p k n", p=P)
                return w[:, 2 * half:2 * half + 2, :] if kind == "down" else w[:, :, HC * half:HC * half + HC]

            def load(n, src, k):
                s = PL.pieces[n]["slot"]
                sp.dma_start(piece(n).rearrange("p (k n) -> p k n", k=k), src).then_inc(sem(f"landed{s}"), 16)

            def static_piece(n):
                pc = PL.pieces[n]
                kind, what = pc["kind"], pc["what"]
                for e in pc["after"]:
                    if e is not None:
                        sp.wait_ge(sem(e[0]), e[1])
                if kind == "ada":
                    src = a["ada_w"][0].rearrange("(p t) n -> p (t n)", t=KD)
                    load(n, src[:, what * PIECE:(what + 1) * PIECE].unsqueeze(1), 1)
                elif kind == "gemm":
                    name, o = what
                    g = PL.gemms[name]
                    src = {"even_in": a["even_w_in"][0], "even_out": a["even_w_out"][0], "odd_in": a["odd_w_in"][0],
                           "odd_out": a["odd_w_out"][0], "mem0": a["mem_w_kv_2"][0], "mem1": a["mem_w_kv_2"][1],
                           "a_in": a["a_w_in_2"][0], "a_out": a["a_w_out_2"][0], "kv": a["kv_w_2"],
                           "b_q": a["b_w_q_2"][0], "b_out": a["b_w_out_2"][0]}[name]
                    load(n, src.rearrange("(k p) n -> p k n", p=P)[:, :, o:o + g["cols"]], PIECE // g["cols"])
                elif kind == "rwkv":
                    for m, (o, src) in enumerate((
                            (0, a["a_w_up_2"][0]), (0, a["a_a_up_2"][0]), (768, a["a_g_up_2"][0]),
                            (1536, a["a_lnx_g_2"][0].partition_broadcast(P)),
                            (2304, a["a_lnx_b_2"][0].partition_broadcast(P)), (3072, a["c_rw_masks"]))):
                        rows = rwkv_par[64:P] if m == 1 else rwkv_par[0:src.shape[0]]
                        sp.dma_start(rows[:, o:o + src.shape[1]], src).then_inc(sem("rwkv_in"), 16)
                else:
                    name, c = what
                    src = expert(kind, int(name[-1]), c // 2, c % 2) if name.startswith("moe") else \
                        source(kind, name, c)
                    load(n, src, 2 if kind == "down" else KD)

            ada_1 = a["ada_w"][1].rearrange("(p t) (h n) -> p t h n", t=KD, h=2)

            def ada_half(t, h, before):
                src = ada_1[:, t, h, :]
                sp.wait_ge(sem("ada_used"), ADA_PIECES + before)
                sp.dma_start(ada1, src).then_inc(sem("ada1_landed"), 16)

            def moe(name):
                s = PL.swi[name]
                layer, first = int(name[-1]), s["first"]
                loops = (s["n"] - 1) // 4
                for n in range(first, first + 14):
                    static_piece(n)
                if layer == 0:
                    sp.wait_ge(sem("moe_ready"), 1)
                    ada_half(0, 0, 0)
                with sp.Fori(0, loops - 1) as i:
                    for q in range(4):
                        r = 2 + 3 * q
                        for j, (kind, e, half) in enumerate((("gate", 2 * i + 2 + (q + 1) // 2, (q + 1) % 2),
                                                             ("up", 2 * i + 2 + (q + 1) // 2, (q + 1) % 2),
                                                             ("down", 2 * (i + 1) + q // 2, q % 2))):
                            src = expert(kind, layer, e, half)
                            sp.wait_ge(sem("w_lo"), s["split"] + 12 * i + 12 + r + j - 2)
                            load(first + r + j, src, 2 if kind == "down" else KD)
                        if layer == 0 and q == 0:
                            ada_half(i, 1, 2 * i + 1)
                        if layer == 0 and q == 2:
                            ada_half(i + 1, 0, 2 * i + 2)
                for n in range(first + 12 * loops + 2, first + 3 * s["n"]):
                    static_piece(n)
                    at = n - first - 12 * loops - 2
                    if layer == 0 and at == 2:
                        ada_half(loops - 1, 1, 2 * loops - 1)
                    if layer == 0 and at == 8:
                        ada_half(loops, 0, 2 * loops)
                if layer == 0:
                    ada_half(loops, 1, 2 * loops + 1)

            n = 0
            while n < len(PL.pieces):
                kind, what = PL.pieces[n]["kind"], PL.pieces[n]["what"]
                if kind == "gate" and what[0].startswith("moe"):
                    moe(what[0])
                    n += 3 * PL.swi[what[0]]["n"]
                else:
                    static_piece(n)
                    n += 1
            sp.wait_ge(sem("x_new"), 10)
            sp.dma_start(out.rearrange("a (t p) d -> p (a t) d", p=P), x[:, :, :]).then_inc(sem("stored"), 16)
            sp.wait_ge(sem("stored"), 16)

        @block.gpsimd
        def _(pl):
            pl.dma_start(cact[:, :], a["c"].rearrange("a (p t) -> p (a t)", t=KD)).then_inc(sem("c_in"), 16)
            for part in acc_0:
                pl.memset(part, 0.0).then_inc(sem("acc_zero"), 1)
            pl.wait_ge(sem("acc_zero"), 3)
            for third, part in enumerate(acc_0):
                pl.dma_start(part[0:1, :], a["ada_b"][0:1, third * PIECE:(third + 1) * PIECE])\
                  .then_inc(sem("ada_b_in"), 16)
            pl.dma_start(x[:, :, :], a["x"].rearrange("a (t p) d -> p (a t) d", p=P)).then_inc(sem("x_in"), 16)
            pl.dma_start(keep[:, :], a["c_keep"]).then_inc(sem("keep_in"), 16)
            pl.dma_start(gcols[:, :, :], a["gain_cols"].rearrange("p (n k) -> p n k", k=KD)).then_inc(sem("cols_in"), 16)
            pl.dma_start(rcols[:, :], a["rwkv_cols"]).then_inc(sem("cols_in"), 16)
            pl.dma_start(gains64[:, :, :], a["gains64"].partition_broadcast(P).rearrange("p (n d) -> p n d", d=64))\
              .then_inc(sem("cols_in"), 16)
            pl.dma_start(router_b[:, :], a["router_b"].partition_broadcast(P)).then_inc(sem("cols_in"), 16)
            pl.dma_start(router_w[:, :, :], a["router_w"].rearrange("(k p) n -> p k n", p=P)).then_inc(sem("cols_in"), 16)
            pl.memset(zbf[:, :], 0.0).then_inc(sem("zbf_zero"), 1)
            hot = view(WORK + 2176, 4, 512)
            pl.dma_start(hot[:, 0:2, :], a["c_hot_rel"].rearrange("(k p) n -> p k n", p=P)).then_inc(sem("hot_in"), 16)
            pl.dma_start(hot[0:32, 2, :], a["c_hot_t5"]).then_inc(sem("hot_in"), 16)
            pl.dma_start(hot[0:12, 3, :], a["c_ban"]).then_inc(sem("hot_in"), 16)
            pl.dma_start(view(WORK + 4224, 2, 8), a["rel_t"].rearrange("(k p) n -> p k n", p=P)).then_inc(sem("hot_in"), 16)
            pl.dma_start(view(WORK + 4240, 12)[0:32, :], a["rel_bias_2"]).then_inc(sem("hot_in"), 16)
            pl.dma_start(view(WORK, 2176), a["c_even"]).then_inc(sem("even_in"), 16)
            pl.wait_ge(sem("bias_rows"), 2)
            pl.dma_start(scratch_bias[0:8, :], view(WORK + 4256, 512)[0:8, :]).then_inc(sem("bias_out"), 16)
            pl.dma_start(scratch_bias[8:20, :], view(WORK + 4768, 512)[0:12, :]).then_inc(sem("bias_out"), 16)
            pl.wait_ge(sem("bias_out"), 32)

            def toeplitz(dst, row, t):
                n = P * (t + 1)
                src = bass.AP(tensor=scratch_bias.tensor, offset=row * 512 + 128 - P * t, ap=[[1, P], [1, n]])
                return pl.dma_start(dst, src)

            pl.wait_ge(sem("w_used"), PL.done_at[PL.gemms["even_in"]["base"] + 6])
            pl.wait_ge(sem("mod_rows"), 1)
            for h in range(8):
                for t in range(NT):
                    toeplitz(bias_att(h, t), h, t).then_inc(sem("bias_in"), 16)
            pl.dma_start(anti, a["c_anti"]).then_inc(sem("anti_in"), 16)
            pl.wait_ge(sem("bias_in"), 256)
            pl.wait_ge(sem("even_in"), 16)
            for h in range(8):
                for t in range(NT):
                    b_ = bias_att(h, t)
                    pl.tensor_tensor(b_, b_, att_ban[:, 0:P] if t == 0 else att_ban[:, P:384], ALU.add)\
                      .then_inc(sem("bias_banned"), 1)
            pl.wait_ge(sem("x_new"), 1)
            pl.memset(acc, 0.0).then_inc(sem("acc_zero"), 1)
            pl.wait_ge(sem("acc_zero"), 4)
            pl.dma_start(acc[0:1, :], a["ada_b"][1:2, :]).then_inc(sem("ada_b_in"), 16)
            pl.wait_ge(sem("x_new"), 4)
            pl.dma_start(memx, a["mem_2"].rearrange("a (t p) d -> p (a t) d", p=P)).then_inc(sem("mem_in"), 16)
            pl.wait_ge(sem("norm_T"), 4 * (NORMS.index("n_mix0") + 1))
            pl.wait_ge(sem("heads_ok"), 3)
            pl.dma_start(rw_reset, a["c_reset"]).then_inc(sem("reset_in"), 16)
            pl.wait_ge(sem("x_new"), 7)
            pl.dma_start(memx, a["mem_2"].rearrange("a (t p) d -> p (a t) d", p=P)).then_inc(sem("mem_in"), 16)
            pl.wait_ge(sem("x_new"), 8)
            pl.wait_ge(sem("heads_ok"), 5)
            pl.wait_ge(sem("w_used"), PL.done_at[PL.gemms["b_q"]["base"]])
            for g in range(3):
                for h in range(4):
                    for t in range(NT):
                        toeplitz(bias_dil(g, h, t), 8 + 4 * g + h, t).then_inc(sem("bias2_in"), 16)
            pl.dma_start(anti, a["c_anti"]).then_inc(sem("bias2_in"), 16)

        def flat(v):
            return v if len(v.shape) == 2 else v.rearrange("p a b -> p (a b)")

        def blocks_tok(src, tiles, dst):
            s = [src(j, t) for j in range(tiles) for t in range(NT)]
            return [(s[4 * b:4 * b + 4], dst(2 * b, min(2, tiles - 2 * b))) for b in range(-(-tiles // 2))]

        def blocks_feat(srcv, dst):
            s = [srcv[:, i, P * t:P * t + P] for t in range(NT) for i in range(6)]
            return [(s[4 * b:4 * b + 4], dst[:, 512 * b:512 * b + 512]) for b in range(3)]

        def into(v):
            return lambda j, n: flat(v[:, j:j + n, :])

        TRS = {
            "ret_qk": blocks_tok(lambda j, t: proj_e[:, t, P * j:P * j + P], 8, into(qk_t)),
            "att_qk": blocks_tok(lambda j, t: proj_e[:, t, 2048 + P * j:2048 + P * j + P], 8, into(qk_t)),
            "even_mix": blocks_tok(lambda j, t: xn[:, t, P * j:P * j + P], 8, into(hT)),
            "odd_mix": blocks_tok(lambda j, t: xn[:, t, P * j:P * j + P], 8, into(hT)),
            "mem0_k": blocks_tok(lambda j, t: mem_kv[:, t, P * j:P * j + P], 2, into(mem_kt)),
            "mem0_q": blocks_tok(lambda j, t: q_mem_a[:, t, P * j:P * j + P], 2, into(qk_t)),
            "rw_v": blocks_feat(Fv, flat(v_tok)),
            "rw_b": blocks_feat(W[5], flat(b_tok)),
            "rw_k": blocks_feat(Fk, flat(k_tok)),
            "a_mix": blocks_tok(lambda j, t: xn[:, t, P * j:P * j + P], 8, into(hT)),
            "kd": blocks_tok(lambda j, t: kd[:, t, P * j:P * j + P], 6, into(kd_t)),
            "mem1_k": blocks_tok(lambda j, t: mem_kv[:, t, P * j:P * j + P], 2, into(mem_kt)),
            "dil_q": blocks_tok(lambda j, t: q_d[:, t, P * j:P * j + P], 8, into(qd_t)),
            "b_mix": blocks_tok(lambda j, t: xn[:, t, P * j:P * j + P], 4, into(hT)),
        }
        TR_BASE, n = {}, 0
        for nm, bl in TRS.items():
            TR_BASE[nm] = n
            n += len(bl)

        def tr_counts(nm):
            e = TR_BASE[nm] + len(TRS[nm])
            return (e + 1) // 2, e // 2

        @block.tensor
        def _(pe):
            def transposes(nm, *ready):
                for r in ready:
                    pe.wait_ge(sem(r[0]), r[1])
                for i, (srcs, _) in enumerate(TRS[nm]):
                    B = TR_BASE[nm] + i
                    e = B - 4
                    if e >= 0:
                        pe.wait_ge(sem("tr_act" if e % 2 == 0 else "tr_dve"), e // 2 + 1)
                    for k, src in enumerate(srcs):
                        m = pe.transpose(bank(4 + B % 4)[:, P * k:P * k + P], src, ident)
                    m.then_inc(sem("tr_done"), 1)

            def transposed(nm):
                na, nd = tr_counts(nm)
                if na > 0:
                    pe.wait_ge(sem("tr_act"), na)
                if nd > 0:
                    pe.wait_ge(sem("tr_dve"), nd)

            def norm(nm):
                n = NORMS.index(nm)
                pe.wait_ge(sem("norm_xn"), 2 * (n + 1))
                for b in range(4):
                    for k in range(2):
                        for t in range(NT):
                            j = 2 * b + k
                            m = pe.transpose(bank(b)[:, T * k + P * t:T * k + P * t + P],
                                             xn[:, t, P * j:P * j + P], ident)
                    m.then_inc(sem("norm_T"), 1)
                if nm == "n_even":
                    pe.wait_ge(sem("ada_used"), KD)
                    modulation(0, (0, 1), ())
                pe.wait_ge(sem("norm_act"), 4 * (n + 1))
                pe.wait_ge(sem("norm_dve"), 4 * (n + 1))

            def gemm(nm):
                g = PL.gemms[nm]
                split = SPLIT_OF[nm]
                pe.wait_ge(sem("h_split_lo"), SPLIT_BASE[split] + SPLITS[split])
                for c in range(g["n"]):
                    G = g["base"] + c
                    kind = gemm_dst(nm, c)[0]
                    if G >= 4:
                        for e in EVAC[G - 4]:
                            pe.wait_ge(sem(e[0]), e[1])
                    pair, cols = 2 * (G % 4), g["cols"]
                    ks = PIECE // cols
                    for o in range(512 * c, min(512 * c + 512, g["width"]), cols):
                        n = g["split"] + o // cols
                        pe.wait_ge(sem("w_lo"), n + 1)
                        wh, wl = (w[:, n % 3, :].rearrange("p (k n) -> p k n", k=ks) for w in (w_hi, w_lo))
                        lo = o - 512 * c
                        for f in range(2):
                            fs = slice(P * f, P * f + P)
                            dst = bank(pair + lo // 256)[:, T * f:T * f + T] if kind in ("feat", "shift") else \
                                bank(pair + f)[:, lo:lo + cols]
                            for k in range(ks):
                                for q, (wt, ht) in enumerate(((wh, h_hi), (wh, h_lo), (wl, h_hi))):
                                    lhs, rhs = (wt[:, k, fs], ht[:, k, :]) if kind in ("feat", "shift") else \
                                        (ht[:, k, fs], wt[:, k, :])
                                    m = pe.matmul(dst, lhs, rhs, start=k == 0 and q == 0, stop=k == ks - 1 and q == 2)
                        m.then_inc(sem("w_used"), 1)

            def swiglu(nm):
                s = PL.swi[nm]
                G0, U0 = s["base"], s["split"]

                def zero_products(start):
                    for b in range(4):
                        m = pe.matmul(bank(b), zbf[:, :], spread, start=start, stop=not start, skip_group_check=True)
                    if not start:
                        m.then_inc(sem("sums_done"), 1)

                def gate_up(c, q, n, j, r):
                    pe.wait_ge(sem("w_lo"), U0 + n + 1)
                    pe.wait_ge(sem("silu_done" if j == 0 else "hid_ready"), max(G0 + c, 1) if isinstance(c, int) else G0 + c)
                    wh, wl = (w[:, (U0 + r) % 3, :].rearrange("p (k n) -> p k n", k=KD) for w in (w_hi, w_lo))
                    for f in range(2):
                        for k in range(KD):
                            o, fs = bank(4 + 2 * (q % 2) + j)[:, T * f:T * f + T], slice(P * f, P * f + P)
                            pe.matmul(o, wh[:, k, fs], h_hi[:, k, :], start=k == 0, stop=False)
                            pe.matmul(o, wh[:, k, fs], h_lo[:, k, :], start=False, stop=False)
                            m = pe.matmul(o, wl[:, k, fs], h_hi[:, k, :], start=False, stop=k == KD - 1)
                    m.then_inc(sem("w_used"), 1)

                def down(c, q, n, r):
                    pe.wait_ge(sem("w_lo"), U0 + n + 1)
                    pe.wait_ge(sem("hid_ready"), G0 + c + 2)
                    wh, wl = (w[:, (U0 + r) % 3, :].rearrange("p (k n) -> p k n", n=D) for w in (w_hi, w_lo))
                    hh, hl = hid_hi[:, q % 2], hid_lo[:, q % 2]
                    for f in range(2):
                        for t in range(NT):
                            ts = slice(P * t, P * t + P)
                            for h in range(2):
                                o, hs = bank(2 * t + h), slice(512 * h, 512 * h + 512)
                                for lhs, rhs in ((hh, wh), (hh, wl), (hl, wh)):
                                    m = pe.matmul(o, lhs[:, f, ts], rhs[:, f, hs], start=False, stop=False,
                                                  skip_group_check=True)
                    m.then_inc(sem("w_used"), 1)

                if XSEEN["n_" + nm] > 0:
                    pe.wait_ge(sem("x_new"), XSEEN["n_" + nm])
                zero_products(True)
                pe.wait_ge(sem("h_split_lo"), SPLIT_BASE["n_" + nm] + 4)
                gate_up(0, 0, 0, 0, 0)
                gate_up(0, 0, 1, 1, 1)
                loops = (s["n"] - 1) // 4
                with pe.Fori(0, loops) as i:
                    for q in range(4):
                        gate_up(4 * i + q + 1, (q + 1) % 4, 12 * i + 3 * q + 2, 0, 2)
                        gate_up(4 * i + q + 1, (q + 1) % 4, 12 * i + 3 * q + 3, 1, 0)
                        down(4 * i + q, q, 12 * i + 3 * q + 4, 1)
                for c in range(4 * loops + 1, s["n"]):
                    gate_up(c, c % 4, 3 * c - 1, 0, 2)
                    gate_up(c, c % 4, 3 * c, 1, 0)
                    down(c - 1, (c - 1) % 4, 3 * c + 1, 1)
                last = s["n"] - 1
                down(last, last % 4, 3 * last + 2, 2)
                zero_products(False)

            def attention(kind, *ready):
                for r in ready:
                    pe.wait_ge(sem(r[0]), r[1])
                jobs, base = JOBS[kind], JOB_BASE[kind]
                for j in range(len(jobs) + 2):
                    J = base + j
                    if j < len(jobs):
                        if J > 1:
                            pe.wait_ge(sem("att_exp"), J - 1)
                        lg = psum[:, 2 * (j % 2):2 * (j % 2) + 2, :].rearrange("p b n -> p (b n)")
                        for k, sg in enumerate(job(*jobs[j])[0]):
                            o = lg[:, T * k:T * k + sg["n"]]
                            if sg["bias"] is not None:
                                pe.matmul(o, anti, sg["bias"], start=True, stop=False)
                            m = pe.matmul(o, sg["q"], sg["k"], start=sg["bias"] is None, stop=True)
                        m.then_inc(sem("att_scores"), 1)
                    if 0 <= j - 2:
                        J2 = J - 2
                        pe.wait_ge(sem("att_pts"), J2 + 1)
                        if J2 > 1:
                            pe.wait_ge(sem("att_o"), J2 - 1)
                        vs = [v for sg in job(*jobs[j - 2])[0] for v in sg["v"]]
                        for k, v in enumerate(vs):
                            m = pe.matmul(bank(6 + j % 2)[:, 0:64], att_pt[:, P * k:P * k + P], v,
                                          start=k == 0, stop=k == len(vs) - 1)
                        m.then_inc(sem("att_pv"), 1)
                    if 0 <= j - 1 < len(jobs):
                        J1 = J - 1
                        pe.wait_ge(sem("att_exp"), J1 + 1)
                        if J1 > 0:
                            pe.wait_ge(sem("att_pts"), J1)
                        k = 0
                        for sg_i, sg in enumerate(job(*jobs[j - 1])[0]):
                            for kt in range(len(sg["v"])):
                                o = T * sg_i + P * kt
                                m = pe.transpose(bank(4, 2)[:, P * k:P * k + P],
                                                 att_p[:, (j - 1) % 2, o:o + P], ident)
                                k += 1
                        m.then_inc(sem("att_pt"), 1)

            def modulation(layer, columns, rows):
                def sums(col, n):
                    third, o = col // PIECE, col % PIECE
                    return acc_0[third][:, o:o + n] if layer == 0 else acc[:, col:col + n]

                for j in columns:
                    for k in range(KD):
                        m = pe.matmul(bank(4)[:, KD * j + k:KD * j + k + 1], sums(D * (0, 1, 3, 4)[j] + P * k, P),
                                      K["ones"][:, 0:1], start=True, stop=True)
                m.then_inc(sem("mod_cols"), 1)
                for j in rows:
                    for h in range(2):
                        m = pe.matmul(bank(2 * j + h), K["ones"], sums(D * (2, 5)[j] + 512 * h, 512),
                                      start=True, stop=True)
                if rows:
                    m.then_inc(sem("mod_rows"), 1)

            pe.wait_ge(sem("keep_in"), 16)
            pe.wait_ge(sem("hot_in"), 80)
            hot = view(WORK + 2176, 4, 512)
            for k in range(2):
                m = pe.matmul(bank(6)[0:8, :], view(WORK + 4224, 2, 8)[:, k, :], hot[:, k, :], start=k == 0, stop=k == 1)
            m.then_inc(sem("bias_ps"), 1)
            pe.matmul(bank(7)[0:12, :], view(WORK + 4240, 12)[0:32, :], hot[0:32, 2, :], start=True, stop=True)\
              .then_inc(sem("bias_ps"), 1)
            norm("n_even")
            pe.wait_ge(sem("mod_moved"), 1)
            gemm("even_in")
            pe.wait_ge(sem("ada_used"), ADA_PIECES)
            for e in moved("even_in", 6) + moved("even_in", 5) + moved("even_in", 4) + moved("even_in", 3):
                pe.wait_ge(sem(e[0]), e[1])
            modulation(0, (2, 3), (0, 1))
            pe.wait_ge(sem("rotated"), 1)
            pe.wait_ge(sem("mod_moved"), 2)
            pe.wait_ge(sem("mod_rows_in"), 2)
            transposes("ret_qk")
            transposed("ret_qk")
            for h in range(5):
                if h < 4:
                    if h > 1:
                        pe.wait_ge(sem("ret_decayed"), h - 1)
                    o = bank(h % 2)
                    pe.matmul(o[:, 0:T], qk_t[:, 4 + h, 0:P], qk_t[:, h, :], start=True, stop=True)
                    pe.matmul(o[:, T:T + P], qk_t[:, 4 + h, P:T], qk_t[:, h, P:T], start=True, stop=True)\
                      .then_inc(sem("ret_scores"), 1)
                if h >= 1:
                    g = h - 1
                    pe.wait_ge(sem("ret_decayed"), g + 1)
                    if g > 1:
                        pe.wait_ge(sem("ret_moved"), g - 1)
                    o = bank(2 + g % 2)
                    v = proj_e[:, :, D + P * g:D + P * g + P]
                    s = ret_s[:, g % 2, :]
                    pe.matmul(o[:, 0:P], s[:, 0:P], v[:, 0, :], start=True, stop=True)
                    pe.matmul(o[:, P:T], s[:, P:T], v[:, 0, :], start=True, stop=False)
                    pe.matmul(o[:, P:T], s[:, T:T + P], v[:, 1, :], start=False, stop=True)\
                      .then_inc(sem("ret_pv"), 1)
            transposes("att_qk", ("heads_ok", 1))
            transposed("att_qk")
            attention("att", ("bias_banned", 16), ("anti_in", 16))
            transposes("even_mix", ("att_o", 16), ("even_mixed", 1))
            transposed("even_mix")
            gemm("even_out")

            def router(layer):
                pe.wait_ge(sem("x_new"), 1 + 2 * layer)
                for t in range(NT):
                    for k in range(KD):
                        m = pe.matmul(bank(4)[:, NE * t:NE * t + NE], hT[:, k, P * t:P * t + P], router_w[:, k, :],
                                      start=k == 0, stop=k == KD - 1)
                m.then_inc(sem("router_ps"), 1)
                pe.wait_ge(sem("comb_tok"), layer + 1)
                for t in range(NT):
                    m = pe.transpose(bank(5)[0:NE, P * t:P * t + P], comb_tok[:, NE * t:NE * t + NE], ident)
                m.then_inc(sem("comb_T_ps"), 1)
                pe.wait_ge(sem("comb_T"), layer + 1)
                for e in range(NE):
                    m = pe.matmul(bank(e // 2)[:, T * (e % 2):T * (e % 2) + T],
                                  bc(ident[0:NE, e:e + 1], [NE, P]), comb_t, start=True, stop=True)
                    if e % 2:
                        m.then_inc(sem("comb_ps"), 1)
                pe.wait_ge(sem("comb_act"), 4 * (layer + 1))
                pe.wait_ge(sem("comb_dve"), 4 * (layer + 1))

            norm("n_moe0")
            router(0)
            swiglu("moe0")
            pe.wait_ge(sem("ada_used"), ADA_PIECES + ADA_HALVES)
            pe.wait_ge(sem("x_new"), 2)
            modulation(1, (0, 1, 2, 3), (0, 1))
            norm("n_odd")
            gemm("odd_in")
            for e in moved("odd_in", 5):
                pe.wait_ge(sem(e[0]), e[1])
            for s_ in range(18):
                if s_ < 16:
                    h = s_
                    half = slice(64 * (h % 2), 64 * (h % 2) + 64)
                    kk, qq = kf[half, h // 2, :], qf[half, h // 2, :]
                    if h > 1:
                        pe.wait_ge(sem("sb_soft"), h - 1)
                    if h > 1:
                        pe.wait_ge(sem("sb_exp"), h - 1)
                    for bk in (h % 2, 2 + h % 2):
                        last = bk >= 2
                        pe.matmul(bank(bk)[:, 0:T], kk[:, 0:P], qq[:, 0:T], start=True, stop=not last,
                                  skip_group_check=True)
                        m = pe.matmul(bank(bk)[:, T:T + P], kk[:, P:T], qq[:, P:T], start=not last, stop=not last,
                                      skip_group_check=True)
                        if not last:
                            m.then_inc(sem("sb_z"), 1)
                if 1 <= s_ <= 16:
                    h = s_ - 1
                    pe.wait_ge(sem("sb_masked"), h + 1)
                    o, sp_ = bank(2 + h % 2), sb_sp[h % 2]
                    pe.matmul(o[:, 0:P], K["neg_from"], sp_[:, 0:P], start=False, stop=False, skip_group_check=True)
                    pe.matmul(o[:, P:T], K["neg_from"], sp_[:, P:T], start=False, stop=False, skip_group_check=True)
                    pe.matmul(o[:, P:T], K["neg_ones"], sp_[:, T:T + P], start=False, stop=False,
                              skip_group_check=True)
                    pe.matmul(o[:, T:T + P], K["neg_from"], sp_[:, T:T + P], start=False, stop=True,
                              skip_group_check=True).then_inc(sem("sb_sums"), 1)
                if s_ >= 2:
                    h = s_ - 2
                    pe.wait_ge(sem("sb_weights"), h + 1)
                    if h > 1:
                        pe.wait_ge(sem("sb_out"), h - 1)
                    o, av = bank(4 + h % 2), sb_a[h % 2]
                    v = v_o[:, :, 64 * h:64 * h + 64]
                    pe.matmul(o[:, 0:64], av[:, 0:P], v[:, 0, :], start=True, stop=True)
                    pe.matmul(o[:, 64:128], av[:, P:T], v[:, 0, :], start=True, stop=False)
                    pe.matmul(o[:, 64:128], av[:, T:T + P], v[:, 1, :], start=False, stop=True)\
                      .then_inc(sem("sb_pv"), 1)
            transposes("odd_mix", ("sb_out", 16))
            transposed("odd_mix")
            gemm("odd_out")
            norm("n_moe1")
            router(1)
            swiglu("moe1")
            norm("n_pre0")
            swiglu("pre0")
            norm("n_mem0")
            gemm("mem0")
            transposes("mem0_k", ("heads_ok", 2))
            norm("n_mix0")
            gemm("a_in")
            pe.wait_ge(sem("shift_mixed"), SHIFT_TILES)
            transposes("mem0_q", ("heads_ok", 3))
            transposed("mem0_q")
            attention("mem0")
            pe.wait_ge(sem("att_o"), 24)
            pe.wait_ge(sem("rwkv_in"), 96)
            par = rwkv_par
            pe.wait_ge(sem("rw_low"), 2)
            for i in range(6):
                m = pe.matmul(bank(i // 2)[:, T * (i % 2):T * (i % 2) + T], par[0:64, P * i:P * i + P],
                              F[0:64, 18, :], start=True, stop=True)
            m.then_inc(sem("rw_w_ps"), 1)
            for i in range(6):
                m = pe.matmul(bank(3 + i // 2)[:, T * (i % 2):T * (i % 2) + T], par[64:P, P * i:P * i + P],
                              F[64:P, 18, :], start=True, stop=True)
            m.then_inc(sem("rw_a_ps"), 1)
            pe.wait_ge(sem("rw_sig"), 1)
            for n in range(6):
                t, s = n // 3, n % 3
                m = pe.matmul(bank((6 + n // 2) % 8)[:, T * (n % 2):T * (n % 2) + T], F[:, 19, P * t:P * t + P],
                              par[:, 768 + T * s:768 + T * s + T], start=True, stop=True)
            m.then_inc(sem("rw_g_ps"), 1)
            pe.wait_ge(sem("rw_sq"), 1)
            pe.wait_ge(sem("rw_sig"), 2)
            for i in range(6):
                m = pe.matmul(bank(3 + i // 2)[:, T * (i % 2):T * (i % 2) + T], K["head_ones"], W[4][:, i, :],
                              start=True, stop=True)
            m.then_inc(sem("rw_ss_ps"), 1)
            pe.wait_ge(sem("rw_rk"), 1)
            for t in range(NT):
                for i in range(6):
                    m = pe.matmul(bank(1)[:, 12 * t + 2 * i:12 * t + 2 * i + 2], W[4][:, i, P * t:P * t + P],
                                  K["head_cols"], start=True, stop=True)
            m.then_inc(sem("rw_bonus_ps"), 1)
            pe.wait_ge(sem("rw_gate"), 1)
            pe.wait_ge(sem("rw_ss"), 1)
            pe.wait_ge(sem("rw_bonus"), 1)
            transposes("rw_v", ("rw_scaled", 1))
            transposes("rw_b")
            transposes("rw_k")
            transposed("rw_k")
            halves = [slice(64 * e, 64 * e + 64) for e in range(2)]
            for g in range(3):
                for s in range(2):
                    i = 2 * g + s
                    if g > 0:
                        pe.wait_ge(sem("rw_t"), i - 1)
                        pe.wait_ge(sem("rw_u"), i - 1)
                    for e in range(2):
                        for t in range(NT):
                            tk = slice(P * t, P * t + P)
                            bT, kkT, kT = W[5][halves[e], i, tk], W[3][halves[e], i, tk], Fk[halves[e], i, tk]
                            pe.matmul(bank(3 * s + e)[:, P * t:P * t + P], bT, kkT, start=True, stop=True)
                            pe.matmul(bank(3 * s + e)[:, T + P * t:T + P * t + P], kkT, bT, start=True, stop=True)
                            m = pe.matmul(bank((3 * s + 2, 6 + s)[e])[:, P * t:P * t + P], kT, kkT, start=True, stop=True)
                    m.then_inc(sem("rw_l_ps"), 1)
                for l in range(5):
                    n = 10 * g + 2 * l
                    for s in range(2):
                        pe.wait_ge(sem("rw_lm"), n + s + 1)
                        for m4 in range(4):
                            m = pe.matmul(bank(3 * s)[:, P * m4:P * m4 + P], t_lm[s][:, m4, :], t_t[s][:, m4, :],
                                          start=True, stop=True)
                        m.then_inc(sem("rw_x_ps"), 1)
                    for s in range(2):
                        pe.wait_ge(sem("rw_x"), n + s + 1)
                        if l == 0:
                            pe.wait_ge(sem("rw_m"), 2 * g + s + 1)
                        for m4 in range(4):
                            cols = slice(P * m4, P * m4 + P)
                            if l < 4:
                                pe.matmul(bank(3 * s + 1)[:, cols], TT[:, 2 * g + s, m4, :], t_x[s][:, m4, :],
                                          start=True, stop=True)
                            m = pe.matmul(bank(3 * s + 2)[:, cols], t_x[s][:, m4, :], TT[:, 2 * g + s, m4, :],
                                          start=True, stop=True)
                        m.then_inc(sem("rw_tx_ps"), 1)
                    if l == 0:
                        for s in range(2):
                            i = 2 * g + s
                            for m4 in range(4):
                                m = pe.matmul(bank(6 + s)[:, P * m4:P * m4 + P], t_m[s][:, m4, :],
                                              v_tok[:, m4 % 2, P * i:P * i + P], start=True, stop=True)
                            m.then_inc(sem("rw_u_ps"), 1)
            pe.wait_ge(sem("rw_u"), 6)
            for c in range(4):
                t, q0 = c // 2, 64 * (c % 2)
                pe.wait_ge(sem("rw_state"), c + 1)
                if c > 0:
                    pe.wait_ge(sem("rw_y"), c)
                for i in range(6):
                    m = pe.matmul(bank(0, 2)[:, P * i:P * i + P], W[3][:, i, P * t:P * t + P], state[:, i, :],
                                  start=True, stop=True)
                m.then_inc(sem("rw_z_ps"), 1)
                for i in range(6):
                    m = pe.matmul(bank(2, 2)[:, P * i:P * i + P], Fr[:, i, P * t:P * t + P], state[:, i, :],
                                  start=True, stop=True)
                m.then_inc(sem("rw_y_ps"), 1)
                pe.wait_ge(sem("rw_z"), c + 1)
                for h in range(12):
                    m = pe.matmul(bank(4, 2)[:, 64 * h:64 * h + 64], TT[:, h // 2, 2 * (h % 2) + t, :],
                                  Z[:, 64 * h:64 * h + 64], start=True, stop=True)
                m.then_inc(sem("rw_sa_ps"), 1)
                pe.wait_ge(sem("rw_sa"), c + 1)
                rows = slice(q0, q0 + 64)
                for i in range(6):
                    cols = slice(P * i, P * i + P)
                    o = bank(6, 2)[:, cols]
                    pe.matmul(o, b_tok[rows, t, cols], SA[rows, t, cols], start=True, stop=False)
                    m = pe.matmul(o, k_tok[rows, t, cols], v_tok[rows, t, cols], start=False, stop=True)
                m.then_inc(sem("rw_new_ps"), 1)
            pe.wait_ge(sem("rw_y"), 4)
            pe.wait_ge(sem("rw_z"), 4)
            for i in range(7):
                if i < 6:
                    if i > 1:
                        pe.wait_ge(sem("rw_bk"), i - 1)
                    for e in range(2):
                        half = slice(64 * e, 64 * e + 64)
                        for t in range(NT):
                            tk, o = slice(P * t, P * t + P), bank(2 * (i % 2) + e)
                            pe.matmul(o[:, P * t:P * t + P], W[5][half, i, tk], Fr[half, i, tk], start=True, stop=True)
                            m = pe.matmul(o[:, T + P * t:T + P * t + P], Fk[half, i, tk], Fr[half, i, tk],
                                          start=True, stop=True)
                    m.then_inc(sem("rw_bk_ps"), 1)
                if i >= 1:
                    i1 = i - 1
                    pe.wait_ge(sem("rw_bk"), i1 + 1)
                    if i1 > 1:
                        pe.wait_ge(sem("rw_yadd"), i1 - 1)
                    pair = slice(P * i1, P * i1 + P)
                    for m4 in range(4):
                        o = bank(4 + i1 % 2)[:, P * m4:P * m4 + P]
                        pe.matmul(o, bm[i1 % 2][:, m4, :], SA[:, m4 % 2, pair], start=True, stop=False)
                        m = pe.matmul(o, km[i1 % 2][:, m4, :], v_tok[:, m4 % 2, pair], start=False, stop=True)
                    m.then_inc(sem("rw_g2_ps"), 1)
            transposes("a_mix", ("rw_out", 1))
            transposed("a_mix")
            gemm("a_out")
            norm("n_post0")
            swiglu("post0")
            norm("n_kv")
            gemm("kv")
            transposes("kd", ("heads_ok", 4))
            norm("n_pre1")
            swiglu("pre1")
            norm("n_mem1")
            gemm("mem1")
            transposes("mem1_k", ("heads_ok", 5))
            norm("n_mix1")
            gemm("b_q")
            transposes("dil_q", ("heads_ok", 6))
            transposed("dil_q")
            attention("mem1")
            attention("dil", ("bias2_in", 25 * 16))
            transposes("b_mix", ("att_o", 40))
            transposed("b_mix")
            gemm("b_out")
            norm("n_post1")
            swiglu("post1")

        @block.scalar
        def _(act):
            done = [0]

            def step(ins):
                done[0] += 1
                ins.then_inc(sem("act_step"), 1)
                act.wait_ge(sem("act_step"), done[0])

            def norm(nm):
                n = NORMS.index(nm)
                if nm == "n_even":
                    act.wait_ge(sem("x_in"), 16)
                elif nm == "n_mem0":
                    act.wait_ge(sem("mem_in"), 16)
                elif nm == "n_mem1":
                    act.wait_ge(sem("mem_in"), 32)
                if XSEEN[nm] > 0:
                    act.wait_ge(sem("x_new"), XSEEN[nm])
                if 2 * n > 0:
                    act.wait_ge(sem("norm_xn"), 2 * n)
                for t in range(NT):
                    act.activation(xn[:, t, :], NSRC[nm][:, t, :], ACT.Square, accum_out=ss[:, t:t + 1])\
                       .then_inc(sem("norm_ss"), 1)
                act.wait_ge(sem("norm_var"), n + 1)
                act.activation(rstd, var, ACT.Sqrt).then_inc(sem("norm_rstd"), 1)
                if nm == "n_even":
                    act.wait_ge(sem("mod_moved"), 1)
                for j in (0, 1, 4, 5):
                    b = j // 2
                    act.wait_ge(sem("norm_T"), 4 * n + b + 1)
                    shift = NSHIFT[nm][:, j:j + 1] if nm in NSHIFT else 0.0
                    act.activation(hT[:, j, :], bank(b)[:, T * (j % 2):T * (j % 2) + T], ACT.Identity, bias=shift,
                                   scale=NGAIN[nm][:, j:j + 1]).then_inc(sem("norm_act"), 1)

            def gemm(nm):
                g = PL.gemms[nm]
                count = len(g["pieces"])
                for k in range(1, min(3, count)):
                    split_piece(nm, k, k)
                for c in range(g["n"]):
                    G = g["base"] + c
                    kind, dst = gemm_dst(nm, c)
                    if 2 * c + 3 < count:
                        split_piece(nm, 2 * c + 3, 2 * c + 3)
                    if not kind.startswith("resid"):
                        act.wait_ge(sem("w_used"), PL.done_at[G])
                    ps = bank(2 * (G % 4))
                    if kind == "copy":
                        d = dst[:, 0, :]
                        act.activation(d, ps[:, 0:d.shape[1]], ACT.Copy).then_inc(sem("ev_act"), 1)
                    elif kind == "feat":
                        act.activation(flat(dst[:, 0:2, :]), ps, ACT.Copy,
                                       scale=0.125 if c < 2 else 1.0).then_inc(sem("ev_act"), 1)
                    elif kind == "kv":
                        for lo, hi, d, o in KV_PARTS[c]:
                            m = act.activation(d[:, 0, o:o + hi - lo], ps[:, lo:hi], ACT.Copy)
                        m.then_inc(sem("ev_act"), 1)
                    elif kind == "shift":
                        for f in range(4):
                            n = 4 * c + f
                            if n > 3:
                                act.wait_ge(sem("shift_mixed"), n - 3)
                            tmp = sh_tmp[n % 4]
                            act.activation(tmp[:, 1:T + 1], bank(2 * (G % 4) + f // 2)[:, T * (f % 2):T * (f % 2) + T],
                                           ACT.Copy, scale=rcols[:, n:n + 1]).then_inc(sem("shift_mu"), 1)
                    if 2 * c + 4 < count:
                        split_piece(nm, 2 * c + 4, 2 * c + 4)

            def transposes(nm):
                for i, (srcs, dst) in enumerate(TRS[nm]):
                    B = TR_BASE[nm] + i
                    if B % 2 == 0:
                        act.wait_ge(sem("tr_done"), B + 1)
                        act.activation(dst, bank(4 + B % 4)[:, 0:P * len(srcs)], ACT.Copy).then_inc(sem("tr_act"), 1)

            def heads(n):
                act.wait_ge(sem("heads_var"), n + 1)
                act.activation(hrstd, hvar, ACT.Sqrt).then_inc(sem("heads_rstd"), 1)

            def split_piece(nm, r, n, turn=0):
                s = STAGES[nm]
                pc = PL.pieces[s["pieces"][r]]
                act.wait_ge(sem(f"landed{pc['slot']}"), pc["landed"] + 64 * turn)
                if not isinstance(n, int) or s["split"] + n > 2:
                    act.wait_ge(sem("w_used"), s["split"] + n - 2)
                act.activation(w_hi[:, (s["split"] + r) % 3, :], piece(s["pieces"][r]), ACT.Copy)\
                   .then_inc(sem("w_split_hi"), 1)

            def split_h(nm):
                if nm.startswith("n_"):
                    n = NORMS.index(nm)
                    own, other = [(b, "norm_act", 4 * n + 4) for b in (0, 2)], [(b, "norm_dve", 4 * n + 4) for b in (1, 3)]
                else:
                    n = TR_BASE[nm]
                    own, other = ([(b, ("tr_act", "tr_dve")[(n + b) % 2], (n + b) // 2 + 1)
                                   for b in range(SPLITS[nm]) if (n + b) % 2 == e] for e in range(2))
                for b, written, count in own + other:
                    act.wait_ge(sem(written), count)
                    act.activation(h_hi[:, 2 * b:2 * b + 2, :], hT[:, 2 * b:2 * b + 2, :], ACT.Copy)\
                       .then_inc(sem("h_split_hi"), 1)

            def swiglu(nm):
                s = PL.swi[nm]
                G0, U0 = s["base"], s["split"]

                def chunk(c, q, n, split):
                    act.wait_ge(sem("w_used"), U0 + n + 1)
                    act.wait_ge(sem("hid_ready"), max(G0 + c, 1) if isinstance(c, int) else G0 + c)
                    act.activation(flat(hid[q % 2]), bank(4 + 2 * (q % 2)), ACT.Silu).then_inc(sem("silu_done"), 1)
                    split(3)
                    split(4)
                    split(5)

                split_piece(nm, 1, 1)
                split_piece(nm, 2, 2)
                chunk(0, 0, 0, lambda j: split_piece(nm, j, j) if j < 5 else None)
                loops = (s["n"] - 1) // 4
                with act.Fori(0, loops) as i:
                    for q in range(4):
                        chunk(4 * i + q + 1, q + 1, 12 * i + 3 * q + 2,
                              lambda j: split_piece(nm, 3 * q + 2 + j, 12 * i + 3 * q + 2 + j, i))
                for c in range(4 * loops + 1, s["n"]):
                    chunk(c, c % 4, 3 * c - 1,
                          lambda j: split_piece(nm, 3 * c - 1 + j, 3 * c - 1 + j) if 3 * c - 1 + j < 3 * s["n"] else None)

            def attention(kind):
                jobs, base = JOBS[kind], JOB_BASE[kind]
                for j in range(len(jobs) + 1):
                    J = base + j
                    if j < len(jobs):
                        segs = job(*jobs[j])[0]
                        n = segs[0]["n"]
                        act.wait_ge(sem("att_logits"), J + 1)
                        if J > 1:
                            act.wait_ge(sem("att_pt"), J - 1)
                        src = bank(2 * (j % 2), 2).rearrange("p (s n) -> p s n", n=T)[:, 0:len(segs), 0:n]
                        dst = att_p[:, j % 2, :].rearrange("p (s n) -> p s n", n=T)[:, 0:len(segs), 0:n]
                        act.activation(dst, src, ACT.Exp, bias=nmax[:, j % 2:j % 2 + 1],
                                       accum_out=esum[:, j % 4:j % 4 + 1]).then_inc(sem("att_exp"), 1)
                    if j >= 1:
                        J1 = J - 1
                        nb = sum(len(sg["v"]) for sg in job(*jobs[j - 1])[0])
                        act.wait_ge(sem("att_pt"), J1 + 1)
                        if J1 > 0:
                            act.wait_ge(sem("att_pv"), J1)
                        act.activation(att_pt[:, 0:P * nb], bank(4, 2)[:, 0:P * nb], ACT.Copy)\
                           .then_inc(sem("att_pts"), 1)

            act.wait_ge(sem("c_in"), 16)
            act.activation(csilu[:, :], cact[:, :], ACT.Silu).then_inc(sem("silu_done"), 1)
            act.wait_ge(sem("cols_in"), 80)
            act.wait_ge(sem("keep_in"), 16)


            def modulation(layer):
                act.wait_ge(sem("mod_rows"), layer + 1)
                for j in range(2):
                    act.activation(grow[layer][j], bank(2 * j, 2), ACT.Copy).then_inc(sem("mod_rows_in"), 1)

            norm("n_even")
            split_piece("even_in", 0, 0)
            split_h("n_even")
            gemm("even_in")
            act.wait_ge(sem("ev_act"), 7)
            act.wait_ge(sem("ev_dve"), 7)
            act.activation(proj_e[:, :, 1536:2048], proj_e[:, :, 1536:2048], ACT.Silu).then_inc(sem("even_gate"), 1)
            modulation(0)
            transposes("ret_qk")
            for h in range(4):
                act.wait_ge(sem("ret_pv"), h + 1)
                act.activation(xn[:, :, P * h:P * h + P], bank(2 + h % 2)[:, 0:T].rearrange("p (t n) -> p t n", t=NT),
                               ACT.Copy).then_inc(sem("ret_moved"), 1)
            heads(0)
            heads(1)
            transposes("att_qk")
            attention("att")
            split_piece("even_out", 0, 0)
            transposes("even_mix")
            split_h("even_mix")
            gemm("even_out")

            def router(layer):
                act.wait_ge(sem("router_ps"), layer + 1)
                act.activation(rt_sc, bank(4)[:, 0:2 * NE], ACT.Sigmoid).then_inc(sem("router_sig"), 1)
                for b in range(0, 8, 2):
                    act.wait_ge(sem("comb_ps"), 8 * layer + b + 1)
                    act.activation(flat(comb_b[:, 2 * b:2 * b + 2, :]), bank(b), ACT.Copy).then_inc(sem("comb_act"), 1)

            split_piece("moe0", 0, 0)
            norm("n_moe0")
            split_h("n_moe0")
            router(0)
            swiglu("moe0")
            act.wait_ge(sem("x_new"), 2)
            modulation(1)
            split_piece("odd_in", 0, 0)
            norm("n_odd")
            split_h("n_odd")
            gemm("odd_in")
            for s_ in range(17):
                if s_ < 16:
                    h = s_
                    act.wait_ge(sem("sb_z"), h + 1)
                    if h > 1:
                        act.wait_ge(sem("sb_soft"), h - 1)
                    step(act.activation(sb_abs[h % 2], bank(h % 2)[:, 0:384], ACT.Abs))
                    step(act.activation(sb_abs[h % 2], sb_abs[h % 2], ACT.Exp, scale=-1.0))
                    act.activation(sb_abs[h % 2], sb_abs[h % 2], ACT.Ln, bias=1.0).then_inc(sem("sb_ln"), 1)
                if s_ >= 1:
                    h = s_ - 1
                    act.wait_ge(sem("sb_sums"), h + 1)
                    if h > 1:
                        act.wait_ge(sem("sb_pv"), h - 1)
                    act.activation(sb_a[h % 2], bank(2 + h % 2)[:, 0:384], ACT.Exp).then_inc(sem("sb_exp"), 1)
            split_piece("odd_out", 0, 0)
            transposes("odd_mix")
            split_h("odd_mix")
            gemm("odd_out")
            split_piece("moe1", 0, 0)
            norm("n_moe1")
            split_h("n_moe1")
            router(1)
            swiglu("moe1")
            split_piece("pre0", 0, 0)
            norm("n_pre0")
            split_h("n_pre0")
            swiglu("pre0")
            split_piece("mem0", 0, 0)
            norm("n_mem0")
            split_h("n_mem0")
            gemm("mem0")
            heads(2)
            transposes("mem0_k")
            split_piece("a_in", 0, 0)
            norm("n_mix0")
            split_h("n_mix0")
            gemm("a_in")
            heads(3)
            transposes("mem0_q")
            attention("mem0")
            act.wait_ge(sem("shift_mixed"), SHIFT_TILES)
            act.activation(F[0:64, 18, :], F[0:64, 18, :], ACT.Tanh).then_inc(sem("rw_low"), 1)
            act.activation(F[:, 19, :], F[:, 19, :], ACT.Sigmoid).then_inc(sem("rw_low"), 1)
            act.wait_ge(sem("rw_w_ps"), 1)
            for i in range(6):
                m = act.activation(W[0][:, i, :], bank(i // 2)[:, T * (i % 2):T * (i % 2) + T], ACT.Sigmoid,
                                   bias=rcols[:, 20 + i:21 + i])
            m.then_inc(sem("rw_sig"), 1)
            act.wait_ge(sem("rw_a_ps"), 1)
            for i in range(6):
                m = act.activation(W[1][:, i, :], bank(3 + i // 2)[:, T * (i % 2):T * (i % 2) + T], ACT.Sigmoid,
                                   bias=rcols[:, 26 + i:27 + i])
            m.then_inc(sem("rw_sig"), 1)
            act.wait_ge(sem("rw_g_ps"), 1)
            for n in range(3):
                m = act.activation(flat(gate)[:, 512 * n:512 * n + 512], bank((6 + n) % 8), ACT.Copy)
            m.then_inc(sem("rw_gate"), 1)
            act.wait_ge(sem("rw_ssr"), 1)
            act.activation(Wf[5], Wf[5], ACT.Sqrt).then_inc(sem("rw_kkn"), 1)
            act.wait_ge(sem("rw_prev"), 1)
            act.activation(Wf[0], Wf[0], ACT.Exp, scale=-DECAY).then_inc(sem("rw_dec"), 1)
            act.wait_ge(sem("rw_decayed"), 1)
            act.activation(Wf[0], Wf[2], ACT.Exp, scale=DECAY).then_inc(sem("rw_dec"), 1)
            act.wait_ge(sem("rw_decayed"), 2)
            act.activation(Wf[0], Wf[2], ACT.Exp, scale=-DECAY).then_inc(sem("rw_dec"), 1)
            for nm in ("rw_v", "rw_b", "rw_k"):
                transposes(nm)
            for g in range(3):
                for l in range(5):
                    for s in range(2):
                        n = 10 * g + 2 * l + s
                        act.wait_ge(sem("rw_x_ps"), n + 1)
                        if n > 1:
                            act.wait_ge(sem("rw_tx_ps"), n - 1)
                        act.activation(flat(t_x[s]), bank(3 * s), ACT.Copy).then_inc(sem("rw_x"), 1)
                    if l == 0:
                        for s in range(2):
                            i = 2 * g + s
                            act.wait_ge(sem("rw_u_ps"), i + 1)
                            src = bank(6 + s).rearrange("p (e t n) -> p e t n", e=2, t=NT)
                            for e in range(2):
                                o = P * i + 64 * e
                                m = act.activation(U[:, :, o:o + 64], src[:, e, :, 64 * e:64 * e + 64], ACT.Copy)
                            m.then_inc(sem("rw_u"), 1)
            for c in range(4):
                t, rows = c // 2, slice(64 * (c % 2), 64 * (c % 2) + 64)
                act.wait_ge(sem("rw_y_ps"), c + 1)
                act.activation(y_r[rows, t, :], bank(2, 2)[rows, 0:768], ACT.Copy).then_inc(sem("rw_y"), 1)
            act.wait_ge(sem("rw_yvar"), 1)
            act.activation(hrstd, hvar, ACT.Sqrt).then_inc(sem("rw_yrstd"), 1)
            split_piece("a_out", 0, 0)
            transposes("a_mix")
            split_h("a_mix")
            gemm("a_out")
            split_piece("post0", 0, 0)
            norm("n_post0")
            split_h("n_post0")
            swiglu("post0")
            split_piece("kv", 0, 0)
            norm("n_kv")
            split_h("n_kv")
            gemm("kv")
            heads(4)
            transposes("kd")
            split_piece("pre1", 0, 0)
            norm("n_pre1")
            split_h("n_pre1")
            swiglu("pre1")
            split_piece("mem1", 0, 0)
            norm("n_mem1")
            split_h("n_mem1")
            gemm("mem1")
            heads(5)
            transposes("mem1_k")
            split_piece("b_q", 0, 0)
            norm("n_mix1")
            split_h("n_mix1")
            gemm("b_q")
            heads(6)
            transposes("dil_q")
            attention("mem1")
            attention("dil")
            split_piece("b_out", 0, 0)
            transposes("b_mix")
            split_h("b_mix")
            gemm("b_out")
            split_piece("post1", 0, 0)
            norm("n_post1")
            split_h("n_post1")
            swiglu("post1")

        @block.vector
        def _(dve):
            done = [0]

            def step(ins):
                done[0] += 1
                ins.then_inc(sem("dve_step"), 1)
                dve.wait_ge(sem("dve_step"), done[0])

            def norm(nm):
                n = NORMS.index(nm)
                dve.wait_ge(sem("norm_ss"), 2 * (n + 1))
                step(dve.tensor_scalar(var, ss, 1.0 / D, EPS, ALU.mult, ALU.add))
                dve.reciprocal(var, var).then_inc(sem("norm_var"), 1)
                dve.wait_ge(sem("norm_rstd"), n + 1)
                for t in range(NT):
                    dve.tensor_scalar(xn[:, t, :], NSRC[nm][:, t, :], rstd[:, t:t + 1], None, ALU.mult)\
                       .then_inc(sem("norm_xn"), 1)
                if nm == "n_even":
                    shift_and_scale()
                    dve.wait_ge(sem("mod_moved"), 1)
                for j in (2, 3, 6, 7):
                    b = j // 2
                    dve.wait_ge(sem("norm_T"), 4 * n + b + 1)
                    if nm in NSHIFT:
                        m = dve.tensor_scalar(hT[:, j, :], bank(b)[:, T * (j % 2):T * (j % 2) + T], NGAIN[nm][:, j:j + 1],
                                              NSHIFT[nm][:, j:j + 1], ALU.mult, ALU.add)
                    else:
                        m = dve.tensor_scalar(hT[:, j, :], bank(b)[:, T * (j % 2):T * (j % 2) + T], NGAIN[nm][:, j:j + 1], None, ALU.mult)
                    m.then_inc(sem("norm_dve"), 1)

            def gemm(nm):
                g = PL.gemms[nm]
                count = len(g["pieces"])
                for k in range(1, min(3, count)):
                    split_piece(nm, k, k)
                for c in range(g["n"]):
                    G = g["base"] + c
                    kind, dst = gemm_dst(nm, c)
                    if 2 * c + 3 < count:
                        split_piece(nm, 2 * c + 3, 2 * c + 3)
                    dve.wait_ge(sem("w_used"), PL.done_at[G])
                    pair = 2 * (G % 4)
                    ps = bank(pair + 1)
                    if kind == "copy":
                        d = dst[:, 1, :]
                        dve.tensor_copy(d, ps[:, 0:d.shape[1]]).then_inc(sem("ev_dve"), 1)
                    elif kind == "feat":
                        dve.tensor_scalar(flat(dst[:, 2:4, :]), ps, 0.125 if c < 2 else 1.0, None, ALU.mult)\
                           .then_inc(sem("ev_dve"), 1)
                    elif kind == "kv":
                        for lo, hi, d, o in KV_PARTS[c]:
                            m = dve.tensor_copy(d[:, 1, o:o + hi - lo], ps[:, lo:hi])
                        m.then_inc(sem("ev_dve"), 1)
                    elif kind == "shift":
                        for f in range(4):
                            n = 4 * c + f
                            dve.wait_ge(sem("shift_mu"), n - n % 2 + 2)
                            m = dve.scalar_tensor_tensor(
                                out=F[:, n, :], in0=bank(pair + f // 2)[:, T * (f % 2):T * (f % 2) + T],
                                scalar=omu[:, n:n + 1], in1=sh_tmp[n % 4][:, 0:T], op0=ALU.mult, op1=ALU.add)
                            m.then_inc(sem("shift_mixed"), 1)
                    else:
                        cols = slice(512 * c, 512 * c + 512)
                        both = psum[:, pair:pair + 2, :]
                        if kind == "resid_g":
                            row = grow[dst[0]][0][:, cols].unsqueeze(1)
                            step(dve.tensor_tensor(xn[:, :, cols], both, bc(row, [P, NT, 512]), ALU.mult))
                            m = dve.tensor_tensor(x[:, :, cols], x[:, :, cols], xn[:, :, cols], ALU.add)
                        else:
                            m = dve.tensor_tensor(x[:, :, cols], x[:, :, cols], both, ALU.add)
                        if c == 1:
                            m.then_inc(sem("x_new"), 1)
                        else:
                            m.then_inc(sem("resid_first"), 1)
                    if 2 * c + 4 < count:
                        split_piece(nm, 2 * c + 4, 2 * c + 4)

            def transposes(nm):
                for i, (srcs, dst) in enumerate(TRS[nm]):
                    B = TR_BASE[nm] + i
                    if B % 2 == 1:
                        dve.wait_ge(sem("tr_done"), B + 1)
                        dve.tensor_copy(dst, bank(4 + B % 4)[:, 0:P * len(srcs)]).then_inc(sem("tr_dve"), 1)

            def heads(n, parts, width, gains, scale=1.0):
                col = 0
                for v in parts:
                    H = v.shape[1]
                    sq = pool[:, XN:XN + H * width].rearrange("p (h d) -> p h d", h=H) if n > 1 else \
                        pool[:, WORK + 4992:WORK + 4992 + H * width].rearrange("p (h d) -> p h d", h=H)
                    step(dve.tensor_tensor(sq, v, v, ALU.mult))
                    m = dve.tensor_reduce(hss[:, col:col + H], sq, AX.X, ALU.add)
                    step(m)
                    col += H
                if col < 32:
                    step(dve.memset(hss[:, col:32], 1.0))
                step(dve.tensor_scalar(hvar, hss, 1.0 / width, EPS, ALU.mult, ALU.add))
                dve.reciprocal(hvar, hvar).then_inc(sem("heads_var"), 1)
                dve.wait_ge(sem("heads_rstd"), n + 1)
                col = 0
                for v in parts:
                    H = v.shape[1]
                    m = dve.tensor_tensor(v, v, bc(hrstd[:, col:col + H].unsqueeze(2), [P, H, width]), ALU.mult)
                    col += H
                    step(m)
                    for lo, hi, g, s in gains:
                        vv = v[:, lo:hi, :]
                        step(dve.scalar_tensor_tensor(out=vv, in0=vv, scalar=s,
                                                      in1=bc(gains64[:, g, :].unsqueeze(1), [P, hi - lo, width]),
                                                      op0=ALU.mult, op1=ALU.mult))

            def attention(kind):
                jobs, base = JOBS[kind], JOB_BASE[kind]
                for j in range(len(jobs) + 2):
                    J = base + j
                    if j < len(jobs):
                        segs = job(*jobs[j])[0]
                        n = segs[0]["n"]
                        dve.wait_ge(sem("att_scores"), J + 1)
                        if J > 1:
                            dve.wait_ge(sem("att_exp"), J - 1)
                        lg = bank(2 * (j % 2), 2).rearrange("p (s n) -> p s n", n=T)
                        step(dve.tensor_reduce(mx[:, j % 2:j % 2 + 1], lg[:, 0:len(segs), 0:n], AX.XY, ALU.max))
                        dve.tensor_scalar(nmax[:, j % 2:j % 2 + 1], mx[:, j % 2:j % 2 + 1], -1.0, None, ALU.mult)\
                           .then_inc(sem("att_logits"), 1)
                    if j >= 2:
                        o = job(*jobs[j - 2])[1]
                        if J > 1:
                            dve.wait_ge(sem("att_pv"), J - 1)
                        step(dve.reciprocal(erec[:, j % 2:j % 2 + 1], esum[:, (j - 2) % 4:(j - 2) % 4 + 1]))
                        dve.tensor_scalar(o, bank(6 + j % 2)[:, 0:64], erec[:, j % 2:j % 2 + 1], None, ALU.mult)\
                           .then_inc(sem("att_o"), 1)

            def split_piece(nm, r, n):
                s = STAGES[nm]
                slot = (s["split"] + r) % 3
                dve.wait_ge(sem("w_split_hi"), s["split"] + n + 1)
                dve.tensor_tensor(w_lo[:, slot, :], piece(s["pieces"][r]), w_hi[:, slot, :].bitcast(F32),
                                  ALU.subtract).then_inc(sem("w_lo"), 1)
                if nm == "even_in":
                    ada_piece(KD + n)

            def split_h(nm):
                if nm.startswith("n_"):
                    order = (0, 2, 1, 3)
                else:
                    order = sorted(range(SPLITS[nm]), key=lambda b: (TR_BASE[nm] + b) % 2)
                for i, b in enumerate(order):
                    dve.wait_ge(sem("h_split_hi"), SPLIT_BASE[nm] + i + 1)
                    dve.tensor_tensor(h_lo[:, 2 * b:2 * b + 2, :], hT[:, 2 * b:2 * b + 2, :],
                                      h_hi[:, 2 * b:2 * b + 2, :].bitcast(F32), ALU.subtract)\
                       .then_inc(sem("h_split_lo"), 1)

            def swiglu(nm):
                s = PL.swi[nm]
                G0, U0 = s["base"], s["split"]
                moe = nm.startswith("moe")
                pp = 2 if moe else 1
                P0 = sum(PL.swi[k]["n"] * (2 if k.startswith("moe") else 1) for k in SWIGLUS[:s["no"]])

                def product(c, q, n, e):
                    dve.wait_ge(sem("silu_done"), G0 + c + 2)
                    dve.wait_ge(sem("w_used"), U0 + n + 1)
                    h = hid[q % 2]
                    dve.tensor_tensor(flat(h), flat(h), bank(5 + 2 * (q % 2)), ALU.mult).then_inc(sem("hid_prod"), 1)
                    if moe:
                        dve.wait_ge(sem("hid_prod"), P0 + pp * c + 1)
                        dve.tensor_tensor(h[:, :, :], h[:, :, :], bc(comb_b[:, e, :].unsqueeze(1), [P, 2, T]), ALU.mult)\
                           .then_inc(sem("hid_prod"), 1)
                    dve.wait_ge(sem("hid_prod"), P0 + pp * c + pp)
                    dve.tensor_copy(flat(hid_hi[:, q % 2]), flat(h)).then_inc(sem("hid_round"), 1)
                    dve.wait_ge(sem("hid_round"), G0 + c + 1)
                    dve.tensor_tensor(flat(hid_lo[:, q % 2]), flat(h), flat(hid_hi[:, q % 2]).bitcast(F32), ALU.subtract)\
                       .then_inc(sem("hid_ready"), 1)

                def ada_part(i, q):
                    dve.wait_ge(sem("ada1_landed"), 32 * i + 16 * q + 16)
                    half = acc[:, q * ADA_HALF:(q + 1) * ADA_HALF]
                    dve.scalar_tensor_tensor(out=half, in0=ada1, scalar=csilu[:, bass.ds(i, 1)], in1=half,
                                             op0=ALU.mult, op1=ALU.add).then_inc(sem("ada_used"), 1)

                if nm == "moe0":
                    dve.wait_ge(sem("ada_b_in"), 64)
                for r in (1, 2, 3):
                    split_piece(nm, r, r)
                product(0, 0, 1, 0)
                split_piece(nm, 4, 4)
                loops = (s["n"] - 1) // 4
                with dve.Fori(0, loops) as i:
                    for q in range(4):
                        r = 3 * q + 5
                        split_piece(nm, r, 12 * i + r)
                        product(4 * i + q + 1, q + 1, 12 * i + r - 2, 2 * i + (q + 1) // 2)
                        split_piece(nm, r + 1, 12 * i + r + 1)
                        split_piece(nm, r + 2, 12 * i + r + 2)
                        if nm == "moe0" and q % 2:
                            ada_part(i, q // 2)
                for c in range(4 * loops + 1, s["n"]):
                    if 3 * c + 2 < 3 * s["n"]:
                        split_piece(nm, 3 * c + 2, 3 * c + 2)
                    product(c, c % 4, 3 * c, c // 2)
                    for n in (3 * c + 3, 3 * c + 4):
                        if n < 3 * s["n"]:
                            split_piece(nm, n, n)
                    if nm == "moe0" and c == s["n"] - 2:
                        ada_part(loops, 0)
                if nm == "moe0":
                    ada_part(loops, 1)
                dve.wait_ge(sem("sums_done"), s["no"] + 1)
                for t in range(NT):
                    ps = bank(2 * t, 2)
                    if moe:
                        step(dve.tensor_tensor(xn[:, t, :], ps, grow[int(nm[-1])][1], ALU.mult))
                        m = dve.tensor_tensor(x[:, t, :], x[:, t, :], xn[:, t, :], ALU.add)
                    else:
                        m = dve.scalar_tensor_tensor(out=x[:, t, :], in0=ps, scalar=0.5, in1=x[:, t, :],
                                                     op0=ALU.mult, op1=ALU.add)
                    m.then_inc(sem("x_new" if t else "x_part"), 1)

            def mod_cols(layer, halves, n):
                dve.wait_ge(sem("mod_cols"), n)
                for j in halves:
                    m = dve.tensor_copy(mcols[:, layer, 2 * j:2 * j + 2].rearrange("p j k -> p (j k)"),
                                        bank(4)[:, 2 * KD * j:2 * KD * j + 2 * KD])
                step(m)
                for j in halves:
                    m = dve.scalar_tensor_tensor(out=mgain[:, 2 * layer + j, :], in0=mcols[:, layer, 1 + 2 * j, :],
                                                 scalar=1.0, in1=gcols[:, layer + 2 * j, :], op0=ALU.add, op1=ALU.mult)
                m.then_inc(sem("mod_moved"), 1)

            def ada_piece(n):
                no, row, third = PL.ada_order[n]
                dve.wait_ge(sem(f"landed{PL.pieces[no]['slot']}"), PL.pieces[no]["landed"])
                if row > 0:
                    dve.wait_ge(sem("ada_used"), n if third == 0 else n - 1)
                dve.scalar_tensor_tensor(out=acc_0[third], in0=piece(no), scalar=csilu[:, row:row + 1], in1=acc_0[third],
                                         op0=ALU.mult, op1=ALU.add).then_inc(sem("ada_used"), 1)

            dve.wait_ge(sem("silu_done"), 1)
            dve.wait_ge(sem("ada_b_in"), 48)
            for n in range(EARLY):
                ada_piece(n)

            def shift_and_scale():
                for n in range(EARLY, KD):
                    ada_piece(n)
                dve.wait_ge(sem("bias_ps"), 2)
                dve.wait_ge(sem("hot_in"), 80)
                dve.tensor_copy(view(WORK + 4256, 512)[0:8, :], bank(6)[0:8, :]).then_inc(sem("bias_rows"), 1)
                dve.tensor_tensor(view(WORK + 4768, 512)[0:12, :], bank(7)[0:12, :], view(WORK + 2176, 4, 512)[0:12, 3, :],
                                  ALU.add).then_inc(sem("bias_rows"), 1)
                mod_cols(0, (0,), 1)

            dve.wait_ge(sem("cols_in"), 80)
            dve.tensor_scalar(omu[:, :], rcols[:, 0:SHIFT_TILES], -1.0, 1.0, ALU.mult, ALU.add).then_inc(sem("hid_ready"), 1)
            dve.wait_ge(sem("keep_in"), 16)
            norm("n_even")
            split_piece("even_in", 0, 0)
            split_h("n_even")
            gemm("even_in")
            for n in range(KD + 14, ADA_PIECES):
                ada_piece(n)
            dve.wait_ge(sem("ev_act"), 7)
            dve.wait_ge(sem("ev_dve"), 7)
            dve.wait_ge(sem("even_in"), 16)
            dve.wait_ge(sem("bias_out"), 32)
            for t in range(NT):
                v = proj_e[:, t, 0:1024].rearrange("p (h d) -> p h d", h=8)
                x1, x2 = v[:, :, 0:64], v[:, :, 64:128]
                co = bc(rope_c[:, t, :].unsqueeze(1), [P, 8, 64])
                si = bc(rope_s[:, t, :].unsqueeze(1), [P, 8, 64])
                r = [z.rearrange("p (h d) -> p h d", h=8) for z in (rot_a[:, 0, :], rot_a[:, 1, :],
                                                                    rot_b[:, 0, :], rot_b[:, 1, :])]
                dve.tensor_tensor(r[0], x1, co, ALU.mult)
                dve.tensor_tensor(r[1], x2, si, ALU.mult)
                dve.tensor_tensor(r[2], x1, si, ALU.mult)
                step(dve.tensor_tensor(r[3], x2, co, ALU.mult))
                dve.tensor_tensor(x1, r[0], r[1], ALU.subtract)
                step(dve.tensor_tensor(x2, r[2], r[3], ALU.add))
            dve.memset(tiny[:, 160:161], 0.0).then_inc(sem("rotated"), 1)
            mod_cols(0, (1,), 2)
            transposes("ret_qk")
            for h in range(4):
                dve.wait_ge(sem("ret_scores"), h + 1)
                if h > 1:
                    dve.wait_ge(sem("ret_pv"), h - 1)
                dve.tensor_tensor(ret_s[:, h % 2, :], bank(h % 2)[:, 0:384], decay_t[:, h, :], ALU.mult)\
                   .then_inc(sem("ret_decayed"), 1)
            dve.wait_ge(sem("norm_T"), 4)
            qk = [proj_e[:, t, 2048:3072].rearrange("p (h d) -> p h d", h=16) for t in range(NT)]
            heads(0, qk, 64, [(0, 8, 0, 0.125), (8, 16, 1, 1.0)])
            dve.memset(tiny[:, 160:161], 0.0).then_inc(sem("heads_ok"), 1)
            dve.wait_ge(sem("ret_moved"), 4)
            rr = [xn[:, t, 0:512].rearrange("p (h d) -> p h d", h=4) for t in range(NT)]
            heads(1, rr, P, [])
            dve.wait_ge(sem("even_gate"), 1)
            dve.tensor_tensor(xn[:, :, 0:512], xn[:, :, 0:512], proj_e[:, :, 1536:2048], ALU.mult)\
               .then_inc(sem("even_mixed"), 1)
            transposes("att_qk")
            attention("att")
            split_piece("even_out", 0, 0)
            transposes("even_mix")
            split_h("even_mix")
            gemm("even_out")

            def router(layer):
                dve.wait_ge(sem("router_sig"), layer + 1)
                sel, cmp_, eq = rt[:, 32:64], rt[:, 64:192], rt[:, 192:320]
                rank, pick, gs = rt[:, 320:352], rt[:, 352:384], rt[:, 384:392]
                gpick, tot = rt[:, 392:400], rt[:, 400:402]
                step(dve.tensor_tensor(sel.rearrange("p (t e) -> p t e", t=NT), rt_sc.rearrange("p (t e) -> p t e", t=NT),
                                       bc(router_b[:, :].unsqueeze(1), [P, NT, NE]), ALU.add))

                def ranks(v, groups, out_):
                    n = 16 * groups
                    v3 = v.rearrange("p (g e) -> p g e", e=4)
                    other = bc(v3.unsqueeze(2), [P, groups, 4, 4])
                    own = bc(v3.unsqueeze(3), [P, groups, 4, 4])
                    c4 = cmp_[:, 0:n].rearrange("p (g e j) -> p g e j", g=groups, e=4)
                    q4 = eq[:, 0:n].rearrange("p (g e j) -> p g e j", g=groups, e=4)
                    dve.tensor_tensor(c4, other, own, ALU.is_gt)
                    step(dve.tensor_tensor(q4, other, own, ALU.is_equal))
                    step(dve.tensor_tensor(eq[:, 0:n].rearrange("p (g k) -> p g k", g=groups),
                                           eq[:, 0:n].rearrange("p (g k) -> p g k", g=groups),
                                           bc(K["lower"].unsqueeze(1), [P, groups, 16]), ALU.mult))
                    step(dve.tensor_tensor(cmp_[:, 0:n], cmp_[:, 0:n], eq[:, 0:n], ALU.add))
                    step(dve.tensor_reduce(out_, cmp_[:, 0:n].rearrange("p (g j) -> p g j", j=4), AX.X, ALU.add))

                ranks(sel, 8, rank)
                step(dve.tensor_scalar(pick, rank, 1.5, None, ALU.is_lt))
                step(dve.tensor_tensor(sel, sel, pick, ALU.mult))
                step(dve.tensor_reduce(gs, sel.rearrange("p (g e) -> p g e", e=4), AX.X, ALU.add))
                ranks(gs, 2, gpick)
                step(dve.tensor_scalar(gpick, gpick, 0.5, None, ALU.is_lt))
                step(dve.tensor_tensor(pick.rearrange("p (g e) -> p g e", e=4), pick.rearrange("p (g e) -> p g e", e=4),
                                       bc(gpick.unsqueeze(2), [P, 8, 4]), ALU.mult))
                step(dve.tensor_tensor(pick, pick, rt_sc, ALU.mult))
                step(dve.tensor_reduce(tot, pick.rearrange("p (t e) -> p t e", t=NT), AX.X, ALU.add))
                step(dve.reciprocal(tot, tot))
                dve.tensor_tensor(comb_tok.rearrange("p (t e) -> p t e", t=NT), pick.rearrange("p (t e) -> p t e", t=NT),
                                  bc(tot.unsqueeze(2), [P, NT, NE]), ALU.mult).then_inc(sem("comb_tok"), 1)
                dve.wait_ge(sem("comb_T_ps"), layer + 1)
                dve.tensor_copy(comb_t, bank(5)[0:NE, 0:T]).then_inc(sem("comb_T"), 1)
                for b in range(1, 8, 2):
                    dve.wait_ge(sem("comb_ps"), 8 * layer + b + 1)
                    dve.tensor_copy(flat(comb_b[:, 2 * b:2 * b + 2, :]), bank(b)).then_inc(sem("comb_dve"), 1)

            split_piece("moe0", 0, 0)
            norm("n_moe0")
            split_h("n_moe0")
            router(0)
            dve.memset(tiny[:, 160:161], 0.0).then_inc(sem("moe_ready"), 1)
            swiglu("moe0")
            mod_cols(1, (0, 1), 3)
            dve.wait_ge(sem("mod_rows_in"), 4)
            split_piece("odd_in", 0, 0)
            norm("n_odd")
            split_h("n_odd")
            gemm("odd_in")
            step(dve.memset(sb_zero, 0.0))
            for s_ in range(18):
                if s_ < 16:
                    h = s_
                    dve.wait_ge(sem("sb_ln"), h + 1)
                    if h > 1:
                        dve.wait_ge(sem("sb_sums"), h - 1)
                    dve.scalar_tensor_tensor(out=sb_sp[h % 2], in0=bank(h % 2)[:, 0:384], scalar=0.0, in1=sb_abs[h % 2],
                                             op0=ALU.max, op1=ALU.add).then_inc(sem("sb_soft"), 1)
                    dve.wait_ge(sem("sb_soft"), h + 1)
                    diag = sb_sp[h % 2].rearrange("p (b n) -> p b n", b=3)
                    dve.copy_predicated(diag[:, 0, :], K["neg_from"].bitcast(U32), sb_zero)
                    dve.copy_predicated(diag[:, 2, :], K["neg_from"].bitcast(U32), sb_zero)\
                       .then_inc(sem("sb_masked"), 1)
                if 1 <= s_ <= 16:
                    h = s_ - 1
                    dve.wait_ge(sem("sb_exp"), h + 1)
                    diag = sb_a[h % 2].rearrange("p (b n) -> p b n", b=3)
                    dve.copy_predicated(diag[:, 0, :], K["neg_from"].bitcast(U32), sb_zero)
                    dve.copy_predicated(diag[:, 2, :], K["neg_from"].bitcast(U32), sb_zero)\
                       .then_inc(sem("sb_weights"), 1)
                if s_ >= 2:
                    h = s_ - 2
                    dve.wait_ge(sem("sb_pv"), h + 1)
                    dve.tensor_copy(xn[:, :, 64 * h:64 * h + 64],
                                    bank(4 + h % 2)[:, 0:128].rearrange("p (t d) -> p t d", t=NT))\
                       .then_inc(sem("sb_out"), 1)
            split_piece("odd_out", 0, 0)
            transposes("odd_mix")
            split_h("odd_mix")
            gemm("odd_out")
            split_piece("moe1", 0, 0)
            norm("n_moe1")
            split_h("n_moe1")
            router(1)
            swiglu("moe1")
            split_piece("pre0", 0, 0)
            norm("n_pre0")
            split_h("n_pre0")
            swiglu("pre0")
            split_piece("mem0", 0, 0)
            norm("n_mem0")
            split_h("n_mem0")
            gemm("mem0")

            def mem_keys(n, q):
                for e in moved(f"mem{q}", 0):
                    dve.wait_ge(sem(e[0]), e[1])
                mk = [mem_kv[:, t, 0:256].rearrange("p (h d) -> p h d", h=4) for t in range(NT)]
                dve.wait_ge(sem("norm_T"), 4 * (NORMS.index(f"n_mem{q}") + 1))
                heads(n, mk, 64, [(0, 4, 4 + q, 1.0)])
                dve.tensor_copy(mem_v, mem_kv[:, :, 256:512]).then_inc(sem("heads_ok"), 1)
                transposes(f"mem{q}_k")

            mem_keys(2, 0)
            split_piece("a_in", 0, 0)
            norm("n_mix0")
            split_h("n_mix0")
            for z in sh_tmp:
                m = dve.memset(z[:, 0:1], 0.0)
            step(m)
            gemm("a_in")
            dve.wait_ge(sem("shift_mixed"), SHIFT_TILES)
            dve.wait_ge(sem("rwkv_in"), 96)
            par = rwkv_par
            for e in moved("a_in", 5):
                dve.wait_ge(sem(e[0]), e[1])
            mq = [q_mem_a[:, t, :].rearrange("p (h d) -> p h d", h=4) for t in range(NT)]
            dve.wait_ge(sem("norm_T"), 4 * (NORMS.index("n_mix0") + 1))
            heads(3, mq, 64, [(0, 4, 2, 0.125)])
            dve.memset(tiny[:, 160:161], 0.0).then_inc(sem("heads_ok"), 1)
            transposes("mem0_q")
            attention("mem0")
            for i in range(6):
                m = dve.tensor_scalar(W[3][:, i, :], Fk[:, i, :], rcols[:, 32 + i:33 + i], None, ALU.mult)
            step(m)
            dve.tensor_tensor(Wf[4], Wf[3], Wf[3], ALU.mult).then_inc(sem("rw_sq"), 1)
            dve.wait_ge(sem("rw_sig"), 1)
            dve.wait_ge(sem("reset_in"), 16)
            for i in range(6):
                m = dve.tensor_tensor_scan(W[2][:, i, :], rw_reset, W[0][:, i, :], 0.0, ALU.mult, ALU.add)
            step(m)
            dve.tensor_tensor(Wf[0], Wf[2], Wf[0], ALU.subtract).then_inc(sem("rw_prev"), 1)
            dve.wait_ge(sem("rw_ss_ps"), 1)
            dve.tensor_scalar(Wf[5], bank(3, 3), 1e-24, None, ALU.max).then_inc(sem("rw_ss"), 1)
            dve.wait_ge(sem("rw_ss"), 1)
            dve.reciprocal(Wf[5], Wf[5]).then_inc(sem("rw_ssr"), 1)
            dve.wait_ge(sem("rw_sig"), 2)
            for i in range(6):
                m = dve.tensor_scalar(W[4][:, i, :], W[1][:, i, :], -1.0, rcols[:, 38 + i:39 + i], ALU.add, ALU.mult)
            step(m)
            step(dve.scalar_tensor_tensor(out=flat(Fk), in0=Wf[4], scalar=1.0, in1=flat(Fk), op0=ALU.add, op1=ALU.mult))
            for i in range(6):
                m = dve.scalar_tensor_tensor(out=W[4][:, i, :], in0=Fr[:, i, :], scalar=rcols[:, 44 + i:45 + i],
                                             in1=Fk[:, i, :], op0=ALU.mult, op1=ALU.mult)
            m.then_inc(sem("rw_rk"), 1)
            dve.wait_ge(sem("rw_kkn"), 1)
            step(dve.tensor_tensor(Wf[3], Wf[3], Wf[5], ALU.mult))
            step(dve.tensor_tensor(Wf[1], Wf[1], Wf[3], ALU.mult))
            dve.wait_ge(sem("rw_dec"), 1)
            dve.tensor_tensor(Wf[3], Wf[3], Wf[0], ALU.mult).then_inc(sem("rw_decayed"), 1)
            dve.wait_ge(sem("rw_dec"), 2)
            dve.tensor_tensor(Wf[5], Wf[1], Wf[0], ALU.mult)
            dve.tensor_tensor(flat(Fk), flat(Fk), Wf[0], ALU.mult).then_inc(sem("rw_decayed"), 1)
            dve.wait_ge(sem("rw_dec"), 3)
            dve.tensor_tensor(flat(Fr), flat(Fr), Wf[0], ALU.mult)
            for c in range(4):
                m = dve.tensor_copy(pend[:, :, c:c + 1], W[0][:, :, 64 * c + 63:64 * c + 64])
            step(m)
            dve.wait_ge(sem("rw_bonus_ps"), 1)
            dve.tensor_copy(bonus, bank(1)[:, 0:24]).then_inc(sem("rw_bonus"), 1)
            dve.memset(state, 0.0).then_inc(sem("rw_scaled"), 1)
            for nm in ("rw_v", "rw_b", "rw_k"):
                transposes(nm)
            levels = par[:, 3072:3712].rearrange("p (l n) -> p l n", l=5)
            lvl0_t, lvl0, strict = par[:, 3712:3840], par[:, 3840:3968], par[:, 3968:4096]

            def four(m_):
                return bc(m_.unsqueeze(1), [P, 4, P])

            def masks(i):
                s = i % 2
                dve.wait_ge(sem("rw_l_ps"), i + 1)
                pv = psum[:, 3 * s:3 * s + 2, 0:T].rearrange("p e (t n) -> p e t n", t=NT)
                lo_ = psum[:, 3 * s:3 * s + 2, T:2 * T].rearrange("p e (t n) -> p e t n", t=NT)
                lt4 = t_lt[s].rearrange("p (e t) n -> p e t n", e=2)
                x4 = t_lm[s].rearrange("p (e t) n -> p e t n", e=2)
                for e in range(2):
                    dve.tensor_tensor(lt4[:, e], pv[:, e], bc(strict.unsqueeze(1), [P, 2, P]), ALU.mult)
                    m = dve.tensor_tensor(x4[:, e], lo_[:, e], bc(lvl0.unsqueeze(1), [P, 2, P]), ALU.mult)
                step(m)
                step(dve.tensor_tensor(t_t[s], four(ident), t_lm[s], ALU.subtract))
                step(dve.tensor_tensor(t_lm[s], t_lt[s], four(lvl0_t), ALU.mult))
                step(dve.tensor_tensor(TT[:, i], four(ident), t_lm[s], ALU.subtract))
                dve.tensor_tensor(t_lm[s], t_lt[s], four(levels[:, 0, :]), ALU.mult).then_inc(sem("rw_lm"), 1)
                if i > 1:
                    dve.wait_ge(sem("rw_u_ps"), i - 1)
                for e in range(2):
                    src = bank((3 * s + 2, 6 + s)[e])[:, 0:T].rearrange("p (t n) -> p t n", t=NT)
                    m = dve.tensor_tensor(t_m[s][:, 2 * e:2 * e + 2], src, bc(strict.unsqueeze(1), [P, 2, P]), ALU.mult)
                m.then_inc(sem("rw_m"), 1)

            dve.wait_ge(sem("tr_act"), tr_counts("rw_v")[0])
            dve.wait_ge(sem("tr_act"), tr_counts("rw_k")[0])
            for g in range(3):
                masks(2 * g)
                masks(2 * g + 1)
                for l in range(5):
                    for s in range(2):
                        tt = flat(TT[:, 2 * g + s])
                        dve.wait_ge(sem("rw_tx_ps"), 10 * g + 2 * l + s + 1)
                        if l < 4:
                            dve.tensor_tensor(flat(t_t[s]), flat(t_t[s]), bank(3 * s + 1), ALU.subtract)
                            step(dve.tensor_tensor(tt, tt, bank(3 * s + 2), ALU.subtract))
                            dve.tensor_tensor(t_lm[s], t_lt[s], four(levels[:, l + 1, :]), ALU.mult)\
                               .then_inc(sem("rw_lm"), 1)
                        else:
                            dve.tensor_tensor(tt, tt, bank(3 * s + 2), ALU.subtract).then_inc(sem("rw_t"), 1)
            dve.wait_ge(sem("rw_t"), 6)
            step(dve.memset(SA, 0.0))
            dve.memset(tiny[:, 161:162], 0.0).then_inc(sem("rw_state"), 1)
            for c in range(4):
                t, q0 = c // 2, 64 * (c % 2)
                rows = slice(q0, q0 + 64)
                dve.wait_ge(sem("rw_z_ps"), c + 1)
                dve.wait_ge(sem("rw_u"), 6)
                dve.tensor_tensor(Z, bank(0, 2)[:, 0:768], U[:, t, :], ALU.add).then_inc(sem("rw_z"), 1)
                dve.wait_ge(sem("rw_sa_ps"), c + 1)
                dve.tensor_scalar(SA[rows, t, :], bank(4, 2)[rows, 0:768], -1.0, None, ALU.mult)\
                   .then_inc(sem("rw_sa"), 1)
                dve.wait_ge(sem("rw_new_ps"), c + 1)
                dve.wait_ge(sem("rw_y_ps"), c + 1)
                for e in range(2):
                    hf = slice(64 * e, 64 * e + 64)
                    st = state[hf, :, hf]
                    new = bank(6, 2)[hf, 0:768].rearrange("p (i n) -> p i n", i=6)[:, :, hf]
                    m = dve.tensor_tensor(st, st, new, ALU.add)
                step(m)
                for e in range(2):
                    hf = slice(64 * e, 64 * e + 64)
                    st = state[hf, :, hf]
                    m = dve.tensor_tensor(st, st, bc(pend[hf, :, c:c + 1], [64, 6, 64]), ALU.mult)
                m.then_inc(sem("rw_state"), 1)
            inc = bc(K["chunk_incl"].unsqueeze(1), [P, 2, P])
            for i in range(7):
                if i < 6:
                    dve.wait_ge(sem("rw_bk_ps"), i + 1)
                    if i > 1:
                        dve.wait_ge(sem("rw_g2_ps"), i - 1)
                    for e in range(2):
                        src = bank(2 * (i % 2) + e).rearrange("p (m n) -> p m n", m=4)
                        dve.tensor_tensor(bm[i % 2][:, 2 * e:2 * e + 2], src[:, 0:2], inc, ALU.mult)
                        m = dve.tensor_tensor(km[i % 2][:, 2 * e:2 * e + 2], src[:, 2:4], inc, ALU.mult)
                    m.then_inc(sem("rw_bk"), 1)
                if i >= 1:
                    dve.wait_ge(sem("rw_g2_ps"), i)
                    dve.wait_ge(sem("rw_y"), 4)
                    src = bank(4 + (i - 1) % 2).rearrange("p (e t n) -> p e t n", e=2, t=NT)
                    for e in range(2):
                        o = P * (i - 1) + 64 * e
                        m = dve.tensor_tensor(y_r[:, :, o:o + 64], y_r[:, :, o:o + 64], src[:, e, :, 64 * e:64 * e + 64],
                                              ALU.add)
                    m.then_inc(sem("rw_yadd"), 1)
            dve.wait_ge(sem("rw_yadd"), 6)
            ys = [y_r[:, t, :].rearrange("p (h d) -> p h d", h=12) for t in range(NT)]
            ycs = [yc[:, t, :].rearrange("p (h d) -> p h d", h=12) for t in range(NT)]
            for t in range(NT):
                m = dve.tensor_reduce(hss[:, 12 * t:12 * t + 12], ys[t], AX.X, ALU.add)
            step(m)
            step(dve.tensor_scalar(hss[:, 0:24], hss[:, 0:24], 1.0 / 64, None, ALU.mult))
            for t in range(NT):
                m = dve.tensor_tensor(ycs[t], ys[t], bc(hss[:, 12 * t:12 * t + 12].unsqueeze(2), [P, 12, 64]), ALU.subtract)
            step(m)
            for t in range(NT):
                m = dve.tensor_tensor(ys[t], ycs[t], ycs[t], ALU.mult)
            step(m)
            for t in range(NT):
                m = dve.tensor_reduce(hss[:, 12 * t:12 * t + 12], ys[t], AX.X, ALU.add)
            step(m)
            step(dve.tensor_scalar(hvar[:, 0:24], hss[:, 0:24], 1.0 / 64, LNX_EPS, ALU.mult, ALU.add))
            dve.reciprocal(hvar[:, 0:24], hvar[:, 0:24]).then_inc(sem("rw_yvar"), 1)
            dve.wait_ge(sem("rw_yrstd"), 1)
            for t in range(NT):
                m = dve.tensor_tensor(ycs[t], ycs[t], bc(hrstd[:, 12 * t:12 * t + 12].unsqueeze(2), [P, 12, 64]), ALU.mult)
            step(m)
            for o, op in ((1536, ALU.mult), (2304, ALU.add)):
                for t in range(NT):
                    m = dve.tensor_tensor(yc[:, t, :], yc[:, t, :], par[:, o:o + 768], op)
                step(m)
            for t in range(NT):
                m = dve.tensor_tensor(ys[t], v_tok[:, t, :].rearrange("p (h d) -> p h d", h=12),
                                      bc(bonus[:, 12 * t:12 * t + 12].unsqueeze(2), [P, 12, 64]), ALU.mult)
            step(m)
            step(dve.tensor_tensor(y_r, y_r, yc, ALU.add))
            dve.wait_ge(sem("rw_gate"), 1)
            step(dve.tensor_tensor(y_r, y_r, gate, ALU.mult))
            dve.memset(tiny[:, 161:162], 0.0).then_inc(sem("rwkv_over"), 1)
            dve.memset(tiny[:, 160:161], 0.0).then_inc(sem("rw_out"), 1)
            split_piece("a_out", 0, 0)
            transposes("a_mix")
            split_h("a_mix")
            gemm("a_out")
            split_piece("post0", 0, 0)
            norm("n_post0")
            split_h("n_post0")
            swiglu("post0")
            split_piece("kv", 0, 0)
            norm("n_kv")
            split_h("n_kv")
            gemm("kv")
            for e in moved("kv", 2):
                dve.wait_ge(sem(e[0]), e[1])
            dve.wait_ge(sem("norm_T"), 4 * (NORMS.index("n_kv") + 1))
            heads(4, [kd[:, t, :].rearrange("p (h d) -> p h d", h=12) for t in range(NT)], 64, [(0, 12, 7, 1.0)])
            dve.memset(tiny[:, 160:161], 0.0).then_inc(sem("heads_ok"), 1)
            transposes("kd")
            split_piece("pre1", 0, 0)
            norm("n_pre1")
            split_h("n_pre1")
            swiglu("pre1")
            split_piece("mem1", 0, 0)
            norm("n_mem1")
            split_h("n_mem1")
            gemm("mem1")
            mem_keys(5, 1)
            split_piece("b_q", 0, 0)
            norm("n_mix1")
            split_h("n_mix1")
            gemm("b_q")
            for e in moved("b_q", 1):
                dve.wait_ge(sem(e[0]), e[1])
            dve.wait_ge(sem("norm_T"), 4 * (NORMS.index("n_mix1") + 1))
            heads(6, [q_d[:, t, :].rearrange("p (h d) -> p h d", h=16) for t in range(NT)], 64,
                  [(0, 12, 6, 0.125), (12, 16, 3, 0.125)])
            dve.memset(tiny[:, 160:161], 0.0).then_inc(sem("heads_ok"), 1)
            transposes("dil_q")
            attention("mem1")
            attention("dil")
            split_piece("b_out", 0, 0)
            transposes("b_mix")
            split_h("b_mix")
            gemm("b_out")
            split_piece("post1", 0, 0)
            norm("n_post1")
            split_h("n_post1")
            swiglu("post1")


_WEIGHTS = ["x", "c", "ada_w", "ada_b", "even_w_in", "even_w_out", "odd_w_in", "odd_w_out", "router_w", "exp_w_gate",
            "exp_w_up", "exp_w_down", "mem_2", "ffn_pre_w_in_2", "ffn_pre_w_out_2", "ffn_post_w_in_2",
            "ffn_post_w_out_2", "mem_w_kv_2", "a_w_in_2", "a_w_up_2", "a_a_up_2", "a_g_up_2", "a_w_out_2", "b_w_q_2",
            "b_w_out_2", "kv_w_2", "rel_bias_2", "a_lnx_g_2", "a_lnx_b_2", "router_b"]


def kernel(**inputs):
    import concourse.bacc as _bacc
    from concourse.bass_utils import run_bass_kernel_spmd as _run

    n = {k: np.ascontiguousarray(v) for k, v in inputs.items()}
    arrays = {k: n[k] for k in _WEIGHTS}

    def cols(v):
        return v.reshape(-1, P).T

    gains = [n["norm1_g"][0], n["norm1_g"][1], n["norm2_g"][0], n["norm2_g"][1], n["ffn_pre_norm_2"][0],
             n["ffn_pre_norm_2"][1], n["mix_norm_2"][0], n["mix_norm_2"][1], n["ffn_post_norm_2"][0],
             n["ffn_post_norm_2"][1], n["mem_norm_2"][0], n["mem_norm_2"][1], n["kv_norm_2"]]
    arrays["gain_cols"] = np.ascontiguousarray(np.concatenate([cols(g) for g in gains], 1))
    arrays["rwkv_cols"] = np.ascontiguousarray(np.concatenate(
        [cols(v.reshape(-1)) for v in (n["a_shift_mu_2"], n["a_w0_2"], n["a_a0_2"], n["a_kk_scale_2"], n["a_k_a_2"],
                                       n["a_r_k_2"])], 1))
    arrays["gains64"] = np.ascontiguousarray(np.concatenate(
        [n["att_q_norm_g"].reshape(-1), n["att_k_norm_g"].reshape(-1), n["mem_q_norm_2"].reshape(-1),
         n["mem_k_norm_2"].reshape(-1), n["b_q_norm_2"].reshape(-1), n["kv_k_norm_2"].reshape(-1)]))
    rel = n["att_rel_bias"][0].T
    arrays["rel_t"] = np.ascontiguousarray(np.concatenate([rel, np.zeros((256 - rel.shape[0], 8), rel.dtype)], 0))
    arrays.update(constants())

    nc = _bacc.Bacc("TRN2", target_bir_lowering=False, num_devices=1)
    ins = {k: nc.dram_tensor(f"in_{k}", v.shape, mybir.dt.from_np(v.dtype), kind="ExternalInput").ap()
           for k, v in arrays.items()}
    out = nc.dram_tensor("out_x", (1, T, D), F32, kind="ExternalOutput").ap()
    build(nc, ins, out)
    r = _run(nc, [{f"in_{k}": v for k, v in arrays.items()}], core_ids=[0])
    return r.results[0]["out_x"]
```
